# Optimizing a Trainium2 kernel written in Bass

```python
import math
import jax
import jax.numpy as jnp
from jax import lax
import numpy as np
import jax, jax.numpy as jnp

D_MODEL = 1024
BATCH = 1
SEQ = 256
DEPTH = 1

N_MEM = 256
SSD_EXPAND = 2
D_INNER = SSD_EXPAND * D_MODEL
SSD_HEAD_DIM = 64
SSD_HEADS = D_INNER // SSD_HEAD_DIM
SSD_GROUPS = 4
SSD_STATE = 128
CONV_WIDTH = 4
SSD_CHUNK = 128
XBC_DIM = D_INNER + 2 * SSD_GROUPS * SSD_STATE
MLA_HEADS = 16
QK_NOPE_DIM = 64
QK_ROPE_DIM = 32
QK_HEAD_DIM = QK_NOPE_DIM + QK_ROPE_DIM
V_HEAD_DIM = 64
Q_LORA_RANK = 384
KV_LORA_RANK = 256
ROPE_THETA = 10000.0
Q_BLOCK = 128
XA_HEADS = 4
XA_HEAD_DIM = D_MODEL // XA_HEADS
N_EXPERT_GROUPS = 4
EXPERTS_PER_GROUP = 8
N_EXPERTS = N_EXPERT_GROUPS * EXPERTS_PER_GROUP
TOP_K = 2
D_EXPERT = 256
RMS_EPS = 1e-6

IN_SPLITS = (D_INNER, XBC_DIM, SSD_HEADS, Q_LORA_RANK, KV_LORA_RANK, QK_ROPE_DIM, D_MODEL, D_MODEL)
IN_PROJ_DIM = D_INNER + XBC_DIM + SSD_HEADS + Q_LORA_RANK + KV_LORA_RANK + QK_ROPE_DIM + 2 * D_MODEL


def rms_norm(x, gain):
    xf = x.astype(jnp.float32)
    xf = xf * lax.rsqrt(jnp.mean(xf * xf, axis=-1, keepdims=True) + RMS_EPS)
    return xf.astype(x.dtype) * gain

def split_cols(x, sizes):
    offs = np.cumsum(np.array(sizes))[:-1].tolist()
    return jnp.split(x, offs, axis=-1)

def causal_depthwise_conv(x, w, b):
    k, c = w.shape
    y = lax.conv_general_dilated(x, w[:, None, :], window_strides=(1,), padding=[(k - 1, 0)],
                                 dimension_numbers=('NWC', 'WIO', 'NWC'), feature_group_count=c)
    return y + b

def apply_rope(x, positions):
    half = x.shape[-1] // 2
    inv_freq = ROPE_THETA ** (-jnp.arange(half, dtype=jnp.float32) / half)
    ang = positions.astype(jnp.float32)[..., None] * inv_freq
    cos = jnp.cos(ang)[:, :, None, :]
    sin = jnp.sin(ang)[:, :, None, :]
    xf = x.astype(jnp.float32)
    x1, x2 = xf[..., :half], xf[..., half:]
    return jnp.concatenate([x1 * cos - x2 * sin, x2 * cos + x1 * sin], axis=-1).astype(x.dtype)

def ssd_chunked_scan(xh, dt, a, bm, cm):
    b, s, h, p = xh.shape
    g, n = bm.shape[2], bm.shape[3]
    r = h // g
    nc, l = s // SSD_CHUNK, SSD_CHUNK
    x_dt = (xh.astype(jnp.float32) * dt[..., None]).reshape(b, nc, l, g, r, p)
    a_dt = (dt * a).reshape(b, nc, l, g, r).transpose(0, 3, 4, 1, 2)
    bc = bm.astype(jnp.float32).reshape(b, nc, l, g, n)
    cc = cm.astype(jnp.float32).reshape(b, nc, l, g, n)
    a_cum = jnp.cumsum(a_dt, axis=-1)
    causal = jnp.tril(jnp.ones((l, l), dtype=bool))
    seg = a_cum[..., :, None] - a_cum[..., None, :]
    decay_in = jnp.exp(jnp.where(causal, seg, -jnp.inf))
    cb = jnp.einsum('bclgn,bcsgn->bcgls', cc, bc)
    y_diag = jnp.einsum('bcgls,bgrcls,bcsgrp->bclgrp', cb, decay_in, x_dt)
    decay_to_end = jnp.exp(a_cum[..., -1:] - a_cum)
    chunk_states = jnp.einsum('bclgn,bgrcl,bclgrp->bcgrpn', bc, decay_to_end, x_dt)
    chunk_decay = jnp.exp(a_cum[..., -1])

    def step(state, inp):
        st, dec = inp
        return state * dec[..., None, None] + st, state

    init = jnp.zeros((b, g, r, p, n), jnp.float32)
    _, prev_states = lax.scan(step, init, (jnp.moveaxis(chunk_states, 1, 0), jnp.moveaxis(chunk_decay, -1, 0)))
    prev_states = jnp.moveaxis(prev_states, 0, 1)
    y_off = jnp.einsum('bclgn,bcgrpn,bgrcl->bclgrp', cc, prev_states, jnp.exp(a_cum))
    return (y_diag + y_off).reshape(b, s, h, p)

def ssd_branch(z, xbc, dt_raw, conv_w, conv_b, dt_bias, a_log, d_skip, ssd_norm):
    b, s, _ = z.shape
    xbc = jax.nn.silu(causal_depthwise_conv(xbc, conv_w, conv_b))
    xs, bm, cm = split_cols(xbc, (D_INNER, SSD_GROUPS * SSD_STATE, SSD_GROUPS * SSD_STATE))
    xh = xs.reshape(b, s, SSD_HEADS, SSD_HEAD_DIM)
    bm = bm.reshape(b, s, SSD_GROUPS, SSD_STATE)
    cm = cm.reshape(b, s, SSD_GROUPS, SSD_STATE)
    dt = jax.nn.softplus(dt_raw.astype(jnp.float32) + dt_bias.astype(jnp.float32))
    a = -jnp.exp(a_log.astype(jnp.float32))
    y = ssd_chunked_scan(xh, dt, a, bm, cm)
    y = y + d_skip.astype(jnp.float32)[:, None] * xh.astype(jnp.float32)
    y = y.reshape(b, s, D_INNER) * jax.nn.silu(z.astype(jnp.float32))
    y = y.reshape(b, s, SSD_GROUPS, D_INNER // SSD_GROUPS)
    y = y * lax.rsqrt(jnp.mean(y * y, axis=-1, keepdims=True) + RMS_EPS)
    return y.reshape(b, s, D_INNER).astype(z.dtype) * ssd_norm

def causal_block_attention(q, k, v, scale):
    b, s, h, dq = q.shape
    nb = s // Q_BLOCK
    qb = jnp.moveaxis(q.reshape(b, nb, Q_BLOCK, h, dq), 1, 0)
    kpos = jnp.arange(s)

    def one_block(args):
        i, qi = args
        sc = jnp.einsum('bqhd,bkhd->bhqk', qi, k).astype(jnp.float32) * scale
        qpos = i * Q_BLOCK + jnp.arange(Q_BLOCK)
        sc = jnp.where(kpos[None, :] <= qpos[:, None], sc, -jnp.inf)
        pr = jax.nn.softmax(sc, axis=-1).astype(v.dtype)
        return jnp.einsum('bhqk,bkhd->bqhd', pr, v)

    out = lax.map(one_block, (jnp.arange(nb), qb))
    return jnp.moveaxis(out, 0, 1).reshape(b, s, h, v.shape[-1])

def mla_branch(q_a, c_kv, k_rope, positions, q_a_norm, w_q_b, kv_a_norm, w_kv_b):
    b, s, _ = q_a.shape
    q = (rms_norm(q_a, q_a_norm) @ w_q_b).reshape(b, s, MLA_HEADS, QK_HEAD_DIM)
    kv = (rms_norm(c_kv, kv_a_norm) @ w_kv_b).reshape(b, s, MLA_HEADS, QK_NOPE_DIM + V_HEAD_DIM)
    q_nope, q_pe = q[..., :QK_NOPE_DIM], q[..., QK_NOPE_DIM:]
    k_nope, v = kv[..., :QK_NOPE_DIM], kv[..., QK_NOPE_DIM:]
    q_pe = apply_rope(q_pe, positions)
    k_pe = apply_rope(k_rope[:, :, None, :], positions)
    q = jnp.concatenate([q_nope, q_pe], axis=-1)
    k = jnp.concatenate([k_nope, jnp.broadcast_to(k_pe, (b, s, MLA_HEADS, QK_ROPE_DIM))], axis=-1)
    o = causal_block_attention(q, k, v, QK_HEAD_DIM ** -0.5)
    return o.reshape(b, s, MLA_HEADS * V_HEAD_DIM)

def memory_cross_attention(h, mem, w_xq, w_xkv, w_xo):
    b, s, _ = h.shape
    m = mem.shape[1]
    q = (h @ w_xq).reshape(b, s, XA_HEADS, XA_HEAD_DIM)
    k, v = jnp.split(mem @ w_xkv, 2, axis=-1)
    k = k.reshape(b, m, XA_HEADS, XA_HEAD_DIM)
    v = v.reshape(b, m, XA_HEADS, XA_HEAD_DIM)
    sc = jnp.einsum('bshd,bmhd->bhsm', q, k).astype(jnp.float32) * XA_HEAD_DIM ** -0.5
    pr = jax.nn.softmax(sc, axis=-1).astype(v.dtype)
    o = jnp.einsum('bhsm,bmhd->bshd', pr, v).reshape(b, s, XA_HEADS * XA_HEAD_DIM)
    return o @ w_xo

def hierarchical_moe(h, w_rg, b_rg, w_re, b_re, w_gate, w_up, w_down):
    b, s, d = h.shape
    t = h.reshape(b * s, d)
    g_logits = (t @ w_rg).astype(jnp.float32) + b_rg
    g_prob = jax.nn.softmax(g_logits, axis=-1)
    g_sel = jnp.argmax(g_logits, axis=-1)
    g_w = jnp.take_along_axis(g_prob, g_sel[:, None], axis=1)
    e_logits = ((t @ w_re).astype(jnp.float32) + b_re).reshape(-1, N_EXPERT_GROUPS, EXPERTS_PER_GROUP)
    e_in = jnp.take_along_axis(e_logits, g_sel[:, None, None], axis=1)[:, 0]
    top_v, top_i = lax.top_k(e_in, TOP_K)
    w_top = jax.nn.softmax(top_v, axis=-1) * g_w
    expert_id = g_sel[:, None] * EXPERTS_PER_GROUP + top_i
    combine = jnp.sum(jax.nn.one_hot(expert_id, N_EXPERTS, dtype=jnp.float32) * w_top[..., None], axis=1).astype(t.dtype)
    hg = jnp.einsum('td,edf->tef', t, w_gate)
    hu = jnp.einsum('td,edf->tef', t, w_up)
    act = jax.nn.silu(hg) * hu * combine[:, :, None]
    y = jnp.einsum('tef,efd->td', act, w_down)
    return y.reshape(b, s, d)

def first_inputs(seed: int = 0) -> dict:
    key = jax.random.key(seed)
    ks = iter(jax.random.split(key, 48))
    f32 = jnp.float32
    L = DEPTH

    def nrm(shape, fan_in):
        return jax.random.normal(next(ks), shape, f32) * fan_in ** -0.5

    def gain(shape):
        return 1.0 + 0.02 * jax.random.normal(next(ks), shape, f32)

    x = jax.random.normal(next(ks), (BATCH, SEQ, D_MODEL), f32)
    mem = jax.random.normal(next(ks), (BATCH, N_MEM, D_MODEL), f32)
    offset = jax.random.randint(next(ks), (BATCH, 1), 0, 1024, dtype=jnp.int32)
    positions = (offset + jnp.arange(SEQ, dtype=jnp.int32)[None, :]).astype(jnp.int32)
    dt0 = jnp.exp(jax.random.uniform(next(ks), (L, SSD_HEADS), f32, math.log(1e-3), math.log(1e-1)))
    dt_bias = dt0 + jnp.log(-jnp.expm1(-dt0))
    a_log = jnp.log(jax.random.uniform(next(ks), (L, SSD_HEADS), f32, 1.0, 16.0))
    return {
        'x': x,
        'mem': mem,
        'positions': positions,
        'norm_mix': gain((L, D_MODEL)),
        'w_in': nrm((L, D_MODEL, IN_PROJ_DIM), D_MODEL),
        'conv_w': nrm((L, CONV_WIDTH, XBC_DIM), CONV_WIDTH),
        'conv_b': 0.02 * jax.random.normal(next(ks), (L, XBC_DIM), f32),
        'dt_bias': dt_bias,
        'a_log': a_log,
        'd_skip': 1.0 + 0.1 * jax.random.normal(next(ks), (L, SSD_HEADS), f32),
        'ssd_norm': gain((L, D_INNER)),
        'w_ssd_out': nrm((L, D_INNER, D_MODEL), D_INNER),
        'q_a_norm': gain((L, Q_LORA_RANK)),
        'w_q_b': nrm((L, Q_LORA_RANK, MLA_HEADS * QK_HEAD_DIM), Q_LORA_RANK),
        'kv_a_norm': gain((L, KV_LORA_RANK)),
        'w_kv_b': nrm((L, KV_LORA_RANK, MLA_HEADS * (QK_NOPE_DIM + V_HEAD_DIM)), KV_LORA_RANK),
        'w_mla_out': nrm((L, MLA_HEADS * V_HEAD_DIM, D_MODEL), MLA_HEADS * V_HEAD_DIM),
        'w_o': nrm((L, D_MODEL, D_MODEL), D_MODEL),
        'norm_xattn': gain((L, D_MODEL)),
        'norm_mem': gain((L, D_MODEL)),
        'w_xq': nrm((L, D_MODEL, XA_HEADS * XA_HEAD_DIM), D_MODEL),
        'w_xkv': nrm((L, D_MODEL, 2 * XA_HEADS * XA_HEAD_DIM), D_MODEL),
        'w_xo': nrm((L, XA_HEADS * XA_HEAD_DIM, D_MODEL), XA_HEADS * XA_HEAD_DIM),
        'norm_moe': gain((L, D_MODEL)),
        'w_router_group': nrm((L, D_MODEL, N_EXPERT_GROUPS), D_MODEL),
        'b_router_group': 0.01 * jax.random.normal(next(ks), (L, N_EXPERT_GROUPS), f32),
        'w_router_expert': nrm((L, D_MODEL, N_EXPERTS), D_MODEL),
        'b_router_expert': 0.01 * jax.random.normal(next(ks), (L, N_EXPERTS), f32),
        'w_exp_gate': nrm((L, N_EXPERTS, D_MODEL, D_EXPERT), D_MODEL),
        'w_exp_up': nrm((L, N_EXPERTS, D_MODEL, D_EXPERT), D_MODEL),
        'w_exp_down': nrm((L, N_EXPERTS, D_EXPERT, D_MODEL), D_EXPERT),
        'norm_final': gain((D_MODEL,)),
    }

def first_block(x, mem, positions, norm_mix, w_in, conv_w, conv_b, dt_bias, a_log, d_skip, ssd_norm, w_ssd_out,
              q_a_norm, w_q_b, kv_a_norm, w_kv_b, w_mla_out, w_o, norm_xattn, norm_mem, w_xq, w_xkv, w_xo,
              norm_moe, w_router_group, b_router_group, w_router_expert, b_router_expert,
              w_exp_gate, w_exp_up, w_exp_down, norm_final):
    h = x
    for i in range(DEPTH):
        u = rms_norm(h, norm_mix[i])
        z, xbc, dt_raw, q_a, c_kv, k_rope, gate_ssd, gate_mla = split_cols(u @ w_in[i], IN_SPLITS)
        y_ssd = ssd_branch(z, xbc, dt_raw, conv_w[i], conv_b[i], dt_bias[i], a_log[i], d_skip[i], ssd_norm[i]) @ w_ssd_out[i]
        y_mla = mla_branch(q_a, c_kv, k_rope, positions, q_a_norm[i], w_q_b[i], kv_a_norm[i], w_kv_b[i]) @ w_mla_out[i]
        merged = jax.nn.sigmoid(gate_ssd) * y_ssd + jax.nn.sigmoid(gate_mla) * y_mla
        h = h + merged @ w_o[i]
        h = h + memory_cross_attention(rms_norm(h, norm_xattn[i]), rms_norm(mem, norm_mem[i]), w_xq[i], w_xkv[i], w_xo[i])
        h = h + hierarchical_moe(rms_norm(h, norm_moe[i]), w_router_group[i], b_router_group[i],
                                 w_router_expert[i], b_router_expert[i], w_exp_gate[i], w_exp_up[i], w_exp_down[i])
    return rms_norm(h, norm_final)


PLE_DIM = 256
MIX_WIDTH = D_MODEL
HG_WIDTH = D_MODEL // 2
HG_HEADS = 4
HG_DK = HG_WIDTH // HG_HEADS
HG_DV = HG_WIDTH // HG_HEADS
HG_CHUNK = 64
SB_WIDTH = MIX_WIDTH - HG_WIDTH
SB_HEADS = 8
SB_DH = SB_WIDTH // SB_HEADS
SB_BLOCK = 128
D_FF = -(-8 * D_MODEL // (3 * 256)) * 256
IN_COLS = 4 * HG_WIDTH + 3 * SB_WIDTH
EPS = 1e-6


def rmsnorm(x, w):
    xf = x.astype(jnp.float32)
    xf = xf * lax.rsqrt(jnp.mean(xf * xf, axis=-1, keepdims=True) + EPS)
    return xf.astype(x.dtype) * w

def _to_chunks(a, heads, d):
    B, T, _ = a.shape
    return a.reshape(B, T // HG_CHUNK, HG_CHUNK, heads, d).transpose(1, 0, 3, 2, 4)

def hgrn2_mix(q, f_logit, i_in, lb):
    B, T, _ = q.shape
    q = jax.nn.silu(q.astype(jnp.float32))
    z = f_logit.astype(jnp.float32)
    log_f = jnp.logaddexp(jnp.log(lb), jnp.log1p(-lb) + jax.nn.log_sigmoid(z))
    k = -jnp.expm1(log_f)
    v = i_in.astype(jnp.float32)
    qc = _to_chunks(q, HG_HEADS, HG_DK)
    kc = _to_chunks(k, HG_HEADS, HG_DK)
    gc = _to_chunks(log_f, HG_HEADS, HG_DK)
    vc = _to_chunks(v, HG_HEADS, HG_DV)
    incl = jnp.tril(jnp.ones((HG_CHUNK, HG_CHUNK), dtype=bool))

    def step(S, inp):
        qb, kb, gb, vb = inp
        b = jnp.cumsum(gb, axis=2)
        o_inter = jnp.einsum('bhtk,bhkv->bhtv', qb * jnp.exp(b), S)
        diff = b[:, :, :, None, :] - b[:, :, None, :, :]
        decay = jnp.where(incl[:, :, None], jnp.exp(jnp.minimum(diff, 0.0)), 0.0)
        scores = jnp.einsum('bhtsk,bhsk->bhts', qb[:, :, :, None, :] * decay, kb)
        o_intra = jnp.einsum('bhts,bhsv->bhtv', scores, vb)
        b_last = b[:, :, -1:, :]
        S_new = jnp.exp(b_last[:, :, 0, :])[..., None] * S + jnp.einsum(
            'bhsk,bhsv->bhkv', kb * jnp.exp(b_last - b), vb)
        return S_new, o_inter + o_intra

    S0 = jnp.zeros((B, HG_HEADS, HG_DK, HG_DV), jnp.float32)
    _, oc = lax.scan(step, S0, (qc, kc, gc, vc))
    return oc.transpose(1, 0, 3, 2, 4).reshape(B, T, HG_HEADS * HG_DV)

def stick_breaking_mix(q, k, v):
    B, T, H, d = q.shape
    scale = d ** -0.5
    outs = []
    for blk in range(T // SB_BLOCK):
        t0 = blk * SB_BLOCK
        t1 = t0 + SB_BLOCK
        qb = q[:, t0:t1]
        kp = k[:, :t1]
        vp = v[:, :t1]
        z = jnp.einsum('bthd,bshd->bhts', qb, kp).astype(jnp.float32) * scale
        causal = jnp.arange(t1)[None, :] < jnp.arange(t0, t1)[:, None]
        log_1mb = jnp.where(causal, -jax.nn.softplus(z), 0.0)
        rem = lax.cumsum(log_1mb, axis=3, reverse=True) - log_1mb
        a = jnp.where(causal, jnp.exp(jax.nn.log_sigmoid(z) + rem), 0.0)
        outs.append(jnp.einsum('bhts,bshd->bthd', a.astype(v.dtype), vp))
    return jnp.concatenate(outs, axis=1)

def second_inputs(seed: int = 0) -> dict:
    key = jax.random.key(seed)
    ks = jax.random.split(key, 16)
    f32 = jnp.float32
    nrm = lambda k, shape, s: jax.random.normal(k, shape, f32) * s
    gain = lambda k, shape: 1.0 + 0.05 * jax.random.normal(k, shape, f32)
    return {
        "x": jax.random.normal(ks[0], (BATCH, SEQ, D_MODEL), f32),
        "p": jax.random.normal(ks[1], (DEPTH, BATCH, SEQ, PLE_DIM), f32),
        "attn_pre_norm": gain(ks[2], (DEPTH, D_MODEL)),
        "w_in": nrm(ks[3], (DEPTH, D_MODEL, IN_COLS), D_MODEL ** -0.5),
        "hg_lower_gamma": nrm(ks[4], (DEPTH + 1, HG_WIDTH), 0.5),
        "hg_out_norm": gain(ks[5], (DEPTH, HG_WIDTH)),
        "sb_out_norm": gain(ks[6], (DEPTH, SB_WIDTH)),
        "w_out": nrm(ks[7], (DEPTH, MIX_WIDTH, D_MODEL), MIX_WIDTH ** -0.5),
        "attn_post_norm": gain(ks[8], (DEPTH, D_MODEL)),
        "ffn_pre_norm": gain(ks[9], (DEPTH, D_MODEL)),
        "w_gate_up": nrm(ks[10], (DEPTH, D_MODEL, 2 * D_FF), D_MODEL ** -0.5),
        "w_down": nrm(ks[11], (DEPTH, D_FF, D_MODEL), D_FF ** -0.5),
        "ffn_post_norm": gain(ks[12], (DEPTH, D_MODEL)),
        "ple_proj": nrm(ks[13], (DEPTH, PLE_DIM, D_MODEL), PLE_DIM ** -0.5),
        "ple_gate": nrm(ks[14], (DEPTH, D_MODEL, D_MODEL), D_MODEL ** -0.5),
    }

def second_block(x, p, attn_pre_norm, w_in, hg_lower_gamma, hg_out_norm, sb_out_norm, w_out,
              attn_post_norm, ffn_pre_norm, w_gate_up, w_down, ffn_post_norm, ple_proj, ple_gate):
    B, T, _ = x.shape
    lb_all = jnp.cumsum(jax.nn.softmax(hg_lower_gamma.astype(jnp.float32), axis=0), axis=0)
    splits = [HG_WIDTH, 2 * HG_WIDTH, 3 * HG_WIDTH, 4 * HG_WIDTH,
              4 * HG_WIDTH + SB_WIDTH, 4 * HG_WIDTH + 2 * SB_WIDTH]
    h = x
    for i in range(DEPTH):
        u = rmsnorm(h, attn_pre_norm[i])
        proj = u @ w_in[i]
        hq, hf, hi, hg, sq, sk, sv = jnp.split(proj, splits, axis=-1)
        o_hg = hgrn2_mix(hq, hf, hi, lb_all[i])
        o_hg = rmsnorm(o_hg.astype(x.dtype), hg_out_norm[i]) * jax.nn.silu(hg)
        o_sb = stick_breaking_mix(sq.reshape(B, T, SB_HEADS, SB_DH),
                                  sk.reshape(B, T, SB_HEADS, SB_DH),
                                  sv.reshape(B, T, SB_HEADS, SB_DH)).reshape(B, T, SB_WIDTH)
        o_sb = rmsnorm(o_sb, sb_out_norm[i])
        mix = jnp.concatenate([o_hg, o_sb], axis=-1) @ w_out[i]
        h = h + rmsnorm(mix, attn_post_norm[i])
        u = rmsnorm(h, ffn_pre_norm[i])
        gate, up = jnp.split(u @ w_gate_up[i], [D_FF], axis=-1)
        y = (jax.nn.silu(gate) * up) @ w_down[i]
        h = h + rmsnorm(y, ffn_post_norm[i])
        h = h + (p[i] @ ple_proj[i]) * jax.nn.sigmoid(h @ ple_gate[i])
    return h


def setup_inputs(seed=0):
    out = dict(first_inputs(seed))
    for name, value in second_inputs(seed + 1).items():
        if name != "x":
            out[name + "_2"] = value
    return out


def reference(
    x, mem, positions, norm_mix, w_in, conv_w, conv_b, dt_bias, a_log, d_skip, ssd_norm,
    w_ssd_out, q_a_norm, w_q_b, kv_a_norm, w_kv_b, w_mla_out, w_o, norm_xattn, norm_mem, w_xq,
    w_xkv, w_xo, norm_moe, w_router_group, b_router_group, w_router_expert, b_router_expert,
    w_exp_gate, w_exp_up, w_exp_down, norm_final, p_2, attn_pre_norm_2, w_in_2,
    hg_lower_gamma_2, hg_out_norm_2, sb_out_norm_2, w_out_2, attn_post_norm_2, ffn_pre_norm_2,
    w_gate_up_2, w_down_2, ffn_post_norm_2, ple_proj_2, ple_gate_2,
):
    x = first_block(
        x, mem, positions, norm_mix, w_in, conv_w, conv_b, dt_bias, a_log, d_skip, ssd_norm,
        w_ssd_out, q_a_norm, w_q_b, kv_a_norm, w_kv_b, w_mla_out, w_o, norm_xattn, norm_mem,
        w_xq, w_xkv, w_xo, norm_moe, w_router_group, b_router_group, w_router_expert,
        b_router_expert, w_exp_gate, w_exp_up, w_exp_down, norm_final,
    )
    return second_block(
        x, p_2, attn_pre_norm_2, w_in_2, hg_lower_gamma_2, hg_out_norm_2, sb_out_norm_2,
        w_out_2, attn_post_norm_2, ffn_pre_norm_2, w_gate_up_2, w_down_2, ffn_post_norm_2,
        ple_proj_2, ple_gate_2,
    )


_drawn_inputs = setup_inputs


def setup_inputs(seed=0):
    import zlib

    import numpy as np

    out = dict(_drawn_inputs(seed))
    spreads = {}
    factors = {'ssd_norm': 3.183,
     'q_a_norm': 8.0,
     'kv_a_norm': 4.364,
     'norm_xattn': 5.792,
     'norm_mem': 3.575,
     'b_router_group': 22.523,
     'b_router_expert': 25.839,
     'hg_out_norm_2': 2.814,
     'norm_moe': 6.75,
     'sb_out_norm_2': 2.807}
    for name, (base, spread) in spreads.items():
        noise = np.random.default_rng([zlib.crc32(name.encode()), seed]).standard_normal(out[name].shape)
        drawn = base * np.exp(spread * noise) if base else spread * noise
        out[name] = jnp.asarray(drawn.astype(out[name].dtype))
    for name, factor in factors.items():
        out[name] = (out[name] * factor).astype(out[name].dtype)
    return out
```

```python
import numpy as np
import concourse.bass as bass
from concourse import mybir

F32 = mybir.dt.float32
F32R = mybir.dt.float32r
I32 = mybir.dt.int32
U8 = mybir.dt.uint8
ALU = mybir.AluOpType
ACT = mybir.ActivationFunctionType
AX = mybir.AxisListType
KB = 1024
NEG = -1.0e30
EPS = 1e-6

NRAW = 4
NSPL = 3
PIECE = 2048


def flat(x):
    if x is None:
        return []
    if isinstance(x, list):
        return [t for y in x for t in flat(y)]
    return [x]


class Prog:

    ENGINES = ("pe", "act", "dve", "pool", "sp")

    def __init__(self):
        self.q = {e: [] for e in self.ENGINES}
        self.held = {e: [] for e in self.ENGINES}
        self.count = {}

    def put(self, e, fn, after, chain=True):
        waits = flat(after) + self.held[e]
        self.held[e] = []
        if chain and e in ("act", "dve", "pool") and self.q[e]:
            waits.append((e, len(self.q[e]) - 1))
        self.q[e].append((fn, waits, None))
        return e, len(self.q[e]) - 1

    def dma(self, out, in_, sem, after=None, eng="sp"):
        waits = flat(after) + self.held[eng]
        self.held[eng] = []
        self.count[sem] = self.count.get(sem, 0) + 16
        self.q[eng].append((lambda e: e.dma_start(out, in_), waits, sem))
        return "dma", sem, self.count[sem]

    def last(self):
        return [(e, len(self.q[e]) - 1) for e in ("pe", "act", "dve", "pool") if self.q[e]]

    def barrier(self):
        for e in ("pe", "act", "dve", "pool"):
            self.held[e] += [t for t in self.last() if t[0] != e]

    def act(self, out, in_, func, after=None, chain=True, **kw):
        return self.put("act", lambda e: e.activation(out, in_, func, **kw), after, chain)

    def tt(self, out, a, b, op, after=None, chain=True):
        return self.put("dve", lambda e: e.tensor_tensor(out, a, b, op), after, chain)

    def ts(self, out, a, s1, s2, op0, op1=None, after=None):
        if op1 is None:
            return self.put("dve", lambda e: e.tensor_scalar(out, a, s1, None, op0), after)
        return self.put("dve", lambda e: e.tensor_scalar(out, a, s1, s2, op0, op1), after)

    def stt(self, out, a, s, b, op0, op1, after=None):
        return self.put("dve", lambda e: e.scalar_tensor_tensor(out=out, in0=a, scalar=s, in1=b, op0=op0, op1=op1), after)

    def red(self, out, a, op, after=None):
        return self.put("dve", lambda e: e.tensor_reduce(out, a, AX.X, op), after)

    def copy(self, out, a, after=None):
        return self.put("dve", lambda e: e.tensor_copy(out, a), after)

    def mm(self, out, lhsT, rhs, start=True, stop=True, after=None, loose=False):
        return self.put("pe", lambda e: e.matmul(out, lhsT, rhs, start=start, stop=stop, skip_group_check=loose), after)

    def tr(self, out, in_, ident, after=None):
        return self.put("pe", lambda e: e.transpose(out, in_, ident), after)

    def emit(self, nc, sems):
        need = {e: set() for e in self.ENGINES}
        plans = {}
        for e in self.ENGINES:
            seen, plan = {}, []
            for fn, waits, sem in self.q[e]:
                best = {}
                for t in waits:
                    key, n = (t[0], t[1]) if t[0] != "dma" else (("dma", t[1]), t[2])
                    if key == e and e in ("pe", "sp"):
                        continue
                    if n == "all":
                        n = self.count[t[1]]
                    best[key] = max(best.get(key, -1), n)
                todo = []
                for key, n in best.items():
                    if seen.get(key, -1) < n:
                        seen[key] = n
                        todo.append((key, n))
                        if isinstance(key, str):
                            need[key].add(n)
                plan.append((fn, todo, sem))
            plans[e] = plan
        value = {}
        for e in self.ENGINES:
            n, value[e] = 0, {}
            for i in sorted(need[e]):
                n += 1
                value[e][i] = n

        def run(e, eng):
            for i, (fn, todo, sem) in enumerate(plans[e]):
                for key, n in todo:
                    if isinstance(key, str):
                        eng.wait_ge(sems[key], value[key][n])
                    else:
                        eng.wait_ge(sems[key[1]], n)
                ins = fn(eng)
                if sem is not None:
                    ins.then_inc(sems[sem], 16)
                elif i in need[e]:
                    ins.then_inc(sems[e], 1)

        return run


class Weights:

    def __init__(self, P, raw, hi, lo, seq):
        self.P, self.raw, self.hi, self.lo, self.seq = P, raw, hi, lo, seq
        self.rec = []
        self.nload = self.nsplit = self.i = 0
        self.split_tok, self.load_tok, self.free_tok = {}, {}, {}

    def _load(self, j):
        views, n = self.seq[j][:2]
        s = j % NRAW
        tok = None
        for off, a, b, v in views:
            dst = self.raw[s][:, off:off + a * b].rearrange("p (a b) -> p a b", a=a) if len(views) == 1 else None
            if dst is None:
                tot = sum(x[2] for x in views)
                dst = self.raw[s][:, 0:a * tot].rearrange("p (a b) -> p a b", a=a)[:, :, off:off + b]
            tok = self.P.dma(dst, v, f"w{s}", after=self.split_tok.get(j - NRAW))
        self.load_tok[j] = tok

    def _split(self, j):
        n, maps = self.seq[j][1:]
        s, d = j % NRAW, j % NSPL
        raw, hi, lo = self.raw[s], self.hi[d], self.lo[d]
        for dst, src in maps or [(lambda x: x[:, 0:n], lambda x: x[:, 0:n])]:
            t = self.P.act(dst(hi), src(raw), ACT.Copy, after=[self.load_tok[j], self.free_tok.get(j - NSPL)], chain=False)
            self.split_tok[j] = self.P.tt(dst(lo), src(raw), dst(hi).bitcast(F32), ALU.subtract,
                                          after=[t, self.load_tok[j], self.free_tok.get(j - NSPL)], chain=False)

    def ahead(self):
        while self.nsplit < len(self.seq) and self.nsplit <= self.i + 2 and \
                (self.nsplit < NSPL or self.nsplit - NSPL in self.free_tok):
            while self.nload < len(self.seq) and self.nload <= self.nsplit:
                self._load(self.nload)
                self.nload += 1
            self._split(self.nsplit)
            self.nsplit += 1
        while self.nload < len(self.seq) and self.nload - NRAW < self.nsplit:
            self._load(self.nload)
            self.nload += 1

    def next(self, views, maps=None, out=None):
        kt, cols = views[0][1], sum(v[2] for v in views)
        n = kt * cols
        assert n <= PIECE
        self.rec.append((views, n, maps))
        if self.seq is None:
            i = self.i
            self.i += 1
            self.free_tok[i] = None
            d = 0
            tok = None
        else:
            i = self.i
            self.ahead()
            self.i += 1
            d = i % NSPL
            tok = self.split_tok[i]
        n = out or n
        assert n <= PIECE
        h = self.hi[d][:, 0:n].rearrange("p (a b) -> p a b", a=kt)
        l = self.lo[d][:, 0:n].rearrange("p (a b) -> p a b", a=kt)
        return h, l, tok, i

    def free(self, i, tok):
        self.free_tok[i] = tok


class Banks:
    def __init__(self, P, banks):
        self.P, self.banks, self.i = P, banks, 0
        self.tok = [None] * len(banks)

    def get(self, among=None):
        among = among or range(len(self.banks))
        among = list(among)
        b = among[self.i % len(among)]
        self.i += 1
        t, self.tok[b] = self.tok[b], None
        return b, self.banks[b], t

    def free(self, b, tok):
        self.tok[b] = flat(tok)


NCONST = 8


def constants():
    p = np.arange(128)
    ident = np.eye(128, dtype=np.float32)
    qk = np.where(p[None, :] <= p[:, None], 0.0, NEG).astype(np.float32)
    sl = np.where(p[None, :] >= p[:, None], 0.0, NEG).astype(np.float32)
    st = np.where(p[None, :] > p[:, None], 0.0, NEG).astype(np.float32)
    tri = (p[:, None] >= p[None, :]).astype(np.float32)
    perm = np.zeros((128, 128), np.float32)
    for m in range(128):
        if m % 32 < 16:
            perm[m + 16, m] = -1.0
        else:
            perm[m - 16, m] = 1.0
    inv = (np.float32(10000.0) ** (-(np.arange(16, dtype=np.float32)) / np.float32(16))).astype(np.float32)
    extra = np.zeros((128, 128), np.float32)
    extra[:, 0] = inv[p % 16]
    extra[:, 8:40] = np.arange(32, dtype=np.float32)[None, :]
    cst = np.concatenate([ident, qk, sl, st, tri, perm, extra], axis=1)
    masks = np.zeros((128, 7, 128), np.float32)
    for i in range(7):
        L = 2 << i
        same = (p[:, None] // L) == (p[None, :] // L)
        masks[:, i, :] = same & ((p[:, None] % L) < L // 2) & ((p[None, :] % L) >= L // 2)
    reset = np.tile((np.arange(1024) % 64 != 0).astype(np.float32)[None, :], (128, 1))
    return {"c_mat": cst, "c_masks": masks.reshape(128, 7 * 128), "c_reset": reset}


def program(nc, I, out, P, mem, seq, taps=None):
    sb = mem["sb"]
    W = Weights(P, mem["raw"], mem["hi"], mem["lo"], seq)
    B = Banks(P, mem["ps"])

    def tap(name, ap, after):
        if taps is not None:
            t = P.dma(taps[name], ap, "taps", after=after)
            for e in ("pe", "act", "dve"):
                P.held[e].append(t)

    def kp(v, kt):
        return v.rearrange("(k p) n -> p k n", p=128)

    XUh, XUl, H, T8, T8b = mem["XUh"], mem["XUl"], mem["H"], mem["T8"], mem["T8b"]
    cst, ones = mem["cst"], mem["ones"]
    ident = cst[:, 0:128]
    n_qk, n_sl, n_st, tri, perm = (cst[:, 128 * i:128 * (i + 1)] for i in range(1, 6))
    invf, iota = cst[:, 768:769], cst[:, 776:808]
    masks = mem["masks"]
    vec = mem["vec"]
    small = mem["small"]
    R = mem["R"]

    xin = R("xin", [128, 2, 1024], F32, 0)
    vraw = R("vraw", [128, 2, 128], F32, 16 * KB)
    t_x = P.dma(xin[:, :, :], I["x"][0].rearrange("(t p) d -> p t d", p=128), "x")
    P.dma(cst[:, :], I["c_mat"], "const")

    vecs = [("conv_w", I["conv_w"].rearrange("o k (t p) -> (o k t) p", p=128), 96),
            ("conv_b", I["conv_b"].rearrange("o (t p) -> (o t) p", p=128), 24),
            ("norm_mix", I["norm_mix"].rearrange("o (t p) -> (o t) p", p=128), 8),
            ("ssd_norm", I["ssd_norm"].rearrange("o (t p) -> (o t) p", p=128), 16),
            ("q_a_norm", I["q_a_norm"].rearrange("o (t p) -> (o t) p", p=128), 3),
            ("kv_a_norm", I["kv_a_norm"].rearrange("o (t p) -> (o t) p", p=128), 2),
            ("norm_xattn", I["norm_xattn"].rearrange("o (t p) -> (o t) p", p=128), 8),
            ("norm_mem", I["norm_mem"].rearrange("o (t p) -> (o t) p", p=128), 8),
            ("norm_moe", I["norm_moe"].rearrange("o (t p) -> (o t) p", p=128), 8),
            ("norm_final", I["norm_final"].rearrange("(t p) -> t p", p=128), 8)]
    vecs += [(n, I[n].rearrange("o (t p) -> (o t) p", p=128), k) for n, k in (
        ("attn_pre_norm_2", 8), ("hg_out_norm_2", 4), ("sb_out_norm_2", 4), ("attn_post_norm_2", 8),
        ("ffn_pre_norm_2", 8), ("ffn_post_norm_2", 8), ("hg_lower_gamma_2", 8))]
    col, at = {}, 0
    for name, view, n in vecs:
        assert at // 128 == (at + n - 1) // 128
        P.dma(vraw[at % 128:at % 128 + n, at // 128, :], view, "const")
        col[name] = vec[:, at:at + n]
        at += n
    nvec = at
    dtb, alog = small[:, 0:1], small[:, 1:2]
    dsk = small[:, 8:24]
    for c in range(4):
        P.dma(small[32 * c:32 * c + 32, 0:1], I["dt_bias"].rearrange("o h -> h o"), "const")
        P.dma(small[32 * c:32 * c + 32, 1:2], I["a_log"].rearrange("o h -> h o"), "const")
    d32 = small[:, 32:64]
    P.dma(d32, I["d_skip"].broadcast_to([128, 32]), "const")
    brt = mem["brt"]
    P.dma(brt[:, 0:4], I["b_router_group"].broadcast_to([128, 4]), "const")
    P.dma(brt[:, 4:36], I["b_router_expert"].broadcast_to([128, 32]), "const")
    posi = mem["posi"]
    P.dma(posi[:, :], I["positions"].broadcast_to([128, 256]), "const")
    mraw = R("mraw", [128, 896], F32, 24 * KB)
    P.dma(mraw[:, :], I["c_masks"], "const")
    t_c = ("dma", "const", "all")
    P.put("pool", lambda e: e.tensor_copy(masks[:, :], mraw[:, :]), [t_c])
    t_ones = P.put("pool", lambda e: e.memset(ones[:, :], 1.0), None)
    epsc = small[:, 2:3]
    t_eps = P.put("pool", lambda e: e.memset(epsc, EPS), None)

    if seq is not None:
        W.ahead()

    for j in range(2):
        t_dsk = P.copy(dsk[64 * j:64 * j + 64, :],
                       d32[64 * j:64 * j + 64, :].rearrange("p (i two) -> p two i", two=2)[:, j, :], after=[t_c])

    def split(h, l, src, after):
        t = P.act(h, src, ACT.Copy, after=after)
        return P.tt(l, src, h.bitcast(F32), ALU.subtract, after=[t] + flat(after))

    def rstd(src, nt, D, after):
        sq = T8[:, 0:nt, :]
        t = P.act(sq, src[:, 0:nt, :], ACT.Square, after=after)
        b, ps, tf = B.get()
        for k in range(nt):
            tm = P.mm(ps[:, 0:256], ones[:, :], sq[:, k, :], k == 0, k == nt - 1, after=[t, tf, t_ones])
        r = mem["rs"]
        t = P.act(r[:, 0, :], ps[:, 0:256], ACT.Ln, after=[tm, t_eps], scale=1.0 / D, bias=epsc)
        B.free(b, t)
        t = P.act(r[:, 1, :], r[:, 0, :], ACT.Exp, scale=-0.5)
        return r[:, 1, :], t

    def norm(src, nt, D, gain, dst, after):
        r, t = rstd(src, nt, D, after)
        for k in range(nt):
            t2 = P.stt(dst[:, k, :], src[:, k, :], gain[:, k:k + 1], r, ALU.mult, ALU.mult, after=[t, after])
        return t2

    def norm_split(src, nt, D, gain, h, l, after):
        t = norm(src, nt, D, gain, T8b, after)
        return split(h, l, T8b[:, 0:nt, :], [t])

    def triple(ps, h, l, xh, xl, kt, first, last, after, k0=0, loose=False, hl=None):
        for k in range(kt):
            st, sp = first and k == 0, last and k == kt - 1
            P.mm(ps, h(k), xh(k), st, False, after=after, loose=loose)
            P.mm(ps, h(k), xl(k), False, False, loose=loose)
            t = P.mm(ps, l(k), xh(k), False, sp, loose=loose)
        return t

    def linear(w, c0, ncol, xh, xl, kt, ready, evac, k_cols=256):
        for c in range(c0, c0 + ncol, k_cols):
            h, l, tw, i = W.next([(0, kt, k_cols, kp(w, kt)[:, :, c:c + k_cols])])
            b, ps, tf = B.get()
            nt = k_cols // 128
            for j in range(nt):
                t = triple(ps[:, 256 * j:256 * j + 256], lambda k: h[:, k, 128 * j:128 * j + 128],
                           lambda k: l[:, k, 128 * j:128 * j + 128], lambda k: xh[:, k, :], lambda k: xl[:, k, :],
                           kt, True, True, [tw, tf, ready])
            W.free(i, t)
            B.free(b, evac((c - c0) // 128, nt, ps[:, 0:256 * nt].rearrange("p (t n) -> p t n", t=nt), t))

    def linear_tok(w, c0, ncol, xh, xl, kt, ready, evac):
        for c in range(c0, c0 + ncol, 256):
            h, l, tw, i = W.next([(0, kt, 256, kp(w, kt)[:, :, c:c + 256])])
            b, ps, tf = B.get()
            for j in range(2):
                t = triple(ps[:, 256 * j:256 * j + 256], lambda k: xh[:, k, 128 * j:128 * j + 128],
                           lambda k: xl[:, k, 128 * j:128 * j + 128], lambda k: h[:, k, :], lambda k: l[:, k, :],
                           kt, True, True, [tw, tf, ready])
            W.free(i, t)
            B.free(b, evac(c - c0, ps[:, :].rearrange("p (t n) -> p t n", t=2), t))

    def transposes(dst, srcs, after):
        toks = []
        for g in range(0, len(srcs), 4):
            b, ps, tf = B.get()
            n = min(4, len(srcs) - g)
            for j in range(n):
                t = P.tr(ps[:, 128 * j:128 * j + 128], srcs[g + j], ident, after=[after, tf, t_c])
            t = P.copy(dst(g, n), ps[:, 0:128 * n].rearrange("p (a n) -> p a n", a=n), after=[t])
            B.free(b, t)
            toks.append(t)
        return toks[-1]

    b, ps, tf = B.get()
    t = P.tr(ps[:, 0:128], vraw[:, 0, :], ident, after=[t_c])
    t = P.tr(ps[0:128, 128:128 + nvec - 128], vraw[0:nvec - 128, 1, :], ident[0:nvec - 128, 0:nvec - 128], after=[t_c])
    t_vec = P.copy(vec[:, 0:nvec], ps[:, 0:nvec], after=[t])
    B.free(b, t_vec)
    toks = []
    for d0 in range(0, 8, 2):
        b, ps, tf = B.get()
        for j in range(4):
            t = P.tr(ps[:, 128 * j:128 * j + 128], xin[:, j % 2, (d0 + j // 2) * 128:(d0 + j // 2 + 1) * 128],
                     ident, after=[t_x, t_c, tf])
        t = P.copy(H[:, d0:d0 + 2, :], ps[:, :].rearrange("p (a n) -> p a n", a=2), after=[t])
        B.free(b, t)
    t_h = t
    t_u = norm_split(H, 8, 1024, col["norm_mix"], XUh[:, :, :], XUl[:, :, :], [t_h, t_vec])
    tap("u", T8b[:, :, :], t_u)

    cs = mem["cs"]
    ang, nn, tmp = T8[:, 0, :], T8[:, 1, :], T8[:, 2, :]
    t = P.copy(tmp, posi[:, :], after=[t_c, t_u])
    t = P.ts(ang, tmp, invf, None, ALU.mult)
    TWO = 2.0 * np.pi
    C1 = 6.28125
    C2 = float(np.float32(TWO - C1))
    C2 = float(np.float32(np.round((TWO - C1) * 2 ** 20) / 2 ** 20))
    C3 = float(np.float32(TWO - C1 - C2))
    MAGIC = 12582912.0
    for i, shift in ((0, np.pi / 2), (1, 0.0)):
        P.ts(nn, ang, 1.0 / TWO, shift / TWO, ALU.mult, ALU.add)
        P.ts(nn, nn, MAGIC, MAGIC, ALU.add, ALU.subtract)
        P.stt(tmp, nn, -C1, ang, ALU.mult, ALU.add)
        P.stt(tmp, nn, -C2, tmp, ALU.mult, ALU.add)
        P.stt(tmp, nn, -C3, tmp, ALU.mult, ALU.add)
        P.ts(tmp, tmp, float(np.float32(shift)), None, ALU.add)
        P.ts(tmp, tmp, float(np.float32(3.1415925)), float(np.float32(-3.1415925)), ALU.min, ALU.max)
        t = P.copy(cs[:, i, :], tmp)
    t_cs = P.act(cs[:, :, :], cs[:, :, :], ACT.Sin, after=[t])
    tap("cs", cs[:, :, :], t_cs)

    w_in = I["w_in"][0]
    xh, xl = XUh, XUl
    dtT, acT = R("dtT", [128, 256], F32, 20 * KB), R("acT", [128, 256], F32, 21 * KB)
    dtk = R("dtk", [128, 2, 2, 32], F32, 22 * KB)
    qa, ckv, kpe = R("qa", [128, 3, 256], F32, 10 * KB), R("ckv", [128, 2, 256], F32, 13 * KB), R("kpe", [128, 256], F32, 15 * KB)
    P.barrier()
    rep4 = [(lambda x: x[:, 0:1024].rearrange("p (k c d) -> p k c d", k=8, c=4),
             lambda x: x[:, 0:256].rearrange("p (k d) -> p k d", k=8).unsqueeze(2).broadcast_to([128, 8, 4, 32]))]
    h, l, tw, i = W.next([(0, 8, 32, kp(w_in, 8)[:, :, 5120:5152])], rep4, 1024)
    b, ps, tf = B.get()

    t = triple(ps[:, 0:256], lambda k: h[:, k, :], lambda k: l[:, k, :],
               lambda k: xh[:, k, :], lambda k: xl[:, k, :], 8, True, True, [tw, tf, t_u])
    W.free(i, t)
    s1, s2, s3 = T8[:, 4, :], T8[:, 5, :], T8[:, 6, :]
    t = P.ts(s1, ps[:, 0:256], dtb, None, ALU.add, after=[t, t_c])
    B.free(b, t)
    t = P.act(s2, s1, ACT.Abs, after=[t])
    t = P.act(s2, s2, ACT.Exp, after=[t], scale=-1.0)
    t = P.act(s3, s2, ACT.Ln, scale=1.0, bias=1.0)
    t_dt = P.stt(dtT[:, :], s1, 0.0, s3, ALU.max, ALU.add, after=[t])
    t = P.act(small[:, 3:4], alog, ACT.Exp, after=[t_c])
    t = P.ts(s1, dtT[:, :], small[:, 3:4], -1.0, ALU.mult, ALU.mult, after=[t])
    for c in range(2):
        t_ac = P.put("dve", lambda e, c=c: e.tensor_tensor_scan(
            acT[:, 128 * c:128 * c + 128], ones[:, 0:128], s1[:, 128 * c:128 * c + 128], 0.0, ALU.mult, ALU.add), [t_ones])
    b, ps, tf = B.get()
    for j, src in enumerate((dtT, acT)):
        for c in range(2):
            n = 2 * j + c
            t = P.tr(ps[:, 128 * n:128 * n + 128], src[:, 128 * c:128 * c + 128], ident, after=[tf, t_dt, t_ac])
    t_dtk = P.copy(dtk[:, :, :, :], ps[:, :].rearrange("p (a c n) -> p a c n", a=2, c=2)[:, :, :, 0:32], after=[t])
    B.free(b, t_dtk)
    tap("dtT", dtT[:, :], t_dtk)
    tap("acT", acT[:, :], t_dtk)

    dest = [(qa, 0), (qa, 1), (qa, 2), (ckv, 0), (ckv, 1)]

    def ev_lora(f, n, ps, t, base):
        for j in range(n):
            d, k = dest[base + j]
            t = P.copy(d[:, k, :], ps[:, j, :], after=[t])
        return t

    linear(w_in, 5152, 512, xh, xl, 8, t_u, lambda f, n, ps, t: ev_lora(f, n, ps, t, f))
    b, ps, tf = B.get()
    for j, (c, n, m) in enumerate(((5664, 128, None), (5792, 32, rep4))):
        h, l, tw, i = W.next([(0, 8, n, kp(w_in, 8)[:, :, c:c + n])], m, 1024)
        t = triple(ps[:, 256 * j:256 * j + 256], lambda k: h[:, k, :], lambda k: l[:, k, :],
                   lambda k: xh[:, k, :], lambda k: xl[:, k, :], 8, True, True, [tw, tf])
        W.free(i, t)
    t = P.copy(ckv[:, 1, :], ps[:, 0:256], after=[t])
    t_lora = P.copy(kpe[:, :], ps[:, 256:512], after=[t])
    B.free(b, t_lora)
    tap("qa", qa[:, :, :], t_lora)
    tap("kpe", kpe[:, :], t_lora)

    BT, CT = R("BT", [128, 4, 256], F32, 0), R("CT", [128, 4, 256], F32, 4 * KB)
    xs = R("xs", [128, 16, 256], F32, 24 * KB)
    xdt = R("xdt", [128, 2, 2048], F32, 40 * KB)
    Btok = R("Btok", [128, 4, 128], F32, 8 * KB)
    cw, cb = col["conv_w"], col["conv_b"]
    acc = T8b

    slot = [0]
    acc_tok = [None] * 4

    def ev_conv(ch, n, ps, t, put):
        toks = []
        for j in range(n):
            c = ch + j
            s = slot[0] % 4
            slot[0] += 1
            a = acc[:, s, :]
            t1 = P.act(a, ps[:, j, :], ACT.Identity, after=[t, t_vec, acc_tok[s]],
                       scale=cw[:, 72 + c:73 + c], bias=cb[:, c:c + 1])
            for k in range(3):
                sh = 3 - k
                t1 = P.stt(a[:, sh:256], ps[:, j, 0:256 - sh], cw[:, 24 * k + c:24 * k + c + 1], a[:, sh:256],
                           ALU.mult, ALU.add, after=[t1])
            t2 = P.act(put(c), a, ACT.Silu, after=[t1])
            acc_tok[s] = t2
            toks.append(t1)
        last_silu[0] = t2
        return toks

    last_silu = [None]
    linear(w_in, 4096, 1024, xh, xl, 8, t_u,
           lambda f, n, ps, t: ev_conv(16 + f, n, ps, t, lambda c: BT[:, c - 16, :] if c < 20 else CT[:, c - 20, :]))
    t_bc = last_silu[0]
    linear(w_in, 2048, 2048, xh, xl, 8, t_u, lambda f, n, ps, t: ev_conv(f, n, ps, t, lambda c: xs[:, c, :]))
    t_xs = last_silu[0]
    tap("BT", BT[:, :, :], t_bc)
    tap("xs", xs[:, :, :], t_xs)
    b, ps, tf = B.get()
    for g in range(4):
        t = P.tr(ps[:, 128 * g:128 * g + 128], BT[:, g, 0:128], ident, after=[t_bc, tf])
    t_btok = P.copy(Btok[:, :, :], ps[:, :].rearrange("p (a n) -> p a n", a=4), after=[t])
    B.free(b, t_btok)
    for c in range(2):
        for g in range(4):
            b, ps, tf = B.get()
            for j in range(4):
                t = P.tr(ps[:, 128 * j:128 * j + 128], xs[:, 4 * g + j, 128 * c:128 * c + 128], ident, after=[t_xs, tf])
            t_xdt = P.tt(xdt[:, c, 512 * g:512 * g + 512].rearrange("p (h d) -> p h d", d=64),
                         ps[:, :].rearrange("p (h d) -> p h d", d=64),
                         dtk[:, 0, c, 8 * g:8 * g + 8].unsqueeze(2).broadcast_to([128, 8, 64]), ALU.mult, after=[t, t_dtk])
            B.free(b, t_xdt)

    acb = R("acb", [128, 8, 256], F32, 56 * KB)
    M = R("M", [128, 2, 8, 128], F32, 64 * KB)
    CE = R("CE", [128, 8, 128], F32, 72 * KB)
    xw = R("xw", [128, 512], F32, 16 * KB)
    S0 = R("S0", [128, 512], F32, 18 * KB)
    dte = R("dte", [128, 8], F32, 23 * KB)
    t_y = t_pe = None
    for g in range(4):
        for q in range(4):
            b, ps, tf = B.get()
            for j in range(2):
                hd = 8 * g + 2 * q + j
                t = P.mm(ps[:, 256 * j:256 * j + 256], ident[0:32, hd:hd + 1].broadcast_to([32, 128]), acT[0:32, :],
                         after=[t_ac, tf])
            t_acb = P.act(acb[:, 2 * q:2 * q + 2, :], ps[:, :].rearrange("p (a n) -> p a n", a=2), ACT.Copy,
                          after=[t, t_y])
            B.free(b, t_acb)
        for c in range(2):
            for hl in range(8):
                t_m = P.stt(M[:, c, hl, :], acb[:, hl, 128 * c:128 * c + 128],
                            dtk[:, 1, c, 8 * g + hl:8 * g + hl + 1], n_sl, ALU.subtract, ALU.add,
                            after=[t_acb, t_dtk, t_pe])
        t = P.tt(dte[:, :], acb[:, :, 127], dtk[:, 1, 0, 8 * g:8 * g + 8], ALU.subtract)
        t_ce = P.act(CE[:, :, :], acb[:, :, 128:256], ACT.Exp, after=[t_pe])
        t_dte = P.act(dte[:, :], dte[:, :], ACT.Exp, after=[t])
        t_me = P.act(M[:, :, :, :], M[:, :, :, :], ACT.Exp, after=[t_m])
        b, ps, tf = B.get()
        for c in range(2):
            t = P.mm(ps[:, 128 * c:128 * c + 128], BT[:, g, 128 * c:128 * c + 128], CT[:, g, 128 * c:128 * c + 128],
                     after=[t_bc, tf])
        t_ce = P.tt(CE[:, :, :], CE[:, :, :], CT[:, g, 128:256].unsqueeze(1).broadcast_to([128, 8, 128]), ALU.mult,
                    after=[t_ce, t_bc])
        t_xw = P.tt(xw[:, :].rearrange("p (h d) -> p h d", d=64),
                    xdt[:, 0, 512 * g:512 * g + 512].rearrange("p (h d) -> p h d", d=64),
                    dte[:, :].unsqueeze(2).broadcast_to([128, 8, 64]), ALU.mult, after=[t_dte, t_pe])
        for c in range(2):
            t_m = P.tt(M[:, c, :, :], M[:, c, :, :], ps[:, 128 * c:128 * c + 128].unsqueeze(1).broadcast_to([128, 8, 128]),
                       ALU.mult, after=[t, t_me])
        B.free(b, t_m)
        b, ps, tf = B.get()
        t = P.mm(ps[:, :], Btok[:, g, :], xw[:, :], after=[t_xw, t_btok, tf])
        t_s0 = P.copy(S0[:, :], ps[:, :], after=[t, t_pe])
        B.free(b, t_s0)
        for q in range(4):
            b, ps, tf = B.get()
            for j in range(2):
                hl = 2 * q + j
                hd = 8 * g + hl
                o = 64 * j
                P.mm(ps[o:o + 64, 0:128], xdt[:, 0, 64 * hd:64 * hd + 64], M[:, 0, hl, :], after=[t_m, t_xdt, tf])
                P.mm(ps[o:o + 64, 128:256], xdt[:, 1, 64 * hd:64 * hd + 64], M[:, 1, hl, :], True, False)
                t_pe = P.mm(ps[o:o + 64, 128:256], S0[:, 64 * hl:64 * hl + 64], CE[:, hl, :], False, True,
                            after=[t_s0, t_ce])
            i = 4 * g + q
            t_y = P.stt(xs[:, i, :], xs[:, i, :], dsk[:, i:i + 1], ps[:, 0:256], ALU.mult, ALU.add, after=[t_pe, t_dsk])
            B.free(b, t_y)
    tap("y", xs[:, :, :], t_y)

    sz = mem["T8b"]

    def ev_z(f, n, ps, t):
        s = (f // 2) % 2
        t = P.act(sz[:, 2 * s:2 * s + n, :], ps, ACT.Silu, after=[t, zt[s]])
        zt[s] = P.tt(xs[:, f:f + n, :], xs[:, f:f + n, :], sz[:, 2 * s:2 * s + n, :], ALU.mult, after=[t])
        return t

    zt = [t_y, t_y]
    linear(w_in, 0, 2048, xh, xl, 8, t_u, ev_z)
    t_z = zt[1]
    P.barrier()
    YAh, YAl = R("YAh", [128, 16, 256], F32R, 40 * KB), R("YAl", [128, 16, 256], F32R, 56 * KB)
    for g in range(4):
        t_ya = norm_split(xs[:, 4 * g:4 * g + 4, :], 4, 512, col["ssd_norm"][:, 4 * g:4 * g + 4],
                          YAh[:, 4 * g:4 * g + 4, :], YAl[:, 4 * g:4 * g + 4, :], [t_z])
    G = R("G", [128, 8, 256], F32, 0)
    t_g = [None]

    def ev_gate(f, n, ps, t):
        t_g[0] = P.act(G[:, f:f + n, :], ps, ACT.Sigmoid, after=[t])
        return t_g[0]

    linear(w_in, 5824, 1024, xh, xl, 8, t_u, ev_gate)

    def ev_ssd(f, n, ps, t):
        t_g[0] = P.tt(G[:, f:f + n, :], G[:, f:f + n, :], ps, ALU.mult, after=[t, t_g0])
        return t_g[0]

    t_g0 = t_g[0]
    linear(I["w_ssd_out"][0], 0, 1024, YAh, YAl, 16, t_ya, ev_ssd, k_cols=128)
    tap("G", G[:, :, :], t_g[0])
    t_gs = t_g[0]

    P.barrier()
    XCh, XCl = R("XCh", [128, 5, 256], F32R, 16 * KB), R("XCl", [128, 5, 256], F32R, 21 * KB)
    t1 = norm_split(qa, 3, 384, col["q_a_norm"], XCh[:, 0:3, :], XCl[:, 0:3, :], [t_lora])
    t_xc = norm_split(ckv, 2, 256, col["kv_a_norm"], XCh[:, 3:5, :], XCl[:, 3:5, :], [t_lora])
    qn, qp = R("qn", [128, 8, 256], F32, 26 * KB), R("qp", [128, 4, 256], F32, 34 * KB)
    kn, V = (R("kn", [128, 8, 256], F32, 38 * KB), T8b), R("V", [128, 2, 1024], F32, 46 * KB)
    kpm = R("kpm", [128, 4, 256], F32, 10 * KB)
    P.put("pool", lambda e: e.memset(kn[0][64:128, :, :], 0.0), [t_xc])
    P.put("pool", lambda e: e.memset(kn[1][0:64, :, :], 0.0), [t_xc])
    t_zero = P.put("pool", lambda e: e.memset(kpm[:, :, :], 0.0), [t_xc])
    wq, wkv = I["w_q_b"][0], I["w_kv_b"][0]
    qmap = [(lambda x: x[:, 0:768].rearrange("p (k h d) -> p k h d", k=3, h=4),
             lambda x: x[:, 0:1152].rearrange("p (k h d) -> p k h d", k=3, h=4)[:, :, :, 0:64]),
            (lambda x: x[:, 768:1152].rearrange("p (k h d) -> p k h d", k=3, h=4),
             lambda x: x[:, 0:1152].rearrange("p (k h d) -> p k h d", k=3, h=4)[:, :, :, 64:96])]
    for q in range(4):
        h, l, tw, i = W.next([(0, 3, 384, kp(wq, 3)[:, :, 384 * q:384 * q + 384])], qmap)
        h, l = (x.rearrange("p a b -> p (a b)") for x in (h, l))

        b, ps, tf = B.get()
        for j in range(2):
            t = triple(ps[:, 256 * j:256 * j + 256], lambda k: h[:, 256 * k + 128 * j:256 * k + 128 * j + 128], lambda k: l[:, 256 * k + 128 * j:256 * k + 128 * j + 128],
                       lambda k: XCh[:, k, :], lambda k: XCl[:, k, :], 3, True, True, [tw, tf, t1])
        t2 = P.act(qn[:, 2 * q:2 * q + 2, :], ps[:, :].rearrange("p (a n) -> p a n", a=2), ACT.Copy, after=[t])
        B.free(b, t2)
        b, ps, tf = B.get()
        t = triple(ps[:, 0:256], lambda k: h[:, 768 + 128 * k:896 + 128 * k], lambda k: l[:, 768 + 128 * k:896 + 128 * k],
                   lambda k: XCh[:, k, :], lambda k: XCl[:, k, :], 3, True, True, [tf])
        W.free(i, t)
        t_q = P.act(qp[:, q, :], ps[:, 0:256], ACT.Copy, after=[t])
        B.free(b, t_q)
    kvmap = [(lambda x, k=k: x[:, 1024 * k:1024 * k + 1024].rearrange("p (t h d) -> p t h d", t=2, h=8),
              lambda x, k=k: x[:, 1024 * k:1024 * k + 1024].rearrange("p (h t d) -> p t h d", t=2, h=8)) for k in range(2)]
    for q in range(2):
        h, l, tw, i = W.next([(0, 2, 1024, kp(wkv, 2)[:, :, 1024 * q:1024 * q + 1024])], kvmap)

        for r in range(2):
            b, ps, tf = B.get()
            for j in range(2):
                a = 4 * r + 2 * j
                t = triple(ps[:, 256 * j:256 * j + 256], lambda k: h[:, k, 64 * a:64 * a + 128], lambda k: l[:, k, 64 * a:64 * a + 128],
                           lambda k: XCh[:, 3 + k, :], lambda k: XCl[:, 3 + k, :], 2, True, True, [tw, tf, t_xc])
            for o in range(2):
                p = slice(64 * o, 64 * o + 64)
                t_kn = P.act(kn[o][p, 4 * q + 2 * r:4 * q + 2 * r + 2, :], ps[p, :].rearrange("p (a n) -> p a n", a=2),
                             ACT.Copy, after=[t])
            B.free(b, t_kn)
        for j in range(2):
            b, ps, tf = B.get()
            t = triple(ps[:, :], lambda k: XCh[:, 3 + k, 128 * j:128 * j + 128], lambda k: XCl[:, 3 + k, 128 * j:128 * j + 128],
                       lambda k: h[:, k, 512:1024], lambda k: l[:, k, 512:1024], 2, True, True, [tf])
            t_v = P.act(V[:, j, 512 * q:512 * q + 512], ps[:, :], ACT.Copy, after=[t])
            B.free(b, t_v)
        W.free(i, t)
    t_r = []
    for q in range(5):
        src = qp[:, q, :] if q < 4 else kpe[:, :]
        b, ps, tf = B.get()
        t = P.mm(ps[:, 0:256], perm, src, after=[t_q, t_lora, tf, t_c])
        t = P.tt(T8[:, q, :], ps[:, 0:256], cs[:, 1, :], ALU.mult, after=[t, t_cs])
        B.free(b, t)
        P.tt(src, src, cs[:, 0, :], ALU.mult, after=[t])
        t_r = P.tt(src, src, T8[:, q, :], ALU.add)
    for hl in range(4):
        p = slice(32 * hl, 32 * hl + 32)
        t_r = P.copy(kpm[p, hl, :], kpe[p, :], after=[t_zero])
    tap("qn", qn[:, :, :], t_r)
    tap("qp", qp[:, :, :], t_r)
    tap("kpr", kpe[:, :], t_r)
    tap("V", V[:, :, :], [t_r, t_v])
    Pm0, Pm1 = R("Pm0", [128, 4, 128], F32, 54 * KB), R("Pm1", [128, 4, 256], F32, 56 * KB)
    PT0, PT1 = R("PT0", [128, 4, 256], F32, 60 * KB), R("PT1", [128, 4, 128], F32, 64 * KB)
    OAh, OAl = R("OAh", [128, 8, 256], F32R, 66 * KB), R("OAl", [128, 8, 256], F32R, 16 * KB)
    sm = mem["sm"]
    SC = 96.0 ** -0.5
    t_pv = t_ptr = None
    nqk4 = n_qk.unsqueeze(1).broadcast_to([128, 4, 128])
    for g in range(4):
        b0, p0, f0 = B.get()
        bs = [B.get() for _ in range(2)]
        for hl in range(4):
            hd = 4 * g + hl
            qN, kN = qn[:, hd // 2, :], kn[hd % 2][:, hd // 2, :]
            qP, kP = qp[:, g, :], kpm[:, hl, :]
            d0 = p0[:, 128 * hl:128 * hl + 128]
            P.mm(d0, qN[:, 0:128], kN[:, 0:128], True, False, after=[t_r, t_kn, t_zero, f0])
            t0 = P.mm(d0, qP[:, 0:128], kP[:, 0:128], False, True)
            d1 = bs[hl // 2][1][:, 256 * (hl % 2):256 * (hl % 2) + 256]
            P.mm(d1, qN[:, 128:256], kN[:, :], True, False, after=[bs[hl // 2][2]])
            t1 = P.mm(d1, qP[:, 128:256], kP[:, :], False, True)
        ta = P.stt(Pm0[:, :, :], p0[:, :].rearrange("p (a n) -> p a n", a=4), SC, nqk4, ALU.mult, ALU.add, after=[t0, t_ptr])
        B.free(b0, ta)
        for j in range(2):
            bb, pp, _ = bs[j]
            v = pp[:, :].rearrange("p (a n) -> p a n", a=2)
            P.ts(Pm1[:, 2 * j:2 * j + 2, 0:128], v[:, :, 0:128], SC, None, ALU.mult, after=[t1, t_ptr])
            ta = P.stt(Pm1[:, 2 * j:2 * j + 2, 128:256], v[:, :, 128:256], SC,
                       n_qk.unsqueeze(1).broadcast_to([128, 2, 128]), ALU.mult, ALU.add)
            B.free(bb, ta)
        P.red(sm[:, 0:4], Pm0[:, :, :], ALU.max)
        P.red(sm[:, 4:8], Pm1[:, :, :], ALU.max)
        t = P.ts(sm[:, 8:16], sm[:, 0:8], -1.0, None, ALU.mult)
        for hl in range(4):
            P.act(Pm0[:, hl, :], Pm0[:, hl, :], ACT.Exp, after=[t], bias=sm[:, 8 + hl:9 + hl], accum_out=sm[:, 16 + hl:17 + hl])
            t2 = P.act(Pm1[:, hl, :], Pm1[:, hl, :], ACT.Exp, bias=sm[:, 12 + hl:13 + hl], accum_out=sm[:, 20 + hl:21 + hl])
        P.put("dve", lambda e: e.reciprocal(sm[:, 24:32], sm[:, 16:24]), [t2])
        P.tt(Pm0[:, :, :], Pm0[:, :, :], sm[:, 24:28].unsqueeze(2).broadcast_to([128, 4, 128]), ALU.mult)
        t = P.tt(Pm1[:, :, :], Pm1[:, :, :], sm[:, 28:32].unsqueeze(2).broadcast_to([128, 4, 256]), ALU.mult)
        bt = [B.get() for _ in range(3)]
        for hl in range(4):
            d = bt[hl // 2][1][:, 256 * (hl % 2):256 * (hl % 2) + 256]
            P.tr(d[:, 0:128], Pm0[:, hl, :], ident, after=[t, bt[hl // 2][2]])
            P.tr(d[:, 128:256], Pm1[:, hl, 0:128], ident)
            t_ptr = P.tr(bt[2][1][:, 128 * hl:128 * hl + 128], Pm1[:, hl, 128:256], ident, after=[bt[2][2]])
        for j in range(2):
            t = P.act(PT0[:, 2 * j:2 * j + 2, :], bt[j][1][:, :].rearrange("p (a n) -> p a n", a=2), ACT.Copy, after=[t_ptr, t_pv])
            B.free(bt[j][0], t)
        t = P.act(PT1[:, :, :], bt[2][1][:, :].rearrange("p (a n) -> p a n", a=4), ACT.Copy)
        B.free(bt[2][0], t)
        b, ps, tf = B.get()
        for j in range(2):
            for r in range(2):
                hl = 2 * j + r
                hd = 4 * g + hl
                o = 64 * r
                P.mm(ps[o:o + 64, 256 * j:256 * j + 256], V[:, 0, 64 * hd:64 * hd + 64], PT0[:, hl, :], True, False, after=[t, t_v, tf])
                t_pv = P.mm(ps[o:o + 64, 256 * j + 128:256 * j + 256], V[:, 1, 64 * hd:64 * hd + 64], PT1[:, hl, :], False, True)
        t_oa = split(OAh[:, 2 * g:2 * g + 2, :], OAl[:, 2 * g:2 * g + 2, :], ps[:, :].rearrange("p (a n) -> p a n", a=2), [t_pv])
        B.free(b, t_oa)

    G2 = R("G2", [128, 8, 256], F32, 26 * KB)
    P.barrier()

    def ev_gate2(f, n, ps, t):
        t_g[0] = P.act(G2[:, f:f + n, :], ps, ACT.Sigmoid, after=[t])
        return t_g[0]

    linear(w_in, 6848, 1024, xh, xl, 8, t_u, ev_gate2)
    t_g0 = t_g[0]
    MXh, MXl = R("MXh", [128, 8, 256], F32R, 34 * KB), R("MXl", [128, 8, 256], F32R, 42 * KB)

    def ev_mla(f, n, ps, t):
        t = P.tt(G2[:, f:f + n, :], G2[:, f:f + n, :], ps, ALU.mult, after=[t, t_g0])
        P.tt(G[:, f:f + n, :], G[:, f:f + n, :], G2[:, f:f + n, :], ALU.add, after=[t_gs])
        t_g[0] = t_mx[0] = split(MXh[:, f:f + n, :], MXl[:, f:f + n, :], G[:, f:f + n, :], P.last())
        return t

    t_mx = [None]
    linear(I["w_mla_out"][0], 0, 1024, OAh, OAl, 8, t_oa, ev_mla)

    def ev_res(f, n, ps, t):
        t_g[0] = P.tt(H[:, f:f + n, :], H[:, f:f + n, :], ps, ALU.add, after=[t])
        return t_g[0]

    linear(I["w_o"][0], 0, 1024, MXh, MXl, 8, t_mx[0], ev_res)
    t_h = t_g[0]
    tap("h1", H[:, :, :], t_h)

    P.barrier()
    memin, memT = R("memin", [128, 2, 1024], F32, 0), R("memT", [128, 8, 256], F32, 8 * KB)
    t_mem = P.dma(memin[:, :, :], I["mem"][0].rearrange("(t p) d -> p t d", p=128), "mem", after=P.last())
    for d0 in range(0, 8, 2):
        b, ps, tf = B.get()
        for j in range(4):
            t = P.tr(ps[:, 128 * j:128 * j + 128], memin[:, j % 2, (d0 + j // 2) * 128:(d0 + j // 2 + 1) * 128],
                     ident, after=[t_mem, t_c, tf])
        t_memT = P.copy(memT[:, d0:d0 + 2, :], ps[:, :].rearrange("p (a n) -> p a n", a=2), after=[t])
        B.free(b, t_memT)

    MMh, MMl = R("MMh", [128, 8, 256], F32R, 16 * KB), R("MMl", [128, 8, 256], F32R, 24 * KB)
    XVh, XVl = R("XVh", [128, 8, 256], F32R, 32 * KB), R("XVl", [128, 8, 256], F32R, 40 * KB)
    t_mm = norm_split(memT, 8, 1024, col["norm_mem"], MMh[:, :, :], MMl[:, :, :], [t_memT])
    t_xv = norm_split(H, 8, 1024, col["norm_xattn"], XVh[:, :, :], XVl[:, :, :], [t_h])
    q2, k2 = R("q2", [128, 8, 256], F32, 48 * KB), R("k2", [128, 8, 256], F32, 56 * KB)
    v2 = R("v2", [128, 2, 1024], F32, 64 * KB)

    def ev_to(dst):
        def ev(f, n, ps, t):
            t_g[0] = P.act(dst[:, f:f + n, :], ps, ACT.Copy, after=[t])
            return t_g[0]
        return ev

    def ev_tok(dst):
        def ev(c, ps, t):
            t_g[0] = P.act(dst[:, :, c:c + 256], ps, ACT.Copy, after=[t])
            return t_g[0]
        return ev

    linear(I["w_xkv"][0], 0, 1024, MMh, MMl, 8, t_mm, ev_to(k2))
    linear_tok(I["w_xkv"][0], 1024, 1024, MMh, MMl, 8, t_mm, ev_tok(v2))
    linear(I["w_xq"][0], 0, 1024, XVh, XVl, 8, t_xv, ev_to(q2))
    t_qkv = t_g[0]
    Px = [R(f"Px{j}", [128, 4, 256], F32, (16 + 4 * j) * KB) for j in range(2)]
    PXT = [R(f"PXT{j}", [128, 4, 256], F32, (24 + 4 * j) * KB) for j in range(2)]
    OXh, OXl = R("OXh", [128, 8, 256], F32R, 0), R("OXl", [128, 8, 256], F32R, 8 * KB)
    toks = []
    for j in range(2):
        bs = [B.get() for _ in range(2)]
        for hd in range(4):
            d = bs[hd // 2][1][:, 256 * (hd % 2):256 * (hd % 2) + 256]
            for e in range(2):
                t = P.mm(d, q2[:, 2 * hd + e, 128 * j:128 * j + 128], k2[:, 2 * hd + e, :], e == 0, e == 1, after=[t_qkv, bs[hd // 2][2]])
        for r in range(2):
            t2 = P.ts(Px[j][:, 2 * r:2 * r + 2, :], bs[r][1][:, :].rearrange("p (a n) -> p a n", a=2), 1.0 / 16, None, ALU.mult, after=[t])
            B.free(bs[r][0], t2)
        sj = sm[:, 64 * j:64 * j + 64]
        P.red(sj[:, 0:4], Px[j][:, :, :], ALU.max)
        t = P.ts(sj[:, 8:12], sj[:, 0:4], -1.0, None, ALU.mult)
        for hd in range(4):
            t2 = P.act(Px[j][:, hd, :], Px[j][:, hd, :], ACT.Exp, after=[t], bias=sj[:, 8 + hd:9 + hd], accum_out=sj[:, 16 + hd:17 + hd])
        P.put("dve", lambda e, sj=sj: e.reciprocal(sj[:, 24:28], sj[:, 16:20]), [t2])
        toks.append(P.tt(Px[j][:, :, :], Px[j][:, :, :], sj[:, 24:28].unsqueeze(2).broadcast_to([128, 4, 256]), ALU.mult))
    for mj in range(2):
        for r in range(2):
            b, ps, tf = B.get()
            for a in range(2):
                for j in range(2):
                    t = P.tr(ps[:, 256 * a + 128 * j:256 * a + 128 * j + 128], Px[j][:, 2 * r + a, 128 * mj:128 * mj + 128], ident, after=[toks, tf])
            t_px = P.act(PXT[mj][:, 2 * r:2 * r + 2, :], ps[:, :].rearrange("p (a n) -> p a n", a=2), ACT.Copy, after=[t])
            B.free(b, t_px)
    for hd in range(4):
        b, ps, tf = B.get()
        for e in range(2):
            for mj in range(2):
                t = P.mm(ps[:, 256 * e:256 * e + 256], v2[:, mj, 256 * hd + 128 * e:256 * hd + 128 * e + 128],
                         PXT[mj][:, hd, :], mj == 0, mj == 1, after=[t_px, tf])
        t_ox = split(OXh[:, 2 * hd:2 * hd + 2, :], OXl[:, 2 * hd:2 * hd + 2, :], ps[:, :].rearrange("p (a n) -> p a n", a=2), [t])
        B.free(b, t_ox)
    linear(I["w_xo"][0], 0, 1024, OXh, OXl, 8, t_ox, ev_res)
    t_h = t_g[0]
    tap("h2", H[:, :, :], t_h)

    P.barrier()
    t_xt = norm_split(H, 8, 1024, col["norm_moe"], XUh[:, :, :], XUl[:, :, :], [t_h])
    CBt = R("CBt", [128, 32, 256], F32, 0)
    lg = R("lg", [128, 2, 40], F32, 32 * KB)
    rt = R("rt", [128, 256], F32, 33 * KB)
    comb = R("comb", [128, 2, 128], F32, 34 * KB)
    combT = R("combT", [128, 256], F32, 35 * KB)
    h, l, tw, i = W.next([(0, 8, 4, kp(I["w_router_group"][0], 8)), (4, 8, 32, kp(I["w_router_expert"][0], 8))])
    b, ps, tf = B.get()
    for j in range(2):
        t = triple(ps[:, 64 * j:64 * j + 36], lambda k: XUh[:, k, 128 * j:128 * j + 128], lambda k: XUl[:, k, 128 * j:128 * j + 128],
                   lambda k: h[:, k, :], lambda k: l[:, k, :], 8, True, True, [tw, tf, t_xt])
    W.free(i, t)
    t = P.tt(lg[:, :, 0:36], ps[:, 0:128].rearrange("p (a n) -> p a n", a=2)[:, :, 0:36],
             brt[:, 0:36].unsqueeze(1).broadcast_to([128, 2, 36]), ALU.add, after=[t, t_c])
    B.free(b, t)
    tap("lg", lg[:, :, 0:36], t)

    def first_of(dst, v, mx, n, s):
        P.ts(dst, v, mx, None, ALU.is_equal)
        P.ts(s, dst, -1000.0, 1000.0, ALU.mult, ALU.add)
        P.tt(s, s, iota[:, 0:n], ALU.add)
        P.red(rt[:, 255:256], s, ALU.min)
        return P.ts(dst, iota[:, 0:n], rt[:, 255:256], None, ALU.is_equal)

    tzc = P.put("dve", lambda e: e.memset(comb[:, :, :], 0.0), None)
    for j in range(2):
        gl, el = lg[:, j, 0:4], lg[:, j, 4:36]
        gm, ng, gs, gw = (rt[:, i:i + 1] for i in range(0, 4))
        og, s4, e4 = rt[:, 8:12], rt[:, 12:16], rt[:, 16:20]
        ein, o1, o2, s8, ea = rt[:, 24:32], rt[:, 32:40], rt[:, 40:48], rt[:, 48:56], rt[:, 56:64]
        m1, m2, dl, w2, w1, dn = (rt[:, i:i + 1] for i in range(64, 70))
        big = rt[:, 96:128].rearrange("p (g e) -> p g e", g=4)
        P.red(gm, gl, ALU.max)
        t = P.ts(ng, gm, -1.0, None, ALU.mult)
        t = P.act(e4, gl, ACT.Exp, after=[t], bias=ng, accum_out=gs)
        P.put("dve", lambda e, gw=gw, gs=gs: e.reciprocal(gw, gs), [t])
        first_of(og, gl, gm, 4, s4)
        P.tt(big, el.rearrange("p (g e) -> p g e", g=4), og.unsqueeze(2).broadcast_to([128, 4, 8]), ALU.mult)
        P.tt(ein, big[:, 0, :], big[:, 1, :], ALU.add)
        P.tt(ein, ein, big[:, 2, :], ALU.add)
        P.tt(ein, ein, big[:, 3, :], ALU.add)
        P.red(m1, ein, ALU.max)
        first_of(o1, ein, m1, 8, s8)
        P.ts(ea, o1, -3.0e38, None, ALU.mult)
        P.tt(ea, ein, ea, ALU.add)
        P.red(m2, ea, ALU.max)
        first_of(o2, ea, m2, 8, s8)
        t = P.tt(dl, m2, m1, ALU.subtract)
        t = P.act(w2, dl, ACT.Exp, after=[t])
        P.ts(dn, w2, 1.0, None, ALU.add, after=[t])
        P.put("dve", lambda e, w1=w1, dn=dn: e.reciprocal(w1, dn), None)
        P.tt(w1, w1, gw, ALU.mult)
        P.tt(w2, w2, w1, ALU.mult)
        P.ts(o1, o1, w1, None, ALU.mult)
        P.stt(o1, o2, w2, o1, ALU.mult, ALU.add)
        t = P.tt(comb[:, j, 0:32].rearrange("p (g e) -> p g e", g=4), o1.unsqueeze(1).broadcast_to([128, 4, 8]),
                 og.unsqueeze(2).broadcast_to([128, 4, 8]), ALU.mult)
    b, ps, tf = B.get()
    for j in range(2):
        t2 = P.tr(ps[:, 128 * j:128 * j + 128], comb[:, j, :], ident, after=[t, tf])
    t = P.copy(combT[:, :], ps[:, 0:256], after=[t2])
    B.free(b, t)
    tap("combT", combT[0:32, :], t)
    for q in range(16):
        b, ps, tf = B.get()
        for j in range(2):
            e = 2 * q + j
            t2 = P.mm(ps[:, 256 * j:256 * j + 256], ident[0:32, e:e + 1].broadcast_to([32, 128]), combT[0:32, :], after=[t, tf])
        t_cb = P.act(CBt[:, 2 * q:2 * q + 2, :], ps[:, :].rearrange("p (a n) -> p a n", a=2), ACT.Copy, after=[t2])
        B.free(b, t_cb)

    def gated(pfx, steps, xh, xl, ready):
        hs = [R(f"{pfx}hs{j}", [128, 2, 256], F32, (40 + 2 * j) * KB) for j in range(2)]
        ah = [R(f"{pfx}ah{j}", [128, 2, 256], F32R, (44 + 2 * j) * KB) for j in range(2)]
        al = [R(f"{pfx}al{j}", [128, 2, 256], F32R, (48 + 2 * j) * KB) for j in range(2)]
        ybanks = [B.banks[4 + j] for j in range(4)]
        yfree = flat([B.tok[4 + j] for j in range(4)])
        n = len(steps)
        used = [None, None]

        def up(e):
            g, u, _, scale, ts = steps[e]
            res = []
            for w in (g, u):
                h, l, tw, i = W.next([(0, 8, 256, kp(w, 8))])
                b, ps, tf = B.get(range(4))
                for j in range(2):
                    t = triple(ps[:, 256 * j:256 * j + 256], lambda k: h[:, k, 128 * j:128 * j + 128],
                               lambda k: l[:, k, 128 * j:128 * j + 128], lambda k: xh[:, k, :], lambda k: xl[:, k, :],
                               8, True, True, [tw, tf, ready])
                W.free(i, t)
                res.append((b, ps[:, :].rearrange("p (a n) -> p a n", a=2), t))
            s = e % 2
            (bg, pg, tg), (bu, pu, tu) = res
            t = P.act(hs[s][:, :, :], pg, ACT.Silu, after=[tg, used[s]])
            B.free(bg, t)
            t = P.tt(hs[s][:, :, :], hs[s][:, :, :], pu, ALU.mult, after=[t, tu])
            B.free(bu, t)
            if scale is not None:
                t = P.tt(hs[s][:, :, :], hs[s][:, :, :], scale.unsqueeze(1).broadcast_to([128, 2, 256]), ALU.mult, after=[ts])
            return split(ah[s][:, :, :], al[s][:, :, :], hs[s][:, :, :], [t, used[s]])

        def down(e, ta):
            h, l, tw, i = W.next([(0, 2, 1024, kp(steps[e][2], 2))])
            s = e % 2
            for d in range(8):
                ps = ybanks[d // 2][:, 256 * (d % 2):256 * (d % 2) + 256]
                for k in range(2):
                    st, sp = e == 0 and k == 0 and d % 2 == 0, e == n - 1 and k == 1
                    c = slice(128 * d, 128 * d + 128)
                    P.mm(ps, h[:, k, c], ah[s][:, k, :], st, False, after=[tw, ta, yfree], loose=True)
                    P.mm(ps, h[:, k, c], al[s][:, k, :], False, False, loose=True)
                    t = P.mm(ps, l[:, k, c], ah[s][:, k, :], False, sp, loose=True)
            W.free(i, t)
            used[s] = t
            return t

        ta = up(0)
        for e in range(n):
            tb = up(e + 1) if e + 1 < n else None
            t = down(e, ta)
            ta = tb
        return [y[:, :].rearrange("p (a n) -> p a n", a=2) for y in ybanks], t

    wg, wu, wd = I["w_exp_gate"][0], I["w_exp_up"][0], I["w_exp_down"][0]
    ys, t = gated("moe", [(wg[e], wu[e], wd[e], CBt[:, e, :], t_cb) for e in range(32)], XUh, XUl, t_xt)
    for j in range(4):
        t_h = P.tt(H[:, 2 * j:2 * j + 2, :], H[:, 2 * j:2 * j + 2, :], ys[j], ALU.add, after=[t])
        B.free(4 + j, t_h)
    t_h = norm(H, 8, 1024, col["norm_final"], H, [t_h])
    tap("h3", H[:, :, :], t_h)

    P.barrier()
    reset = R("reset", [128, 1024], F32, 70 * KB)
    t_reset = P.dma(reset[:, :], I["c_reset"], "reset", after=P.last())
    t_u2 = norm_split(H, 8, 1024, col["attn_pre_norm_2"], XUh[:, :, :], XUl[:, :, :], [t_h])
    w2 = I["w_in_2"][0]
    hq, hz = R("hq", [128, 4, 256], F32, 0), R("hz", [128, 4, 256], F32, 4 * KB)
    hv_, hg = R("hv", [128, 2, 512], F32, 8 * KB), R("hg", [128, 4, 256], F32, 12 * KB)
    sq_, sk_ = R("sq", [128, 4, 256], F32, 16 * KB), R("sk", [128, 4, 256], F32, 20 * KB)
    sv_ = R("sv", [128, 2, 512], F32, 24 * KB)

    def ev_f(dst, func):
        def ev(f, n, ps, t):
            t_g[0] = P.act(dst[:, f:f + n, :], ps, func, after=[t])
            return t_g[0]
        return ev

    linear(w2, 0, 512, XUh, XUl, 8, t_u2, ev_f(hq, ACT.Silu))
    linear(w2, 1536, 512, XUh, XUl, 8, t_u2, ev_f(hg, ACT.Silu))
    linear(w2, 512, 512, XUh, XUl, 8, t_u2, ev_f(hz, ACT.Copy))
    linear_tok(w2, 1024, 512, XUh, XUl, 8, t_u2, ev_tok(hv_))
    linear(w2, 2048, 512, XUh, XUl, 8, t_u2, ev_f(sq_, ACT.Copy))
    linear(w2, 2560, 512, XUh, XUl, 8, t_u2, ev_f(sk_, ACT.Copy))
    linear_tok(w2, 3072, 512, XUh, XUl, 8, t_u2, ev_tok(sv_))
    t_in = t_g[0]
    tap("hz", hz[:, :, :], t_in)
    tap("hq", hq[:, :, :], t_in)

    gam = col["hg_lower_gamma_2"]
    lb = mem["lb"]
    P.tt(lb[:, 0:4], gam[:, 0:4], gam[:, 4:8], ALU.max, after=[t_vec])
    P.tt(lb[:, 4:8], gam[:, 0:4], lb[:, 0:4], ALU.subtract)
    t = P.tt(lb[:, 8:12], gam[:, 4:8], lb[:, 0:4], ALU.subtract)
    t = P.act(lb[:, 12:20], lb[:, 4:12], ACT.Exp, after=[t])
    t = P.tt(lb[:, 20:24], lb[:, 12:16], lb[:, 16:20], ALU.add, after=[t])
    t = P.act(lb[:, 20:24], lb[:, 20:24], ACT.Ln, after=[t])
    P.tt(lb[:, 24:28], lb[:, 4:8], lb[:, 20:24], ALU.subtract, after=[t])
    t = P.tt(lb[:, 28:32], lb[:, 8:12], lb[:, 20:24], ALU.subtract)
    lA = lb[:, 24:28].unsqueeze(2).broadcast_to([128, 4, 256])
    lC = lb[:, 28:32].unsqueeze(2).broadcast_to([128, 4, 256])
    e1, e2, e3 = (R(f"he{j}", [128, 4, 256], F32, (28 + 4 * j) * KB) for j in range(3))
    hk, hb = R("hk", [128, 4, 256], F32, 40 * KB), R("hb", [128, 4, 256], F32, 44 * KB)
    a = lambda x: x[:, :, :]
    t = P.act(a(e1), a(hz), ACT.Abs, after=[t_in])
    t = P.act(a(e1), a(e1), ACT.Exp, after=[t], scale=-1.0)
    t = P.act(a(e1), a(e1), ACT.Ln, bias=1.0, scale=1.0)
    P.stt(a(e2), a(hz), 0.0, a(e1), ALU.min, ALU.subtract, after=[t])
    P.tt(a(e2), a(e2), lC, ALU.add)
    t = P.tt(a(hk), a(e2), a(hz), ALU.subtract)
    t_hk = P.act(a(hk), a(hk), ACT.Exp, after=[t])
    P.tt(a(e3), a(e2), lA, ALU.max)
    t = P.tt(a(e2), a(e2), lA, ALU.subtract)
    t = P.act(a(e2), a(e2), ACT.Abs, after=[t])
    t = P.act(a(e2), a(e2), ACT.Exp, after=[t], scale=-1.0)
    t = P.act(a(e2), a(e2), ACT.Ln, bias=1.0, scale=1.0)
    P.tt(a(e3), a(e3), a(e2), ALU.add, after=[t])
    t_b = P.put("dve", lambda e: e.tensor_tensor_scan(hb[:, :, :].rearrange("p a n -> p (a n)"), reset[:, :],
                                                      e3[:, :, :].rearrange("p a n -> p (a n)"), 0.0, ALU.mult, ALU.add), [t_reset])
    tap("hb", a(hb), t_b)
    tap("hk", a(hk), [t_b, t_hk])
    SC0, SC1 = R("SC0", [128, 4, 256], F32, 48 * KB), R("SC1", [128, 4, 128], F32, 52 * KB)
    Xs = [R(f"X{j}", [128, 4, 256], F32, (54 + 4 * j) * KB) for j in range(2)]
    diag = [SC0[:, :, 0:128], SC1[:, :, :]]
    id4 = ident.unsqueeze(1).broadcast_to([128, 4, 128])
    for j in range(2):
        b, ps, tf = B.get()
        for hd in range(4):
            t = P.mm(ps[:, 128 * hd:128 * hd + 128], hk[:, hd, 128 * j:128 * j + 128], hq[:, hd, 128 * j:128 * j + 128], after=[t_hk, t_in, tf])
        t_sc = P.tt(diag[j], ps[:, :].rearrange("p (a n) -> p a n", a=4), id4, ALU.mult, after=[t])
        B.free(b, t_sc)
    xt = [None, None]
    for lv in range(8):
        L = 2 << lv
        m = L // 2
        X = Xs[lv % 2]
        if L <= 64:
            v = lambda z: z[:, :, :].rearrange("p a (n l) -> p (a n) l", l=L)
            nb = 1024 // L
            mid = v(hb)[:, :, m - 1:m].broadcast_to([128, nb, m])
            P.tt(v(X)[:, :, 0:m], mid, v(hb)[:, :, 0:m], ALU.subtract, after=[t_b, xt[lv % 2]])
            t = P.tt(v(X)[:, :, m:L], v(hb)[:, :, m:L], mid, ALU.subtract)
        elif L == 128:
            v = lambda z: z[:, :, :].rearrange("p a (n l) -> p (a n) l", l=128)
            mid = v(hb)[:, :, 63:64].broadcast_to([128, 8, 64])
            P.tt(v(X)[:, :, 0:64], mid, v(hb)[:, :, 0:64], ALU.subtract, after=[xt[lv % 2]])
            t = P.copy(v(X)[:, :, 64:128], v(hb)[:, :, 64:128])
        else:
            v = lambda z: z[:, :, :]
            m = 128
            en = lambda c: hb[:, :, 64 * c + 63:64 * c + 64].broadcast_to([128, 4, 64])
            sl = lambda z, c: z[:, :, 64 * c:64 * c + 64]
            P.tt(sl(X, 0), en(0), sl(hb, 0), ALU.subtract, after=[xt[lv % 2]])
            P.tt(sl(X, 0), sl(X, 0), en(1), ALU.add)
            P.tt(sl(X, 1), en(1), sl(hb, 1), ALU.subtract)
            P.copy(sl(X, 2), sl(hb, 2))
            t = P.tt(sl(X, 3), sl(hb, 3), en(2), ALU.add)
        t = P.act(a(X), a(X), ACT.Exp, after=[t])
        if L == 256:
            P.tt(X[:, :, 0:128], X[:, :, 0:128], hk[:, :, 0:128], ALU.mult, after=[t, t_hk])
            t = P.tt(X[:, :, 128:256], X[:, :, 128:256], hq[:, :, 128:256], ALU.mult)
            b, ps, tf = B.get()
            for hd in range(4):
                t2 = P.mm(ps[:, 128 * hd:128 * hd + 128], X[:, hd, 0:128], X[:, hd, 128:256], after=[t, tf])
            t_sc = P.copy(SC0[:, :, 128:256], ps[:, :].rearrange("p (a n) -> p a n", a=4), after=[t2])
            B.free(b, t_sc)
        else:
            P.tt(v(X)[:, :, 0:m], v(X)[:, :, 0:m], v(hk)[:, :, 0:m], ALU.mult, after=[t, t_hk])
            t = P.tt(v(X)[:, :, m:L], v(X)[:, :, m:L], v(hq)[:, :, m:L], ALU.mult)
            mk = masks[:, 128 * lv:128 * lv + 128].unsqueeze(1).broadcast_to([128, 4, 128])
            for j in range(2):
                b, ps, tf = B.get()
                for hd in range(4):
                    s = X[:, hd, 128 * j:128 * j + 128]
                    t2 = P.mm(ps[:, 128 * hd:128 * hd + 128], s, s, after=[t, tf])
                t_sc = P.put("dve", lambda e, j=j, mk=mk, ps=ps: e.copy_predicated(
                    diag[j], mk, ps[:, :].rearrange("p (a n) -> p a n", a=4)), [t2])
                B.free(b, t_sc)
            xt[lv % 2] = t2
    tap("SC0", SC0[:, :, :], t_sc)
    oh = R("oh", [128, 4, 256], F32, 28 * KB)
    for q in range(2):
        b, ps, tf = B.get()
        for r in range(2):
            hd = 2 * q + r
            d = ps[:, 256 * r:256 * r + 256]
            P.mm(d, hv_[:, 0, 128 * hd:128 * hd + 128], SC0[:, hd, :], True, False, after=[t_sc, tf])
            t = P.mm(d[:, 128:256], hv_[:, 1, 128 * hd:128 * hd + 128], SC1[:, hd, :], False, True)
        t_oh = P.copy(oh[:, 2 * q:2 * q + 2, :], ps[:, :].rearrange("p (a n) -> p a n", a=2), after=[t])
        B.free(b, t_oh)
    MIh, MIl = R("MIh", [128, 8, 256], F32R, 62 * KB), R("MIl", [128, 8, 256], F32R, 0)
    t = norm(oh, 4, 512, col["hg_out_norm_2"], T8b, [t_oh])
    t = P.tt(T8b[:, 0:4, :], T8b[:, 0:4, :], a(hg), ALU.mult)
    tap("ohg", T8b[:, 0:4, :], t)
    t_mi = split(MIh[:, 0:4, :], MIl[:, 0:4, :], T8b[:, 0:4, :], [t])

    osb = R("osb", [128, 4, 256], F32, 32 * KB)
    Z = R("Z", [128, 4, 384], F32, 36 * KB)
    Sp = R("Sp", [128, 4, 384], F32, 42 * KB)
    P.barrier()
    t_pv = None
    for g in range(2):
        for hl in range(4):
            hd = 4 * g + hl
            o, tl = 64 * (hd % 2), hd // 2
            b, ps, tf = B.get()
            P.mm(ps[:, 0:256], sk_[o:o + 64, tl, 0:128], sq_[o:o + 64, tl, :], after=[t_in, tf])
            t = P.mm(ps[:, 256:384], sk_[o:o + 64, tl, 128:256], sq_[o:o + 64, tl, 128:256])
            P.stt(Z[:, hl, 0:128], ps[:, 0:128], 0.125, n_st, ALU.mult, ALU.add, after=[t, t_pv])
            P.ts(Z[:, hl, 128:256], ps[:, 128:256], 0.125, None, ALU.mult)
            t = P.stt(Z[:, hl, 256:384], ps[:, 256:384], 0.125, n_st, ALU.mult, ALU.add)
            B.free(b, t)
        t = P.act(a(Sp), a(Z), ACT.Abs, after=[t, t_pv])
        t = P.act(a(Sp), a(Sp), ACT.Exp, after=[t], scale=-1.0)
        t = P.act(a(Sp), a(Sp), ACT.Ln, bias=1.0, scale=1.0)
        t_sp = P.stt(a(Sp), a(Z), 0.0, a(Sp), ALU.max, ALU.add, after=[t])
        for hl in range(4):
            b, ps, tf = B.get()
            P.mm(ps[:, 0:256], tri, Sp[:, hl, 0:256], True, False, after=[t_sp, tf])
            P.mm(ps[:, 128:256], ones[:, :], Sp[:, hl, 256:384], False, True)
            t = P.mm(ps[:, 256:384], tri, Sp[:, hl, 256:384])
            t = P.tt(Z[:, hl, :], Z[:, hl, :], ps[:, 0:384], ALU.subtract, after=[t])
            B.free(b, t)
        t = P.act(a(Z), a(Z), ACT.Exp, after=[t])
        b, ps, tf = B.get()
        for hl in range(4):
            hd = 4 * g + hl
            o = 64 * (hl % 2)
            d = ps[o:o + 64, 256 * (hl // 2):256 * (hl // 2) + 256]
            P.mm(d, sv_[:, 0, 64 * hd:64 * hd + 64], Z[:, hl, 0:256], True, False, after=[t, tf])
            t_pv = P.mm(d[:, 128:256], sv_[:, 1, 64 * hd:64 * hd + 64], Z[:, hl, 256:384], False, True)
        t_os = P.copy(osb[:, 2 * g:2 * g + 2, :], ps[:, :].rearrange("p (a n) -> p a n", a=2), after=[t_pv])
        B.free(b, t_os)
    tap("osb", osb[:, :, :], t_os)
    t_mi = norm_split(osb, 4, 512, col["sb_out_norm_2"], MIh[:, 4:8, :], MIl[:, 4:8, :], [t_os])

    mx = R("mx", [128, 8, 256], F32, 48 * KB)
    linear(I["w_out_2"][0], 0, 1024, MIh, MIl, 8, t_mi, ev_to(mx))

    def post(src, gain, after):
        t = norm(src, 8, 1024, gain, T8b, after)
        return P.tt(H[:, :, :], H[:, :, :], T8b[:, :, :], ALU.add)

    t_h = post(mx, col["attn_post_norm_2"], [t_g[0]])
    tap("h4", H[:, :, :], t_h)

    P.barrier()
    t_u3 = norm_split(H, 8, 1024, col["ffn_pre_norm_2"], XUh[:, :, :], XUl[:, :, :], [t_h])
    pin = R("pin", [128, 2, 256], F32, 0)
    pT = R("pT", [128, 2, 256], F32, 2 * KB)
    PTh, PTl = R("PTh", [128, 2, 256], F32R, 4 * KB), R("PTl", [128, 2, 256], F32R, 6 * KB)
    wgu, wdn = I["w_gate_up_2"][0], I["w_down_2"][0]
    ys, t = gated("ffn", [(wgu[:, 256 * c:256 * c + 256], wgu[:, 2816 + 256 * c:2816 + 256 * c + 256],
                           wdn[256 * c:256 * c + 256, :], None, None) for c in range(11)], XUh, XUl, t_u3)
    ff = R("ff", [128, 8, 256], F32, 52 * KB)
    for j in range(4):
        t2 = P.copy(ff[:, 2 * j:2 * j + 2, :], ys[j], after=[t])
        B.free(4 + j, t2)
    t_h = post(ff, col["ffn_post_norm_2"], [t2])
    tap("h5", H[:, :, :], t_h)

    t_p = P.dma(pin[:, :, :], I["p_2"][0, 0].rearrange("(t p) d -> p t d", p=128), "p", after=[t_u3])
    b, ps, tf = B.get()
    for j in range(4):
        t = P.tr(ps[:, 128 * j:128 * j + 128], pin[:, j % 2, 128 * (j // 2):128 * (j // 2) + 128], ident, after=[t_p, tf])
    t = P.copy(pT[:, :, :], ps[:, :].rearrange("p (a n) -> p a n", a=2), after=[t])
    B.free(b, t)
    t_pt = split(PTh[:, :, :], PTl[:, :, :], pT[:, :, :], [t])
    t_hx = split(XUh[:, :, :], XUl[:, :, :], H[:, :, :], [t_h] + P.last())
    pg = R("pg", [128, 8, 256], F32, 60 * KB)
    linear(I["ple_gate_2"][0], 0, 1024, XUh, XUl, 8, t_hx, ev_f(pg, ACT.Sigmoid))
    t_pg = t_g[0]

    def ev_ple(f, n, ps, t):
        t = P.tt(pg[:, f:f + n, :], pg[:, f:f + n, :], ps, ALU.mult, after=[t, t_pg])
        t_g[0] = P.tt(H[:, f:f + n, :], H[:, f:f + n, :], pg[:, f:f + n, :], ALU.add, after=[t_h])
        return t

    linear(I["ple_proj_2"][0], 0, 1024, PTh, PTl, 2, t_pt, ev_ple, k_cols=256)
    t_h = t_g[0]
    ot = R("ot", [128, 2, 1024], F32, 68 * KB)
    for j in range(2):
        for q in range(2):
            b, ps, tf = B.get()
            for r in range(4):
                t = P.tr(ps[:, 128 * r:128 * r + 128], H[:, 4 * q + r, 128 * j:128 * j + 128], ident, after=[t_h, tf])
            t = P.copy(ot[:, j, 512 * q:512 * q + 512], ps[:, :], after=[t])
            B.free(b, t)
        P.dma(out[0, 128 * j:128 * j + 128, :], ot[:, j, :], "out", after=[t])
    return W.rec


def build(nc, I, out, taps=None):
    base = (nc.sbuf_base + 63) // 64 * 64
    at = [base]
    used = set()

    def sb(name, shape, dt, offset=None):
        n = 1
        for s in shape[1:]:
            n *= s
        n *= 1 if dt == U8 else 4
        if offset is None:
            offset = at[0]
            at[0] += (n + 63) // 64 * 64
        return nc.alloc_sbuf_tensor_at(name, shape, dt, offset=offset)

    mem = {"sb": sb}
    mem["raw"] = [sb(f"raw{i}", [128, PIECE], F32) for i in range(NRAW)]
    mem["hi"] = [sb(f"whi{i}", [128, PIECE], F32R) for i in range(NSPL)]
    mem["lo"] = [sb(f"wlo{i}", [128, PIECE], F32R) for i in range(NSPL)]
    mem["XUh"], mem["XUl"] = sb("XUh", [128, 8, 256], F32R), sb("XUl", [128, 8, 256], F32R)
    mem["H"] = sb("H", [128, 8, 256], F32)
    mem["T8"] = sb("T8", [128, 8, 256], F32)
    mem["T8b"] = sb("T8b", [128, 8, 256], F32)
    mem["cst"] = sb("cst", [128, 896], F32)
    mem["ones"] = sb("ones", [128, 128], F32)
    mem["masks"] = sb("masks", [128, 896], U8)
    mem["vec"] = sb("vec", [128, 256], F32)
    mem["small"] = sb("small", [128, 64], F32)
    mem["brt"] = sb("brt", [128, 36], F32)
    mem["rs"] = sb("rs", [128, 2, 256], F32)
    mem["cs"] = sb("cs", [128, 2, 256], F32)
    mem["sm"] = sb("sm", [128, 128], F32)
    mem["lb"] = sb("lb", [128, 32], F32)
    top = nc.sbuf_usable_end // 64 * 64
    rbase = at[0]
    size = top - rbase
    made = {}

    def R(name, shape, dt, offset):
        if name not in made:
            n = 4
            for s in shape[1:]:
                n *= s
            assert offset + n <= size, (name, offset + n, size)
            made[name] = sb(name, shape, dt, rbase + offset)
        return made[name]

    mem["R"] = R
    mem["posi"] = R("posi", [128, 256], I32, 18 * KB)
    mem["ps"] = [nc.alloc_psum_tensor(f"ps{i}", [128, 512], F32) for i in range(8)]
    rec = program(nc, I, out, Prog(), mem, None, taps)
    P = Prog()
    program(nc, I, out, P, mem, rec, taps)
    sems = {n: nc.alloc_semaphore(f"s_{n}") for n in list(Prog.ENGINES) + sorted(P.count)}
    run = P.emit(nc, sems)
    with nc.Block() as block:

        @block.tensor
        def _(e):
            run("pe", e)

        @block.scalar
        def _(e):
            run("act", e)

        @block.vector
        def _(e):
            run("dve", e)

        @block.gpsimd
        def _(e):
            run("pool", e)

        @block.sync
        def _(e):
            run("sp", e)
            for n in ("out", "taps"):
                if n in P.count:
                    e.wait_ge(sems[n], P.count[n])


def kernel(**inputs):
    import concourse.bacc as bacc
    from concourse.bass_utils import run_bass_kernel_spmd

    nc = bacc.Bacc("TRN2", target_bir_lowering=False, num_devices=1)
    arrays = {f"in_{k}": np.ascontiguousarray(v) for k, v in inputs.items()}
    arrays.update({f"in_{k}": v for k, v in constants().items()})
    aps = {k[3:]: nc.dram_tensor(k, a.shape, mybir.dt.from_np(a.dtype), kind="ExternalInput").ap() for k, a in arrays.items()}
    out = nc.dram_tensor("out_0", (1, 256, 1024), F32, kind="ExternalOutput").ap()
    build(nc, aps, out)
    r = run_bass_kernel_spmd(nc, [arrays], core_ids=[0])
    return r.results[0]["out_0"]
```

```python
import numpy as np
import concourse.bass as bass
from concourse import mybir

F32 = mybir.dt.float32
F32R = mybir.dt.float32r
I32 = mybir.dt.int32
U8 = mybir.dt.uint8
ALU = mybir.AluOpType
ACT = mybir.ActivationFunctionType
AX = mybir.AxisListType
KB = 1024
NEG = -1.0e30
EPS = 1e-6

NRAW = 4
NSPL = 3
PIECE = 2048
CAP = 64


def flat(x):
    if x is None:
        return []
    if isinstance(x, list):
        return [t for y in x for t in flat(y)]
    return [x]


class Prog:

    ENGINES = ("pe", "act", "dve", "pool", "sp")

    def __init__(self, part):
        self.part = part
        self.q = {e: [] for e in self.ENGINES}
        self.held = {e: [] for e in self.ENGINES}
        self.end = {}
        self.count = {}
        self.table = self.TABLES[ACT.Ln if part in ("start", "end") else ACT.Silu]
        self.tables = {0: self.table}

    TABLES = {ACT.Ln: "natural_log_exp_and_others", ACT.Exp: "natural_log_exp_and_others",
              ACT.Silu: "silu_and_others", ACT.Sigmoid: "sigmoid_and_others", ACT.Sin: "silu_and_others"}

    def put(self, e, fn, after, chain=True):
        waits = flat(after) + self.held[e]
        self.held[e] = []
        if chain and e in ("act", "dve", "pool") and e in self.end:
            waits.append((e, self.end[e], self.part))
        self.end[e] = len(self.q[e])
        self.q[e].append((fn, waits, None))
        return e, len(self.q[e]) - 1, self.part

    def dma(self, out, in_, sem, after=None, eng="sp"):
        waits = flat(after) + self.held[eng]
        self.held[eng] = []
        self.count[sem] = self.count.get(sem, 0) + 16
        self.q[eng].append((lambda e: e.dma_start(out, in_), waits, sem))
        return "dma", sem, self.count[sem]

    def last(self):
        return [(e, self.end[e], self.part) for e in ("pe", "act", "dve", "pool") if e in self.end]

    def barrier(self):
        for e in ("pe", "act", "dve", "pool"):
            self.held[e] += [t for t in self.last() if t[0] != e]

    def act(self, out, in_, func, after=None, chain=True, **kw):
        table = self.TABLES.get(func, self.table)
        if table != self.table:
            self.table = self.tables[len(self.q["act"])] = table
        return self.put("act", lambda e: e.activation(out, in_, func, **kw), after, chain)

    def tt(self, out, a, b, op, after=None, chain=True):
        return self.put("dve", lambda e: e.tensor_tensor(out, a, b, op), after, chain)

    def ts(self, out, a, s1, s2, op0, op1=None, after=None):
        if op1 is None:
            return self.put("dve", lambda e: e.tensor_scalar(out, a, s1, None, op0), after)
        return self.put("dve", lambda e: e.tensor_scalar(out, a, s1, s2, op0, op1), after)

    def stt(self, out, a, s, b, op0, op1, after=None):
        return self.put("dve", lambda e: e.scalar_tensor_tensor(out=out, in0=a, scalar=s, in1=b, op0=op0, op1=op1), after)

    def red(self, out, a, op, after=None):
        return self.put("dve", lambda e: e.tensor_reduce(out, a, AX.X, op), after)

    def copy(self, out, a, after=None):
        return self.put("dve", lambda e: e.tensor_copy(out, a), after)

    def mm(self, out, lhsT, rhs, start=True, stop=True, after=None, loose=False):
        return self.put("pe", lambda e: e.matmul(out, lhsT, rhs, start=start, stop=stop, skip_group_check=loose), after)

    def tr(self, out, in_, ident, after=None):
        return self.put("pe", lambda e: e.transpose(out, in_, ident), after)

    def emit(self, nc, sems):
        need = {e: set() for e in self.ENGINES}
        plans = {}
        for e in self.ENGINES:
            seen, plan = {}, []
            for fn, waits, sem in self.q[e]:
                best = {}
                for t in waits:
                    if t[0] != "dma" and t[2] != self.part:
                        continue
                    key, n = (t[0], t[1]) if t[0] != "dma" else (("dma", t[1]), t[2])
                    if key == e and e in ("pe", "sp"):
                        continue
                    if n == "all":
                        n = self.count[t[1]]
                    best[key] = max(best.get(key, -1), n)
                todo = []
                for key, n in best.items():
                    if seen.get(key, -1) < n:
                        seen[key] = n
                        todo.append((key, n))
                        if isinstance(key, str):
                            need[key].add(n)
                plan.append((fn, todo, sem))
            plans[e] = plan
        for e, n, _ in self.last():
            need[e].add(n)
        value = {}
        for e in self.ENGINES:
            n, value[e] = 0, {}
            for i in sorted(need[e]):
                n += 1
                value[e][i] = n

        def run(e, eng):
            for i, (fn, todo, sem) in enumerate(plans[e]):
                if e == "act" and i in self.tables:
                    eng.preload_act_table_set(self.tables[i])
                for key, n in todo:
                    if isinstance(key, str):
                        eng.wait_ge(sems[key + self.part], value[key][n])
                    else:
                        eng.wait_ge(sems[key[1]], n)
                ins = fn(eng)
                if sem is not None:
                    ins.then_inc(sems[sem], 16)
                elif i in need[e]:
                    ins.then_inc(sems[e + self.part], 1)
            for key, n, _ in self.last():
                eng.wait_ge(sems[key + self.part], value[key][n])

        return run


class Weights:

    def __init__(self, P, raw, hi, lo, seq):
        self.P, self.raw, self.hi, self.lo, self.seq = P, raw, hi, lo, seq
        self.base, self.slots = 0, len(hi)
        self.rec = []
        self.nload = self.nsplit = self.i = 0
        self.limit = len(seq) if seq is not None else 0
        self.split_tok, self.load_tok, self.free_tok = {}, {}, {}

    def _load(self, j):
        views, n = self.seq[j][:2]
        s = j % NRAW
        tok = None
        for off, a, b, v in views:
            dst = self.raw[s][:, off:off + a * b].rearrange("p (a b) -> p a b", a=a) if len(views) == 1 else None
            if dst is None:
                tot = sum(x[2] for x in views)
                dst = self.raw[s][:, 0:a * tot].rearrange("p (a b) -> p a b", a=a)[:, :, off:off + b]
            tok = self.P.dma(dst, v, f"w{s}", after=self.split_tok.get(j - NRAW))
        self.load_tok[j] = tok

    def _split(self, j):
        n, maps = self.seq[j][1:]
        s, d = j % NRAW, (j - self.base) % self.slots
        raw, hi, lo = self.raw[s], self.hi[d], self.lo[d]
        for dst, src in maps or [(lambda x: x[:, 0:n], lambda x: x[:, 0:n])]:
            t = self.P.act(dst(hi), src(raw), ACT.Copy, after=[self.load_tok[j], self.free_tok.get(j - self.slots)], chain=False)
            self.split_tok[j] = self.P.tt(dst(lo), src(raw), dst(hi).bitcast(F32), ALU.subtract,
                                          after=[t, self.load_tok[j], self.free_tok.get(j - self.slots)], chain=False)

    def preload(self):
        while self.nload < NRAW:
            self._load(self.nload)
            self.nload += 1

    def ahead(self):
        while self.nsplit < self.limit and self.nsplit < self.i + self.slots and \
                (self.nsplit < self.slots or self.nsplit - self.slots in self.free_tok):
            while self.nload < len(self.seq) and self.nload <= self.nsplit:
                self._load(self.nload)
                self.nload += 1
            self._split(self.nsplit)
            self.nsplit += 1
        while self.nload < len(self.seq) and self.nload - NRAW < self.nsplit:
            self._load(self.nload)
            self.nload += 1

    def next(self, views, maps=None, out=None):
        kt, cols = views[0][1], sum(v[2] for v in views)
        n = kt * cols
        assert n <= PIECE
        self.rec.append((views, n, maps))
        if self.seq is None:
            i = self.i
            self.i += 1
            self.free_tok[i] = None
            d = 0
            tok = None
        else:
            i = self.i
            self.ahead()
            self.i += 1
            d = (i - self.base) % self.slots
            tok = self.split_tok[i]
        n = out or n
        assert n <= PIECE
        h = self.hi[d][:, 0:n].rearrange("p (a b) -> p a b", a=kt)
        l = self.lo[d][:, 0:n].rearrange("p (a b) -> p a b", a=kt)
        return h, l, tok, i

    def free(self, i, tok):
        self.free_tok[i] = tok

    def state(self):
        return self.nload, self.nsplit, self.i, dict(self.load_tok)

    def enter(self, P, state, limit, hi, lo):
        self.P, self.limit = P, limit
        self.nload, self.nsplit, self.i, load = state
        self.hi, self.lo, self.base, self.slots = hi, lo, self.i, len(hi)
        self.load_tok = dict(load)
        self.split_tok = {j: None for j in range(self.nsplit)}
        self.free_tok = {j: None for j in range(self.i)}


class Banks:
    def __init__(self, P, banks):
        self.P, self.banks, self.i = P, banks, 0
        self.tok = [None] * len(banks)

    def get(self, among=None):
        among = among or range(len(self.banks))
        among = list(among)
        b = among[self.i % len(among)]
        self.i += 1
        t, self.tok[b] = self.tok[b], None
        return b, self.banks[b], t

    def free(self, b, tok):
        self.tok[b] = flat(tok)


NCONST = 8


def constants():
    p = np.arange(128)
    ident = np.eye(128, dtype=np.float32)
    qk = np.where(p[None, :] <= p[:, None], 0.0, NEG).astype(np.float32)
    sl = np.where(p[None, :] >= p[:, None], 0.0, NEG).astype(np.float32)
    st = np.where(p[None, :] > p[:, None], 0.0, NEG).astype(np.float32)
    tri = (p[:, None] >= p[None, :]).astype(np.float32)
    perm = np.zeros((128, 128), np.float32)
    for m in range(128):
        if m % 32 < 16:
            perm[m + 16, m] = -1.0
        else:
            perm[m - 16, m] = 1.0
    inv = (np.float32(10000.0) ** (-(np.arange(16, dtype=np.float32)) / np.float32(16))).astype(np.float32)
    extra = np.zeros((128, 128), np.float32)
    extra[:, 0] = inv[p % 16]
    extra[:, 8:40] = np.arange(32, dtype=np.float32)[None, :]
    cst = np.concatenate([ident, qk, sl, st, tri, perm, extra], axis=1)
    masks = np.zeros((128, 7, 128), np.float32)
    for i in range(7):
        L = 2 << i
        same = (p[:, None] // L) == (p[None, :] // L)
        masks[:, i, :] = same & ((p[:, None] % L) < L // 2) & ((p[None, :] % L) >= L // 2)
    reset = np.tile((np.arange(1024) % 64 != 0).astype(np.float32)[None, :], (128, 1))
    slots = np.concatenate([np.tile(np.arange(256, dtype=np.float32)[None, :], (128, 1)),
                            (128 * np.arange(16)[None, :] + p[:, None]).astype(np.float32)], axis=1)
    return {"c_slots": slots, "c_mat": cst, "c_masks": masks.reshape(128, 7 * 128), "c_reset": reset}


def program(nc, I, out, parts, mem, seq, bounds, taps=None):
    P = parts["start"]
    W = Weights(P, mem["raw"], mem["hi"][:NSPL], mem["lo"][:NSPL], seq)
    W.limit = bounds[0]
    B = Banks(P, mem["ps"])
    ends = []

    def enter(name, state, limit, count, more=0):
        nonlocal P
        P = parts[name]
        P.count = dict(count)
        W.enter(P, state, limit, mem["hi"][:NSPL + more], mem["lo"][:NSPL + more])
        B.P = P
        B.tok = [None] * len(B.banks)
        busy[0] = None

    def tap(name, ap, after):
        if taps is not None:
            t = P.dma(taps[name], ap, "taps", after=after)
            for e in ("pe", "act", "dve"):
                P.held[e].append(t)

    def kp(v, kt):
        return v.rearrange("(k p) n -> p k n", p=128)

    XUh, XUl, H, T8, T8b = mem["XUh"], mem["XUl"], mem["H"], mem["T8"], mem["T8b"]
    cst, ones = mem["cst"], mem["ones"]
    ident = cst[:, 0:128]
    n_qk, n_sl, n_st, tri, perm = (cst[:, 128 * i:128 * (i + 1)] for i in range(1, 6))
    invf, iota = cst[:, 768:769], cst[:, 776:808]
    masks = mem["masks"]
    vec = mem["vec"]
    small = mem["small"]
    R = mem["R"]

    xin = R("xin", [128, 2, 1024], F32, 0)
    vraw = R("vraw", [128, 2, 128], F32, 16 * KB)
    t_x = P.dma(xin[:, :, :], I["x"][0].rearrange("(t p) d -> p t d", p=128), "x")
    t_id = P.dma(cst[:, :], I["c_mat"], "ident", eng="act")

    vecs = [("conv_w", I["conv_w"].rearrange("o k (t p) -> (o k t) p", p=128), 96),
            ("conv_b", I["conv_b"].rearrange("o (t p) -> (o t) p", p=128), 24),
            ("norm_mix", I["norm_mix"].rearrange("o (t p) -> (o t) p", p=128), 8),
            ("ssd_norm", I["ssd_norm"].rearrange("o (t p) -> (o t) p", p=128), 16),
            ("q_a_norm", I["q_a_norm"].rearrange("o (t p) -> (o t) p", p=128), 3),
            ("kv_a_norm", I["kv_a_norm"].rearrange("o (t p) -> (o t) p", p=128), 2),
            ("norm_xattn", I["norm_xattn"].rearrange("o (t p) -> (o t) p", p=128), 8),
            ("norm_mem", I["norm_mem"].rearrange("o (t p) -> (o t) p", p=128), 8),
            ("norm_moe", I["norm_moe"].rearrange("o (t p) -> (o t) p", p=128), 8),
            ("norm_final", I["norm_final"].rearrange("(t p) -> t p", p=128), 8)]
    vecs += [(n, I[n].rearrange("o (t p) -> (o t) p", p=128), k) for n, k in (
        ("attn_pre_norm_2", 8), ("hg_out_norm_2", 4), ("sb_out_norm_2", 4), ("attn_post_norm_2", 8),
        ("ffn_pre_norm_2", 8), ("ffn_post_norm_2", 8), ("hg_lower_gamma_2", 8))]
    col, at = {}, 0
    for name, view, n in vecs:
        assert at // 128 == (at + n - 1) // 128
        t_v = P.dma(vraw[at % 128:at % 128 + n, at // 128, :], view, "vecs", eng="act" if len(col) % 2 else "sp")
        col[name] = vec[:, at:at + n]
        at += n
    nvec = at
    if seq is not None:
        W.preload()
    dtb, alog = small[:, 0:1], small[:, 1:2]
    dsk = small[:, 8:24]
    for c in range(4):
        P.dma(small[32 * c:32 * c + 32, 0:1], I["dt_bias"].rearrange("o h -> h o"), "const")
        P.dma(small[32 * c:32 * c + 32, 1:2], I["a_log"].rearrange("o h -> h o"), "const")
    d32 = small[:, 32:64]
    P.dma(d32, I["d_skip"].broadcast_to([128, 32]), "const")
    brt = mem["brt"]
    P.dma(brt[:, 0:4], I["b_router_group"].broadcast_to([128, 4]), "const")
    P.dma(brt[:, 4:36], I["b_router_expert"].broadcast_to([128, 32]), "const")
    posi = mem["posi"]
    P.dma(posi[:, :], I["positions"].broadcast_to([128, 256]), "const")
    mraw = R("mraw", [128, 896], F32, 24 * KB)
    P.dma(mraw[:, :], I["c_masks"], "const")
    t_c = [t_id, ("dma", "const", "all")]
    t_ones = P.put("pool", lambda e: e.memset(ones[:, :], 1.0), None)
    epsc = small[:, 2:3]
    t_eps = P.put("pool", lambda e: e.memset(epsc, EPS), None)
    P.put("pool", lambda e: e.tensor_copy(masks[:, :], mraw[:, :]), [t_c])

    def split(h, l, src, after):
        t = P.act(h, src, ACT.Copy, after=after)
        return P.tt(l, src, h.bitcast(F32), ALU.subtract, after=[t] + flat(after))

    busy = [None]

    def norm_steps(res, src, nt, D, gain, dst, after, ng=1):
        n, half = ng * nt, nt // 2 if nt % 4 == 0 else 0
        t = P.act(T8[:, 0:n, :], src[:, 0:n, :], ACT.Square, after=[after, busy[0]])
        for k in range(n):
            t_hg = P.act(T8b[:, k, :], src[:, k, :], ACT.Copy, after=[t_vec], scale=gain[:, k:k + 1])
        v = T8[:, 0:n, :].rearrange("p (g k) n -> p g k n", g=ng)
        if half:
            t = P.tt(v[:, :, 0:half, :], v[:, :, 0:half, :], v[:, :, half:nt, :], ALU.add, after=[t])
        yield
        b, ps, tf = B.get()
        m = half or nt
        for k in range(m):
            tm = P.mm(ps[:, 0:256 * ng], ones[:, :], v[:, :, k, :], k == 0, k == m - 1, after=[t, tf, t_ones])
        r = mem["rs"][:, 0:256 * ng]
        t = P.act(r, ps[:, 0:256 * ng], ACT.Ln, after=[tm, t_eps, busy[0]], scale=1.0 / D, bias=epsc)
        B.free(b, t)
        t = P.act(r, r, ACT.Exp, scale=-0.5)
        yield
        cuts = list(range(0, n, nt)) if ng > 1 else [0, n // 2] if n % 4 == 0 else [0]
        for k0, k1 in zip(cuts, cuts[1:] + [n]):
            g = k0 // nt
            t2 = P.tt(dst[:, k0:k1, :], T8b[:, k0:k1, :], r[:, 256 * g:256 * g + 256].unsqueeze(1).broadcast_to([128, k1 - k0, 256]),
                      ALU.mult, after=[t, t_hg])
            res.append((k0, k1, t2))
        busy[0] = t2

    def norm(*args):
        res = []
        finish(norm_steps(res, *args))
        return res

    class Ready(list):
        pass

    def norm_split_steps(ready, src, nt, D, gain, h, l, after, ng=1):
        res = []
        yield from norm_steps(res, src, nt, D, gain, T8b, after, ng)
        for k0, k1, t in res:
            busy[0] = split(h[:, k0:k1, :], l[:, k0:k1, :], T8b[:, k0:k1, :], [t])
            ready += [busy[0]] * (k1 - k0)

    def norm_split(*args):
        ready = Ready()
        finish(norm_split_steps(ready, *args))
        return ready

    def triple(ps, h, l, xh, xl, kt, first, last, after, k0=0, loose=False, hl=None):
        tiles = next((x for x in after if isinstance(x, Ready) and len(x) == kt), None)
        after = [x for x in after if x is not tiles]
        for k in range(kt):
            st, sp = first and k == 0, last and k == kt - 1
            t = tiles[k] if tiles else None
            P.mm(ps, h(k), xh(k), st, False, after=[after, t], loose=loose)
            P.mm(ps, h(k), xl(k), False, False, loose=loose)
            t = P.mm(ps, l(k), xh(k), False, sp, loose=loose)
        return t

    side = []

    def advance():
        if side:
            try:
                next(side[0])
            except StopIteration:
                side.pop(0)

    def finish(gen=None):
        if gen is not None:
            for _ in gen:
                pass
        while gen is None and side:
            advance()

    def linear(w, c0, ncol, xh, xl, kt, ready, evac, k_cols=256):
        for c in range(c0, c0 + ncol, k_cols):
            h, l, tw, i = W.next([(0, kt, k_cols, kp(w, kt)[:, :, c:c + k_cols])])
            b, ps, tf = B.get()
            nt = k_cols // 128
            for j in range(nt):
                t = triple(ps[:, 256 * j:256 * j + 256], lambda k: h[:, k, 128 * j:128 * j + 128],
                           lambda k: l[:, k, 128 * j:128 * j + 128], lambda k: xh[:, k, :], lambda k: xl[:, k, :],
                           kt, True, True, [tw, tf, ready])
            W.free(i, t)
            B.free(b, evac((c - c0) // 128, nt, ps[:, 0:256 * nt].rearrange("p (t n) -> p t n", t=nt), t))
            advance()

    def linear_tok(w, c0, ncol, xh, xl, kt, ready, evac):
        for c in range(c0, c0 + ncol, 256):
            h, l, tw, i = W.next([(0, kt, 256, kp(w, kt)[:, :, c:c + 256])])
            b, ps, tf = B.get()
            for j in range(2):
                t = triple(ps[:, 256 * j:256 * j + 256], lambda k: xh[:, k, 128 * j:128 * j + 128],
                           lambda k: xl[:, k, 128 * j:128 * j + 128], lambda k: h[:, k, :], lambda k: l[:, k, :],
                           kt, True, True, [tw, tf, ready])
            W.free(i, t)
            B.free(b, evac(c - c0, ps[:, :].rearrange("p (t n) -> p t n", t=2), t))
            advance()

    def transposes(dst, srcs, after):
        toks = []
        for g in range(0, len(srcs), 4):
            b, ps, tf = B.get()
            n = min(4, len(srcs) - g)
            for j in range(n):
                t = P.tr(ps[:, 128 * j:128 * j + 128], srcs[g + j], ident, after=[after, tf, t_id])
            t = P.copy(dst(g, n), ps[:, 0:128 * n].rearrange("p (a n) -> p a n", a=n), after=[t])
            B.free(b, t)
            toks.append(t)
        return toks[-1]

    for d0 in range(0, 8, 2):
        b, ps, tf = B.get()
        for j in range(4):
            t = P.tr(ps[:, 128 * j:128 * j + 128], xin[:, j % 2, (d0 + j // 2) * 128:(d0 + j // 2 + 1) * 128],
                     ident, after=[t_x, t_id, tf])
        t = P.copy(H[:, d0:d0 + 2, :], ps[:, :].rearrange("p (a n) -> p a n", a=2), after=[t])
        B.free(b, t)
    t_h = t
    b, ps, tf = B.get()
    t_v = [t_id, ("dma", "vecs", "all")]
    t = P.tr(ps[:, 0:128], vraw[:, 0, :], ident, after=[t_v])
    t = P.tr(ps[0:128, 128:128 + nvec - 128], vraw[0:nvec - 128, 1, :], ident[0:nvec - 128, 0:nvec - 128])
    t_vec = P.copy(vec[:, 0:nvec], ps[:, 0:nvec], after=[t])
    B.free(b, t_vec)
    t_u = Ready()
    steps = norm_split_steps(t_u, H, 8, 1024, col["norm_mix"], XUh[:, :, :], XUl[:, :, :], [t_h])
    next(steps)
    if seq is not None:
        W.ahead()
    finish(steps)
    tap("u", T8b[:, :, :], t_u)

    w_in = I["w_in"][0]
    xh, xl = XUh, XUl
    dtT, acT = R("dtT", [128, 256], F32, 20 * KB), R("acT", [128, 256], F32, 21 * KB)
    dtk = R("dtk", [128, 2, 2, 32], F32, 22 * KB)
    qa, ckv, kpe = R("qa", [128, 3, 256], F32, 10 * KB), R("ckv", [128, 2, 256], F32, 13 * KB), R("kpe", [128, 256], F32, 15 * KB)
    P.barrier()
    rep4 = [(lambda x: x[:, 0:1024].rearrange("p (k c d) -> p k c d", k=8, c=4),
             lambda x: x[:, 0:256].rearrange("p (k d) -> p k d", k=8).unsqueeze(2).broadcast_to([128, 8, 4, 32]))]
    h, l, tw, i = W.next([(0, 8, 32, kp(w_in, 8)[:, :, 5120:5152])], rep4, 1024)
    b, ps, tf = B.get()

    t = triple(ps[:, 0:256], lambda k: h[:, k, :], lambda k: l[:, k, :],
               lambda k: xh[:, k, :], lambda k: xl[:, k, :], 8, True, True, [tw, tf, t_u])
    W.free(i, t)
    s1, s2, s3 = T8[:, 4, :], T8[:, 5, :], T8[:, 6, :]
    t = P.ts(s1, ps[:, 0:256], dtb, None, ALU.add, after=[t, t_c])
    B.free(b, t)
    t = P.act(s2, s1, ACT.Abs, after=[t])
    t = P.act(s2, s2, ACT.Exp, after=[t], scale=-1.0)
    t = P.act(s3, s2, ACT.Ln, scale=1.0, bias=1.0)
    t_dt = P.stt(dtT[:, :], s1, 0.0, s3, ALU.max, ALU.add, after=[t])
    t = P.act(small[:, 3:4], alog, ACT.Exp, after=[t_c])
    t = P.ts(s1, dtT[:, :], small[:, 3:4], -1.0, ALU.mult, ALU.mult, after=[t])
    for c in range(2):
        t_ac = P.put("dve", lambda e, c=c: e.tensor_tensor_scan(
            acT[:, 128 * c:128 * c + 128], ones[:, 0:128], s1[:, 128 * c:128 * c + 128], 0.0, ALU.mult, ALU.add), [t_ones])
    dest = [(qa, 0), (qa, 1), (qa, 2), (ckv, 0), (ckv, 1)]

    def ev_lora(f, n, ps, t, base):
        for j in range(n):
            d, k = dest[base + j]
            t = P.copy(d[:, k, :], ps[:, j, :], after=[t])
        return t

    linear(w_in, 5152, 512, xh, xl, 8, t_u, lambda f, n, ps, t: ev_lora(f, n, ps, t, f))
    b, ps, tf = B.get()
    for j, (c, n, m) in enumerate(((5664, 128, None), (5792, 32, rep4))):
        h, l, tw, i = W.next([(0, 8, n, kp(w_in, 8)[:, :, c:c + n])], m, 1024)
        t = triple(ps[:, 256 * j:256 * j + 256], lambda k: h[:, k, :], lambda k: l[:, k, :],
                   lambda k: xh[:, k, :], lambda k: xl[:, k, :], 8, True, True, [tw, tf])
        W.free(i, t)
    t = P.copy(ckv[:, 1, :], ps[:, 0:256], after=[t])
    t_lora = P.copy(kpe[:, :], ps[:, 256:512], after=[t])
    B.free(b, t_lora)
    tap("qa", qa[:, :, :], t_lora)
    tap("kpe", kpe[:, :], t_lora)

    b, ps, tf = B.get()
    for j, src in enumerate((dtT, acT)):
        for c in range(2):
            n = 2 * j + c
            t = P.tr(ps[:, 128 * n:128 * n + 128], src[:, 128 * c:128 * c + 128], ident, after=[tf, t_dt, t_ac])
    t_dtk = P.copy(dtk[:, :, :, :], ps[:, :].rearrange("p (a c n) -> p a c n", a=2, c=2)[:, :, :, 0:32], after=[t])
    B.free(b, t_dtk)
    tap("dtT", dtT[:, :], t_dtk)
    tap("acT", acT[:, :], t_dtk)

    for j in range(2):
        t_dsk = P.copy(dsk[64 * j:64 * j + 64, :],
                       d32[64 * j:64 * j + 64, :].rearrange("p (i two) -> p two i", two=2)[:, j, :], after=[t_c])

    cs = mem["cs"]
    ang, nn, tmp = T8[:, 0, :], T8[:, 1, :], T8[:, 2, :]
    t = P.copy(tmp, posi[:, :], after=[t_c, t_u])
    t = P.ts(ang, tmp, invf, None, ALU.mult)
    TWO = 2.0 * np.pi
    C1 = 6.28125
    C2 = float(np.float32(TWO - C1))
    C2 = float(np.float32(np.round((TWO - C1) * 2 ** 20) / 2 ** 20))
    C3 = float(np.float32(TWO - C1 - C2))
    MAGIC = 12582912.0
    for i, shift in ((0, np.pi / 2), (1, 0.0)):
        P.ts(nn, ang, 1.0 / TWO, shift / TWO, ALU.mult, ALU.add)
        P.ts(nn, nn, MAGIC, MAGIC, ALU.add, ALU.subtract)
        P.stt(tmp, nn, -C1, ang, ALU.mult, ALU.add)
        P.stt(tmp, nn, -C2, tmp, ALU.mult, ALU.add)
        P.stt(tmp, nn, -C3, tmp, ALU.mult, ALU.add)
        P.ts(tmp, tmp, float(np.float32(shift)), None, ALU.add)
        P.ts(tmp, tmp, float(np.float32(3.1415925)), float(np.float32(-3.1415925)), ALU.min, ALU.max)
        t = P.copy(cs[:, i, :], tmp)
    t_cs = P.act(cs[:, :, :], cs[:, :, :], ACT.Sin, after=[t])
    tap("cs", cs[:, :, :], t_cs)

    BT, CT = R("BT", [128, 4, 256], F32, 0), R("CT", [128, 4, 256], F32, 4 * KB)
    xs = R("xs", [128, 16, 256], F32, 24 * KB)
    xdt = R("xdt", [128, 2, 2048], F32, 40 * KB)
    Btok = R("Btok", [128, 4, 128], F32, 8 * KB)
    cw, cb = col["conv_w"], col["conv_b"]
    acc = T8b

    slot = [0]
    acc_tok = [None] * 4

    def ev_conv(ch, n, ps, t, put):
        toks = []
        for j in range(n):
            c = ch + j
            s = slot[0] % 4
            slot[0] += 1
            a = acc[:, s, :]
            t1 = P.act(a, ps[:, j, :], ACT.Identity, after=[t, t_vec, acc_tok[s]],
                       scale=cw[:, 72 + c:73 + c], bias=cb[:, c:c + 1])
            for k in range(3):
                sh = 3 - k
                t1 = P.stt(a[:, sh:256], ps[:, j, 0:256 - sh], cw[:, 24 * k + c:24 * k + c + 1], a[:, sh:256],
                           ALU.mult, ALU.add, after=[t1])
            t2 = P.act(put(c), a, ACT.Silu, after=[t1])
            acc_tok[s] = t2
            toks.append(t1)
        last_silu[0] = t2
        return toks

    last_silu = [None]
    linear(w_in, 4096, 1024, xh, xl, 8, t_u,
           lambda f, n, ps, t: ev_conv(16 + f, n, ps, t, lambda c: BT[:, c - 16, :] if c < 20 else CT[:, c - 20, :]))
    t_bc = last_silu[0]
    linear(w_in, 2048, 2048, xh, xl, 8, t_u, lambda f, n, ps, t: ev_conv(f, n, ps, t, lambda c: xs[:, c, :]))
    t_xs = last_silu[0]
    tap("BT", BT[:, :, :], t_bc)
    tap("xs", xs[:, :, :], t_xs)
    acb = R("acb", [128, 8, 256], F32, 56 * KB)
    M = R("M", [128, 2, 8, 128], F32, 64 * KB)
    CE = R("CE", [128, 8, 128], F32, 72 * KB)
    xw = R("xw", [128, 512], F32, 16 * KB)
    S0 = R("S0", [128, 512], F32, 18 * KB)
    dte = R("dte", [128, 8], F32, 23 * KB)
    CB = R("CB", [128, 2, 128], F32, 20 * KB)
    below = R("below", [128, 128], F32, 23 * KB + 512)
    nac = R("nac", [128, 2, 32], F32, 23 * KB + 64)
    P.ts(nac[:, :, :], dtk[:, 1, :, :], -1.0, None, ALU.mult, after=[t_dtk])
    P.ts(below[:, :], n_sl, 0.0, None, ALU.is_equal, after=[t_c])
    def ssd_steps():
        t_y = t_pe = None
        b, ps, tf = B.get()
        for g in range(4):
            t = P.tr(ps[:, 128 * g:128 * g + 128], BT[:, g, 0:128], ident, after=[t_bc, tf])
        t_btok = P.copy(Btok[:, :, :], ps[:, :].rearrange("p (a n) -> p a n", a=4), after=[t])
        B.free(b, t_btok)
        for c in range(2):
            for g in range(4):
                b, ps, tf = B.get()
                for j in range(4):
                    t = P.tr(ps[:, 128 * j:128 * j + 128], xs[:, 4 * g + j, 128 * c:128 * c + 128], ident, after=[t_xs, tf])
                t_xdt = P.tt(xdt[:, c, 512 * g:512 * g + 512].rearrange("p (h d) -> p h d", d=64),
                             ps[:, :].rearrange("p (h d) -> p h d", d=64),
                             dtk[:, 0, c, 8 * g:8 * g + 8].unsqueeze(2).broadcast_to([128, 8, 64]), ALU.mult, after=[t, t_dtk])
                B.free(b, t_xdt)
        yield
        for g in range(4):
            for q in range(4):
                b, ps, tf = B.get()
                for j in range(2):
                    hd = 8 * g + 2 * q + j
                    t = P.mm(ps[:, 256 * j:256 * j + 256], ident[0:32, hd:hd + 1].broadcast_to([32, 128]), acT[0:32, :],
                             after=[t_ac, tf])
                t_acb = P.act(acb[:, 2 * q:2 * q + 2, :], ps[:, :].rearrange("p (a n) -> p a n", a=2), ACT.Copy,
                              after=[t, t_y])
                B.free(b, t_acb)
            b, ps, tf = B.get()
            for c in range(2):
                t = P.mm(ps[:, 128 * c:128 * c + 128], BT[:, g, 128 * c:128 * c + 128], CT[:, g, 128 * c:128 * c + 128],
                         after=[t_bc, tf])
            t_cb = P.tt(CB[:, :, :], ps[:, 0:256].rearrange("p (c n) -> p c n", c=2),
                        below[:, :].unsqueeze(1).broadcast_to([128, 2, 128]), ALU.mult, after=[t])
            B.free(b, t_cb)
            t = P.tt(dte[:, :], acb[:, :, 127], dtk[:, 1, 0, 8 * g:8 * g + 8], ALU.subtract, after=[t_acb, t_dtk])
            t_dte = P.act(dte[:, :], dte[:, :], ACT.Exp, after=[t])
            t_ce = P.act(CE[:, :, :], acb[:, :, 128:256], ACT.Exp, after=[t_pe])
            t_xw = P.tt(xw[:, :].rearrange("p (h d) -> p h d", d=64),
                        xdt[:, 0, 512 * g:512 * g + 512].rearrange("p (h d) -> p h d", d=64),
                        dte[:, :].unsqueeze(2).broadcast_to([128, 8, 64]), ALU.mult, after=[t_dte, t_pe])
            t_e = [None, None]
            for hl in range(8):
                t_e[0] = P.ts(M[:, 0, hl, :], acb[:, hl, 0:128], dtk[:, 1, 0, 8 * g + hl:8 * g + hl + 1], 0.0,
                              ALU.subtract, ALU.min, after=[t_acb, t_pe])
                t_e[1] = P.act(M[:, 1, hl, :], acb[:, hl, 128:256], ACT.Abs, after=[t_pe],
                               bias=nac[:, 1, 8 * g + hl:8 * g + hl + 1])
            for c in range(2):
                t_e[c] = P.act(M[:, c, :, :], M[:, c, :, :], ACT.Exp, after=[t_e[c]], scale=1.0 - 2.0 * c)
            for c in range(2):
                t_m = P.tt(M[:, c, :, :], M[:, c, :, :], CB[:, c, :].unsqueeze(1).broadcast_to([128, 8, 128]),
                           ALU.mult, after=[t_e[c]])
            t_ce = P.tt(CE[:, :, :], CE[:, :, :], CT[:, g, 128:256].unsqueeze(1).broadcast_to([128, 8, 128]), ALU.mult,
                        after=[t_ce, t_bc])
            yield
            yield
            b, ps, tf = B.get()
            t = P.mm(ps[:, :], Btok[:, g, :], xw[:, :], after=[t_xw, t_btok, tf])
            t_s0 = P.copy(S0[:, :], ps[:, :], after=[t, t_pe])
            B.free(b, t_s0)
            for q in range(4):
                b, ps, tf = B.get()
                for j in range(2):
                    hl = 2 * q + j
                    hd = 8 * g + hl
                    o = 64 * j
                    P.mm(ps[o:o + 64, 0:128], xdt[:, 0, 64 * hd:64 * hd + 64], M[:, 0, hl, :], after=[t_m, t_xdt, tf])
                    P.mm(ps[o:o + 64, 128:256], xdt[:, 1, 64 * hd:64 * hd + 64], M[:, 1, hl, :], True, False)
                    t_pe = P.mm(ps[o:o + 64, 128:256], S0[:, 64 * hl:64 * hl + 64], CE[:, hl, :], False, True,
                                after=[t_s0, t_ce])
                i = 4 * g + q
                t_y = P.stt(xs[:, i, :], xs[:, i, :], dsk[:, i:i + 1], ps[:, 0:256], ALU.mult, ALU.add, after=[t_pe, t_dsk])
                B.free(b, t_y)
        t_ys[0] = t_y

    t_sz = [None]

    def ev_z(f, n, ps, t):
        t_sz[0] = P.act((T8, T8b)[f // 8][:, f % 8:f % 8 + n, :], ps, ACT.Copy, after=[t, last_acc])
        return t_sz[0]

    t_ys = [None]
    last_acc = P.last()
    side.append(ssd_steps())
    linear(w_in, 0, 2048, xh, xl, 8, t_u, ev_z)
    finish()
    YAh, YAl = R("YAh", [128, 16, 256], F32R, 40 * KB), R("YAl", [128, 16, 256], F32R, 56 * KB)
    t_ya = Ready()

    def ya_steps():
        t_z = []
        for g in range(2):
            sz = (T8, T8b)[g]
            t_z.append(P.act(sz[:, :, :], sz[:, :, :], ACT.Silu, after=[t_sz[0]]))
        for g in range(2):
            t = P.tt(xs[:, 8 * g:8 * g + 8, :], xs[:, 8 * g:8 * g + 8, :], (T8, T8b)[g][:, :, :], ALU.mult, after=[t_z[g], t_ys[0]])
        for g in range(0, 16, 8):
            yield from norm_split_steps(t_ya, xs[:, g:g + 8, :], 4, 512, col["ssd_norm"][:, g:g + 8],
                                        YAh[:, g:g + 8, :], YAl[:, g:g + 8, :], [t], 2)

    side.append(ya_steps())
    advance()
    G = R("G", [128, 8, 256], F32, 0)
    t_g = [None]

    def ev_gate(f, n, ps, t):
        t_g[0] = P.act(G[:, f:f + n, :], ps, ACT.Copy, after=[t, t_ys[0]])
        return t_g[0]

    linear(w_in, 5824, 1024, xh, xl, 8, t_u, ev_gate)

    def ev_ssd(f, n, ps, t):
        t_g[0] = P.tt(G[:, f:f + n, :], G[:, f:f + n, :], ps, ALU.mult, after=[t, t_g0])
        return t_g[0]

    finish()
    t_g0 = P.act(G[:, :, :], G[:, :, :], ACT.Sigmoid)
    XCh, XCl = R("XCh", [128, 5, 256], F32R, 16 * KB), R("XCl", [128, 5, 256], F32R, 21 * KB)
    t1, t_xc = Ready(), Ready()
    side.append(norm_split_steps(t1, qa, 3, 384, col["q_a_norm"], XCh[:, 0:3, :], XCl[:, 0:3, :], [t_lora, P.last()]))
    side.append(norm_split_steps(t_xc, ckv, 2, 256, col["kv_a_norm"], XCh[:, 3:5, :], XCl[:, 3:5, :], [t_lora]))
    linear(I["w_ssd_out"][0], 0, 1024, YAh, YAl, 16, t_ya, ev_ssd, k_cols=128)
    tap("G", G[:, :, :], t_g[0])
    finish()
    t_gs = t_g[0]

    qn, qp = R("qn", [128, 8, 256], F32, 26 * KB), R("qp", [128, 4, 256], F32, 34 * KB)
    kn, V = (R("kn", [128, 8, 256], F32, 38 * KB), T8b), R("V", [128, 2, 1024], F32, 46 * KB)
    kpm = R("kpm", [128, 4, 256], F32, 10 * KB)
    P.put("pool", lambda e: e.memset(kn[0][64:128, :, :], 0.0), [t_xc, P.last()])
    P.put("pool", lambda e: e.memset(kn[1][0:64, :, :], 0.0), [t_xc])
    t_zero = P.put("pool", lambda e: e.memset(kpm[:, :, :], 0.0), [t_xc])
    wq, wkv = I["w_q_b"][0], I["w_kv_b"][0]
    qmap = [(lambda x: x[:, 0:768].rearrange("p (k h d) -> p k h d", k=3, h=4),
             lambda x: x[:, 0:1152].rearrange("p (k h d) -> p k h d", k=3, h=4)[:, :, :, 0:64]),
            (lambda x: x[:, 768:1152].rearrange("p (k h d) -> p k h d", k=3, h=4),
             lambda x: x[:, 0:1152].rearrange("p (k h d) -> p k h d", k=3, h=4)[:, :, :, 64:96])]
    for q in range(4):
        h, l, tw, i = W.next([(0, 3, 384, kp(wq, 3)[:, :, 384 * q:384 * q + 384])], qmap)
        h, l = (x.rearrange("p a b -> p (a b)") for x in (h, l))

        b, ps, tf = B.get()
        for j in range(2):
            t = triple(ps[:, 256 * j:256 * j + 256], lambda k: h[:, 256 * k + 128 * j:256 * k + 128 * j + 128], lambda k: l[:, 256 * k + 128 * j:256 * k + 128 * j + 128],
                       lambda k: XCh[:, k, :], lambda k: XCl[:, k, :], 3, True, True, [tw, tf, t1])
        t2 = P.act(qn[:, 2 * q:2 * q + 2, :], ps[:, :].rearrange("p (a n) -> p a n", a=2), ACT.Copy, after=[t])
        B.free(b, t2)
        b, ps, tf = B.get()
        t = triple(ps[:, 0:256], lambda k: h[:, 768 + 128 * k:896 + 128 * k], lambda k: l[:, 768 + 128 * k:896 + 128 * k],
                   lambda k: XCh[:, k, :], lambda k: XCl[:, k, :], 3, True, True, [tf])
        W.free(i, t)
        t_q = P.act(qp[:, q, :], ps[:, 0:256], ACT.Copy, after=[t])
        B.free(b, t_q)
    kvmap = [(lambda x, k=k: x[:, 1024 * k:1024 * k + 1024].rearrange("p (t h d) -> p t h d", t=2, h=8),
              lambda x, k=k: x[:, 1024 * k:1024 * k + 1024].rearrange("p (h t d) -> p t h d", t=2, h=8)) for k in range(2)]
    for q in range(2):
        h, l, tw, i = W.next([(0, 2, 1024, kp(wkv, 2)[:, :, 1024 * q:1024 * q + 1024])], kvmap)

        for r in range(2):
            b, ps, tf = B.get()
            for j in range(2):
                a = 4 * r + 2 * j
                t = triple(ps[:, 256 * j:256 * j + 256], lambda k: h[:, k, 64 * a:64 * a + 128], lambda k: l[:, k, 64 * a:64 * a + 128],
                           lambda k: XCh[:, 3 + k, :], lambda k: XCl[:, 3 + k, :], 2, True, True, [tw, tf, t_xc])
            for o in range(2):
                p = slice(64 * o, 64 * o + 64)
                t_kn = P.act(kn[o][p, 4 * q + 2 * r:4 * q + 2 * r + 2, :], ps[p, :].rearrange("p (a n) -> p a n", a=2),
                             ACT.Copy, after=[t])
            B.free(b, t_kn)
        for j in range(2):
            b, ps, tf = B.get()
            t = triple(ps[:, :], lambda k: XCh[:, 3 + k, 128 * j:128 * j + 128], lambda k: XCl[:, 3 + k, 128 * j:128 * j + 128],
                       lambda k: h[:, k, 512:1024], lambda k: l[:, k, 512:1024], 2, True, True, [tf])
            t_v = P.act(V[:, j, 512 * q:512 * q + 512], ps[:, :], ACT.Copy, after=[t])
            B.free(b, t_v)
        W.free(i, t)
    t_r = []
    for q in range(5):
        src = qp[:, q, :] if q < 4 else kpe[:, :]
        b, ps, tf = B.get()
        t = P.mm(ps[:, 0:256], perm, src, after=[t_q, t_lora, tf, t_c])
        t = P.tt(T8[:, q, :], ps[:, 0:256], cs[:, 1, :], ALU.mult, after=[t, t_cs])
        B.free(b, t)
        P.tt(src, src, cs[:, 0, :], ALU.mult, after=[t])
        t_r = P.tt(src, src, T8[:, q, :], ALU.add)
    for hl in range(4):
        p = slice(32 * hl, 32 * hl + 32)
        t_r = P.copy(kpm[p, hl, :], kpe[p, :], after=[t_zero])
    tap("qn", qn[:, :, :], t_r)
    tap("qp", qp[:, :, :], t_r)
    tap("kpr", kpe[:, :], t_r)
    tap("V", V[:, :, :], [t_r, t_v])
    Pm0, Pm1 = R("Pm0", [128, 4, 128], F32, 54 * KB), R("Pm1", [128, 4, 256], F32, 56 * KB)
    PT0, PT1 = R("PT0", [128, 4, 256], F32, 60 * KB), R("PT1", [128, 4, 128], F32, 64 * KB)
    OAh, OAl = R("OAh", [128, 8, 256], F32R, 66 * KB), R("OAl", [128, 8, 256], F32R, 16 * KB)
    sm = mem["sm"]
    SC = 96.0 ** -0.5
    t_oa = [None]
    nqk4 = n_qk.unsqueeze(1).broadcast_to([128, 4, 128])

    def mla_steps():
        t_pv = t_ptr = None
        for g in range(4):
            b0, p0, f0 = B.get()
            bs = [B.get() for _ in range(2)]
            for hl in range(4):
                hd = 4 * g + hl
                qN, kN = qn[:, hd // 2, :], kn[hd % 2][:, hd // 2, :]
                qP, kP = qp[:, g, :], kpm[:, hl, :]
                d0 = p0[:, 128 * hl:128 * hl + 128]
                P.mm(d0, qN[:, 0:128], kN[:, 0:128], True, False, after=[t_r, t_kn, t_zero, f0])
                t0 = P.mm(d0, qP[:, 0:128], kP[:, 0:128], False, True)
                d1 = bs[hl // 2][1][:, 256 * (hl % 2):256 * (hl % 2) + 256]
                P.mm(d1, qN[:, 128:256], kN[:, :], True, False, after=[bs[hl // 2][2]])
                t1 = P.mm(d1, qP[:, 128:256], kP[:, :], False, True)
            ta = P.stt(Pm0[:, :, :], p0[:, :].rearrange("p (a n) -> p a n", a=4), SC, nqk4, ALU.mult, ALU.add, after=[t0, t_ptr])
            B.free(b0, ta)
            for j in range(2):
                bb, pp, _ = bs[j]
                v = pp[:, :].rearrange("p (a n) -> p a n", a=2)
                P.ts(Pm1[:, 2 * j:2 * j + 2, 0:128], v[:, :, 0:128], SC, None, ALU.mult, after=[t1, t_ptr])
                ta = P.stt(Pm1[:, 2 * j:2 * j + 2, 128:256], v[:, :, 128:256], SC,
                           n_qk.unsqueeze(1).broadcast_to([128, 2, 128]), ALU.mult, ALU.add)
                B.free(bb, ta)
            P.red(sm[:, 0:4], Pm0[:, :, :], ALU.max)
            P.red(sm[:, 4:8], Pm1[:, :, :], ALU.max)
            t = P.ts(sm[:, 8:16], sm[:, 0:8], -1.0, None, ALU.mult)
            for hl in range(4):
                P.act(Pm0[:, hl, :], Pm0[:, hl, :], ACT.Exp, after=[t], bias=sm[:, 8 + hl:9 + hl], accum_out=sm[:, 16 + hl:17 + hl])
                t2 = P.act(Pm1[:, hl, :], Pm1[:, hl, :], ACT.Exp, bias=sm[:, 12 + hl:13 + hl], accum_out=sm[:, 20 + hl:21 + hl])
            P.put("dve", lambda e: e.reciprocal(sm[:, 24:32], sm[:, 16:24]), [t2])
            P.tt(Pm0[:, :, :], Pm0[:, :, :], sm[:, 24:28].unsqueeze(2).broadcast_to([128, 4, 128]), ALU.mult)
            t = P.tt(Pm1[:, :, :], Pm1[:, :, :], sm[:, 28:32].unsqueeze(2).broadcast_to([128, 4, 256]), ALU.mult)
            yield
            bt = [B.get() for _ in range(3)]
            for hl in range(4):
                d = bt[hl // 2][1][:, 256 * (hl % 2):256 * (hl % 2) + 256]
                P.tr(d[:, 0:128], Pm0[:, hl, :], ident, after=[t, bt[hl // 2][2]])
                P.tr(d[:, 128:256], Pm1[:, hl, 0:128], ident)
                t_ptr = P.tr(bt[2][1][:, 128 * hl:128 * hl + 128], Pm1[:, hl, 128:256], ident, after=[bt[2][2]])
            for j in range(2):
                t = P.act(PT0[:, 2 * j:2 * j + 2, :], bt[j][1][:, :].rearrange("p (a n) -> p a n", a=2), ACT.Copy, after=[t_ptr, t_pv])
                B.free(bt[j][0], t)
            t = P.act(PT1[:, :, :], bt[2][1][:, :].rearrange("p (a n) -> p a n", a=4), ACT.Copy)
            B.free(bt[2][0], t)
            b, ps, tf = B.get()
            for j in range(2):
                for r in range(2):
                    hl = 2 * j + r
                    hd = 4 * g + hl
                    o = 64 * r
                    P.mm(ps[o:o + 64, 256 * j:256 * j + 256], V[:, 0, 64 * hd:64 * hd + 64], PT0[:, hl, :], True, False, after=[t, t_v, tf])
                    t_pv = P.mm(ps[o:o + 64, 256 * j + 128:256 * j + 256], V[:, 1, 64 * hd:64 * hd + 64], PT1[:, hl, :], False, True)
            t_oa[0] = split(OAh[:, 2 * g:2 * g + 2, :], OAl[:, 2 * g:2 * g + 2, :], ps[:, :].rearrange("p (a n) -> p a n", a=2), [t_pv])
            B.free(b, t_oa[0])

    G2 = T8
    t_rope = t_r

    def ev_gate2(f, n, ps, t):
        t_g[0] = P.act(G2[:, f:f + n, :], ps, ACT.Copy, after=[t, t_rope])
        return t_g[0]

    side.append(mla_steps())
    advance()
    linear(w_in, 6848, 1024, xh, xl, 8, t_u, ev_gate2)
    finish()
    t_g0 = P.act(G2[:, :, :], G2[:, :, :], ACT.Sigmoid)
    MXh, MXl = R("MXh", [128, 8, 256], F32R, 34 * KB), R("MXl", [128, 8, 256], F32R, 42 * KB)

    def ev_mla(f, n, ps, t):
        t = P.tt(G2[:, f:f + n, :], G2[:, f:f + n, :], ps, ALU.mult, after=[t, t_g0])
        P.tt(G[:, f:f + n, :], G[:, f:f + n, :], G2[:, f:f + n, :], ALU.add, after=[t_gs])
        t_g[0] = t_mx[0] = split(MXh[:, f:f + n, :], MXl[:, f:f + n, :], G[:, f:f + n, :], P.last())
        return t

    t_mx = [None]
    linear(I["w_mla_out"][0], 0, 1024, OAh, OAl, 8, t_oa[0], ev_mla)

    def ev_res(f, n, ps, t):
        t_g[0] = P.tt(H[:, f:f + n, :], H[:, f:f + n, :], ps, ALU.add, after=[t])
        return t_g[0]

    memin, memT = R("memin", [128, 2, 1024], F32, 0), R("memT", [128, 8, 256], F32, 8 * KB)
    MMh, MMl = R("MMh", [128, 8, 256], F32R, 16 * KB), R("MMl", [128, 8, 256], F32R, 24 * KB)
    t_mem = P.dma(memin[:, :, :], I["mem"][0].rearrange("(t p) d -> p t d", p=128), "mem", after=P.last())
    t_mm = Ready()

    def mem_steps():
        for d0 in range(0, 8, 2):
            b, ps, tf = B.get()
            for j in range(4):
                t = P.tr(ps[:, 128 * j:128 * j + 128], memin[:, j % 2, (d0 + j // 2) * 128:(d0 + j // 2 + 1) * 128],
                         ident, after=[t_mem, tf])
            t = P.act(memT[:, d0:d0 + 2, :], ps[:, :].rearrange("p (a n) -> p a n", a=2), ACT.Copy, after=[t])
            B.free(b, t)
        yield from norm_split_steps(t_mm, memT, 8, 1024, col["norm_mem"], MMh[:, :, :], MMl[:, :, :], [t])

    side.append(mem_steps())
    linear(I["w_o"][0], 0, 1024, MXh, MXl, 8, t_mx[0], ev_res)
    t_h = t_g[0]
    finish()
    tap("h1", H[:, :, :], t_h)

    XVh, XVl = R("XVh", [128, 8, 256], F32R, 32 * KB), R("XVl", [128, 8, 256], F32R, 40 * KB)
    t_xv = Ready()
    side.append(norm_split_steps(t_xv, H, 8, 1024, col["norm_xattn"], XVh[:, :, :], XVl[:, :, :], [t_h]))
    advance()
    q2, k2 = R("q2", [128, 8, 256], F32, 48 * KB), R("k2", [128, 8, 256], F32, 56 * KB)
    v2 = R("v2", [128, 2, 1024], F32, 64 * KB)

    def ev_to(dst):
        def ev(f, n, ps, t):
            t_g[0] = P.act(dst[:, f:f + n, :], ps, ACT.Copy, after=[t])
            return t_g[0]
        return ev

    def ev_tok(dst):
        def ev(c, ps, t):
            t_g[0] = P.act(dst[:, :, c:c + 256], ps, ACT.Copy, after=[t])
            return t_g[0]
        return ev

    linear(I["w_xkv"][0], 0, 1024, MMh, MMl, 8, t_mm, ev_to(k2))
    finish()
    linear(I["w_xq"][0], 0, 1024, XVh, XVl, 8, t_xv, ev_to(q2))
    t_qk = t_g[0]
    Px = [R(f"Px{j}", [128, 4, 256], F32, (32 + 4 * j) * KB) for j in range(2)]
    PXT = [R(f"PXT{j}", [128, 4, 256], F32, (40 + 4 * j) * KB) for j in range(2)]
    OXh, OXl = R("OXh", [128, 8, 256], F32R, 0), R("OXl", [128, 8, 256], F32R, 8 * KB)
    toks = []
    for j in range(2):
        bs = [B.get() for _ in range(2)]
        for hd in range(4):
            d = bs[hd // 2][1][:, 256 * (hd % 2):256 * (hd % 2) + 256]
            for e in range(2):
                t = P.mm(d, q2[:, 2 * hd + e, 128 * j:128 * j + 128], k2[:, 2 * hd + e, :], e == 0, e == 1, after=[t_qk, bs[hd // 2][2]])
        for r in range(2):
            t2 = P.ts(Px[j][:, 2 * r:2 * r + 2, :], bs[r][1][:, :].rearrange("p (a n) -> p a n", a=2), 1.0 / 16, None, ALU.mult, after=[t])
            B.free(bs[r][0], t2)
        sj = sm[:, 64 * j:64 * j + 64]
        P.red(sj[:, 0:4], Px[j][:, :, :], ALU.max)
        t = P.ts(sj[:, 8:12], sj[:, 0:4], -1.0, None, ALU.mult)
        for hd in range(4):
            t2 = P.act(Px[j][:, hd, :], Px[j][:, hd, :], ACT.Exp, after=[t], bias=sj[:, 8 + hd:9 + hd], accum_out=sj[:, 16 + hd:17 + hd])
        P.put("dve", lambda e, sj=sj: e.reciprocal(sj[:, 24:28], sj[:, 16:20]), [t2])
        toks.append(P.tt(Px[j][:, :, :], Px[j][:, :, :], sj[:, 24:28].unsqueeze(2).broadcast_to([128, 4, 256]), ALU.mult))
    linear_tok(I["w_xkv"][0], 1024, 1024, MMh, MMl, 8, t_mm, ev_tok(v2))
    t_v2 = t_g[0]
    for mj in range(2):
        for r in range(2):
            b, ps, tf = B.get()
            for a in range(2):
                for j in range(2):
                    t = P.tr(ps[:, 256 * a + 128 * j:256 * a + 128 * j + 128], Px[j][:, 2 * r + a, 128 * mj:128 * mj + 128], ident, after=[toks, tf])
            t_px = P.act(PXT[mj][:, 2 * r:2 * r + 2, :], ps[:, :].rearrange("p (a n) -> p a n", a=2), ACT.Copy, after=[t])
            B.free(b, t_px)
    for hd in range(4):
        b, ps, tf = B.get()
        for e in range(2):
            for mj in range(2):
                t = P.mm(ps[:, 256 * e:256 * e + 256], v2[:, mj, 256 * hd + 128 * e:256 * hd + 128 * e + 128],
                         PXT[mj][:, hd, :], mj == 0, mj == 1, after=[t_px, t_v2, tf])
        t_ox = split(OXh[:, 2 * hd:2 * hd + 2, :], OXl[:, 2 * hd:2 * hd + 2, :], ps[:, :].rearrange("p (a n) -> p a n", a=2), [t])
        B.free(b, t_ox)
    linear(I["w_xo"][0], 0, 1024, OXh, OXl, 8, t_ox, ev_res)
    t_h = t_g[0]
    tap("h2", H[:, :, :], t_h)

    P.barrier()
    t_xt = norm_split(H, 8, 1024, col["norm_moe"], XUh[:, :, :], XUl[:, :, :], [t_h])
    CBt = R("CBt", [128, 32, 256], F32, 0)
    lg = R("lg", [128, 2, 40], F32, 32 * KB)
    rt = R("rt", [128, 256], F32, 31 * KB)
    comb = R("comb", [128, 2, 128], F32, 33 * KB)
    combT = R("combT", [128, 256], F32, 34 * KB)
    h, l, tw, i = W.next([(0, 8, 4, kp(I["w_router_group"][0], 8)), (4, 8, 32, kp(I["w_router_expert"][0], 8))])
    b, ps, tf = B.get()
    for j in range(2):
        t = triple(ps[:, 64 * j:64 * j + 36], lambda k: XUh[:, k, 128 * j:128 * j + 128], lambda k: XUl[:, k, 128 * j:128 * j + 128],
                   lambda k: h[:, k, :], lambda k: l[:, k, :], 8, True, True, [tw, tf, t_xt])
    W.free(i, t)
    t = P.tt(lg[:, :, 0:36], ps[:, 0:128].rearrange("p (a n) -> p a n", a=2)[:, :, 0:36],
             brt[:, 0:36].unsqueeze(1).broadcast_to([128, 2, 36]), ALU.add, after=[t, t_c])
    B.free(b, t)
    tap("lg", lg[:, :, 0:36], t)

    def first_of(dst, v, mx, n, s):
        P.tt(dst, v, mx.unsqueeze(2).broadcast_to([128, 2, n]), ALU.is_equal)
        P.ts(s, dst, -1000.0, 1000.0, ALU.mult, ALU.add)
        P.tt(s, s, iota[:, 0:n].unsqueeze(1).broadcast_to([128, 2, n]), ALU.add)
        P.red(rt[:, 254:256], s, ALU.min)
        return P.tt(dst, iota[:, 0:n].unsqueeze(1).broadcast_to([128, 2, n]),
                    rt[:, 254:256].unsqueeze(2).broadcast_to([128, 2, n]), ALU.is_equal)

    slots = R("slots", [128, 272], F32, 38 * KB)
    flag = mem["flag"]
    posrow = R("posrow", [128, 2, 256], F32, 36 * KB)
    ohs = R("ohs", [128, 2, 2, 32], F32, 40 * KB)
    sel = R("sel", [128, 2, 32], F32, 41 * KB)
    strict = R("strict", [128, 128], F32, 42 * KB)
    rk = R("rk", [128, 2, 64], F32, 43 * KB)
    t_slots = P.dma(slots[:, :], I["c_slots"], "slots", after=P.last())
    P.put("dve", lambda e: e.memset(comb[:, :, :], 0.0), None)
    P.tt(strict[:, :], ones[:, :], tri, ALU.subtract)
    XTh, XTl = R("XTh", [128, 2, 1024], F32R, 0), R("XTl", [128, 2, 1024], F32R, 8 * KB)
    turned_x = []
    for j in range(2):
        for q in range(2):
            b, ps, tf = B.get()
            for r in range(4):
                t = P.tr(ps[:, 128 * r:128 * r + 128], T8b[:, 4 * q + r, 128 * j:128 * j + 128], ident, after=[tf, t_xt])
            turned_x.append((b, XTh[:, j, 512 * q:512 * q + 512], XTl[:, j, 512 * q:512 * q + 512], ps[:, :], t))

    def pair(i):
        return rt[:, 2 * i:2 * i + 2]

    def eight(i):
        return rt[:, 16 * i:16 * i + 16].rearrange("p (j n) -> p j n", j=2)

    def wide(x, n):
        return x.unsqueeze(2).broadcast_to([128, 2, n])

    gl, el = lg[:, :, 0:4], lg[:, :, 4:36]
    gm, gs, gw, m1, m2, dl, w1, w2 = (pair(i) for i in range(8))
    og, s4, e4 = (rt[:, 16 + 8 * i:24 + 8 * i].rearrange("p (j n) -> p j n", j=2) for i in range(3))
    ein, o1, o2, s8, ea = (eight(i) for i in range(3, 8))
    big = rt[:, 128:192].rearrange("p (j g e) -> p j g e", j=2, g=4)
    P.red(gm, gl, ALU.max)
    t = P.tt(e4, gl, wide(gm, 4), ALU.subtract)
    t_e = P.act(e4, e4, ACT.Exp, after=[t])
    first_of(og, gl, gm, 4, s4)
    P.tt(big, el.rearrange("p j (g e) -> p j g e", g=4), og.unsqueeze(3).broadcast_to([128, 2, 4, 8]), ALU.mult)
    P.red(ein, big.rearrange("p j g e -> p j e g"), ALU.add)
    P.red(m1, ein, ALU.max)
    first_of(o1, ein, m1, 8, s8)
    P.stt(ea, o1, -3.0e38, ein, ALU.mult, ALU.add)
    P.red(m2, ea, ALU.max)
    first_of(o2, ea, m2, 8, s8)
    t = P.tt(dl, m2, m1, ALU.subtract)
    t_w = P.act(w2, dl, ACT.Exp, after=[t])
    for k, o in enumerate((o1, o2)):
        P.tt(ohs[:, :, k, :].rearrange("p j (g e) -> p j g e", g=4), o.unsqueeze(2).broadcast_to([128, 2, 4, 8]),
             og.unsqueeze(3).broadcast_to([128, 2, 4, 8]), ALU.mult)
    t_sel = P.tt(sel[:, :, :], ohs[:, :, 0, :], ohs[:, :, 1, :], ALU.add)
    P.red(gs, e4, ALU.add, after=[t_e])
    P.put("dve", lambda e: e.reciprocal(gw, gs), None)
    P.ts(m1, w2, 1.0, None, ALU.add, after=[t_w])
    P.put("dve", lambda e: e.reciprocal(w1, m1), None)
    P.tt(w1, w1, gw, ALU.mult)
    P.tt(w2, w2, w1, ALU.mult)
    P.tt(comb[:, :, 0:32], ohs[:, :, 0, :], wide(w1, 32), ALU.mult)
    P.tt(rk[:, :, 32:64], ohs[:, :, 1, :], wide(w2, 32), ALU.mult)
    P.tt(comb[:, :, 0:32], comb[:, :, 0:32], rk[:, :, 32:64], ALU.add)
    b, ps, tf = B.get()
    P.mm(ps[:, 0:32], strict[:, :], sel[:, 0, :], after=[t_sel, tf])
    P.mm(ps[:, 32:64], ones[:, :], sel[:, 0, :], True, False)
    P.mm(ps[:, 32:64], strict[:, :], sel[:, 1, :], False, True)
    P.mm(ps[:, 64:96], ones[:, :], sel[:, 0, :], True, False)
    t = P.mm(ps[:, 64:96], ones[:, :], sel[:, 1, :], False, True)
    P.stt(rk[:, :, 0:32], iota.unsqueeze(1).broadcast_to([128, 2, 32]), 64.0, ps[:, 0:64].rearrange("p (j n) -> p j n", j=2),
          ALU.mult, ALU.add, after=[t])
    P.red(rt[:, 253:254], ps[:, 64:96], ALU.max)
    B.free(b, P.copy(flag[:, 0:1], rt[:, 253:254]))
    for k in range(2):
        P.tt(rk[:, :, 32:64], ohs[:, :, k, :], rk[:, :, 0:32], ALU.mult)
        t = P.red(comb[:, :, 32 + k:33 + k], rk[:, :, 32:64], ALU.add)
    b, ps, tf = B.get()
    for j in range(2):
        t2 = P.tr(ps[:, 128 * j:128 * j + 128], comb[:, j, :], ident, after=[t, tf])
    t = P.copy(combT[:, :], ps[:, 0:256], after=[t2])
    B.free(b, t)
    tap("combT", combT[0:32, :], t)
    b, ps, tf = B.get()
    for k in range(2):
        t2 = P.mm(ps[:, 256 * k:256 * k + 256], ident[0:64, 32 + k:33 + k].broadcast_to([64, 128]), combT[0:64, :], after=[t, tf])
    t = P.copy(posrow[:, :, :], ps[:, :].rearrange("p (a n) -> p a n", a=2), after=[t2])
    B.free(b, t)
    for b, h, l, ps, t in turned_x:
        B.free(b, split(h, l, ps, [t]))

    def gated(pfx, steps, xh, xl, ready, group):
        nb = 2 * group
        hs = [R(f"{pfx}hs{j}", [128, 2, 256], F32, (40 + 2 * j) * KB) for j in range(nb)]
        ah = [R(f"{pfx}ah{j}", [128, 2, 256], F32R, (40 + 2 * (nb + j)) * KB) for j in range(nb)]
        al = [R(f"{pfx}al{j}", [128, 2, 256], F32R, (40 + 2 * (2 * nb + j)) * KB) for j in range(nb)]
        ybanks = [B.banks[4 + j] for j in range(4)]
        yfree = flat([B.tok[4 + j] for j in range(4)])
        n = len(steps)
        used = [None] * nb

        def up(e):
            g, u, _, scale, ts = steps[e]
            res = []
            for w in (g, u):
                h, l, tw, i = W.next([(0, 8, 256, kp(w, 8))])
                b, ps, tf = B.get(range(4))
                for j in range(2):
                    t = triple(ps[:, 256 * j:256 * j + 256], lambda k: h[:, k, 128 * j:128 * j + 128],
                               lambda k: l[:, k, 128 * j:128 * j + 128], lambda k: xh[:, k, :], lambda k: xl[:, k, :],
                               8, True, True, [tw, tf, ready])
                W.free(i, t)
                res.append((b, ps[:, :].rearrange("p (a n) -> p a n", a=2), t))
            s = e % nb
            (bg, pg, tg), (bu, pu, tu) = res
            t = P.act(hs[s][:, :, :], pg, ACT.Silu, after=[tg, used[s]])
            B.free(bg, t)
            t = P.tt(hs[s][:, :, :], hs[s][:, :, :], pu, ALU.mult, after=[t, tu])
            B.free(bu, t)
            if scale is not None:
                t = P.tt(hs[s][:, :, :], hs[s][:, :, :], scale.unsqueeze(1).broadcast_to([128, 2, 256]), ALU.mult, after=[ts])
            return split(ah[s][:, :, :], al[s][:, :, :], hs[s][:, :, :], [t, used[s]])

        def down(e, ta):
            h, l, tw, i = W.next([(0, 2, 1024, kp(steps[e][2], 2))])
            s = e % nb
            for d in range(8):
                ps = ybanks[d // 2][:, 256 * (d % 2):256 * (d % 2) + 256]
                for k in range(2):
                    st, sp = e == 0 and k == 0 and d % 2 == 0, e == n - 1 and k == 1
                    c = slice(128 * d, 128 * d + 128)
                    P.mm(ps, h[:, k, c], ah[s][:, k, :], st, False, after=[tw, ta, yfree], loose=True)
                    P.mm(ps, h[:, k, c], al[s][:, k, :], False, False, loose=True)
                    t = P.mm(ps, l[:, k, c], ah[s][:, k, :], False, sp, loose=True)
            W.free(i, t)
            used[s] = t
            return t

        ta = {e: up(e) for e in range(group)}
        for e0 in range(0, n, group):
            for e in range(e0 + group, min(e0 + 2 * group, n)):
                ta[e] = up(e)
            for e in range(e0, min(e0 + group, n)):
                t = down(e, ta[e])
        return [y[:, :].rearrange("p (a n) -> p a n", a=2) for y in ybanks], t

    wg, wu, wd = I["w_exp_gate"][0], I["w_exp_up"][0], I["w_exp_down"][0]

    def add_y(ys, t):
        for j in range(4):
            P.tt(H[:, 2 * j:2 * j + 2, :], H[:, 2 * j:2 * j + 2, :], ys[j], ALU.add, after=[t])

    def dense():
        for q in range(16):
            b, ps, tf = B.get()
            for j in range(2):
                e = 2 * q + j
                t2 = P.mm(ps[:, 256 * j:256 * j + 256], ident[0:32, e:e + 1].broadcast_to([32, 128]), combT[0:32, :], after=[t, tf])
            t_cb = P.act(CBt[:, 2 * q:2 * q + 2, :], ps[:, :].rearrange("p (a n) -> p a n", a=2), ACT.Copy, after=[t2])
            B.free(b, t_cb)
        add_y(*gated("moe", [(wg[e], wu[e], wd[e], CBt[:, e, :], t_cb) for e in range(32)], XUh, XUl, None, 2))

    def sparse():
        Pg = [R(f"Pg{i}", [128, 2, 256], F32R, (16 + 2 * i) * KB) for i in range(2)]
        PT = [R(f"PT_{i}", [128, 256], F32R, (20 + i) * KB) for i in range(2)]
        ah = [R(f"spah{i}", [128, 2, 128], F32R, (22 + i) * KB) for i in range(4)]
        al = [R(f"spal{i}", [128, 2, 128], F32R, (26 + i) * KB) for i in range(4)]
        hs = [R(f"sphs{i}", [128, 256], F32, (34 + i) * KB) for i in range(2)]
        pg = R("pgrp", [128, 8, 2, 2], F32, 30 * KB)
        wsl = R("wsl", [128, 16], F32, 30 * KB + 512)
        eq = [R(f"speq{i}", [128, 256], F32, (31 + i) * KB) for i in range(2)]
        Xgh = [R(f"Xgh{i}", [128, 8, 256], F32R, (40 + 16 * i) * KB) for i in range(2)]
        Xgl = [R(f"Xgl{i}", [128, 8, 256], F32R, (48 + 16 * i) * KB) for i in range(2)]
        Yh = [XUh[:, 4 * i:4 * i + 4, :].rearrange("p a n -> p (a n)") for i in range(2)]
        Yl = [XUl[:, 4 * i:4 * i + 4, :].rearrange("p a n -> p (a n)") for i in range(2)]
        iota256, sid = slots[:, 0:256], slots[:, 256:272]
        ybanks = [B.banks[4 + j] for j in range(4)]
        dbanks = [None, None]

        for i in range(4):
            o = 64 * (1 - i % 2)
            for x in (ah[i], al[i]):
                t_z = P.ts(x[:, :, o:o + 64], ones[:, 0:128].rearrange("p (a n) -> p a n", a=2), 0.0, None, ALU.mult,
                           after=[t_slots])
        for g in range(8):
            t_pg = P.ts(pg[:, g, :, :], comb[:, :, 32:34], -256.0 * g, None, ALU.add)
        used = [None] * 4
        ready = {}

        def gather(g):
            s = g % 2
            for j in range(2):
                P.ts(eq[j][:, :], iota256, pg[:, g, j, 0:1], None, ALU.is_equal)
                t = P.stt(Pg[s][:, j, :], iota256, pg[:, g, j, 1:2], eq[j][:, :], ALU.is_equal, ALU.add, after=used)
            yield
            b, ps, tf = B.get(range(4))
            for r in range(2):
                for j in range(2):
                    t2 = P.mm(ps[:, 2 * r:2 * r + 2], Pg[s][:, j, 128 * r:128 * r + 128].bitcast(F32),
                              comb[:, j, 4 * g + 2 * r:4 * g + 2 * r + 2], j == 0, j == 1, after=[t, tf])
            for r in range(2):
                for o in range(2):
                    p = slice(64 * o, 64 * o + 64)
                    t3 = P.act(wsl[p, 2 * g + r:2 * g + r + 1], ps[p, 2 * r + o:2 * r + o + 1], ACT.Copy, after=[t2])
            B.free(b, t3)
            toks = [t3]
            for q in range(4):
                for x, X, eng in ((XTh, Xgh, "act"), (XTl, Xgl, "dve")):
                    b, ps, tf = B.get(range(4))
                    for r in range(2):
                        for j in range(2):
                            k = 2 * q + r
                            t2 = P.mm(ps[:, 256 * r:256 * r + 256], x[:, j, 128 * k:128 * k + 128], Pg[s][:, j, :],
                                      j == 0, j == 1, after=[t, tf])
                    v = ps[:, :].rearrange("p (a n) -> p a n", a=2)
                    if eng == "act":
                        t3 = P.act(X[s][:, 2 * q:2 * q + 2, :], v, ACT.Copy, after=[t2])
                    else:
                        t3 = P.copy(X[s][:, 2 * q:2 * q + 2, :], v, after=[t2])
                    B.free(b, t3)
                    toks.append(t3)
                    yield
            ready[g] = toks

        def up(e):
            g, s, p = e // 4, (e // 4) % 2, e // 2
            c = slice(128 * (p % 2), 128 * (p % 2) + 128)
            b, ps, tf = B.get(range(4))
            for n, w in enumerate((wg[e], wu[e])):
                h, l, tw, i = W.next([(0, 8, 256, kp(w, 8))])
                t = triple(ps[:, 256 * n:256 * n + 256], lambda k: Xgh[s][:, k, c], lambda k: Xgl[s][:, k, c],
                           lambda k: h[:, k, :], lambda k: l[:, k, :], 8, True, True, [tw, tf, ready[g]])
                W.free(i, t)
            r = slice(64 * (e % 2), 64 * (e % 2) + 64)
            x = hs[p % 2]
            t = P.act(x[r, :], ps[r, 0:256], ACT.Silu, after=[t, turned[p % 2]])
            t = P.stt(x[r, :], x[r, :], wsl[r, p:p + 1], ps[r, 256:512], ALU.mult, ALU.mult, after=[t, ready[g]])
            B.free(b, t)
            return t

        turned = [None, None]

        def turn(p, t):
            b, ps, tf = B.get(range(4))
            for k in range(2):
                t2 = P.tr(ps[:, 128 * k:128 * k + 128], hs[p % 2][:, 128 * k:128 * k + 128], ident, after=[t, tf])
            turned[p % 2] = t2
            v = ps[:, 0:256].rearrange("p (a n) -> p a n", a=2)
            own = [((2 * p + o) % 4, slice(64 * o, 64 * o + 64)) for o in range(2)]
            for u, c in own:
                t3 = P.act(ah[u][:, :, c], v[:, :, c], ACT.Copy, after=[t2, used[u]])
            for u, c in own:
                t3 = P.tt(al[u][:, :, c], v[:, :, c], ah[u][:, :, c].bitcast(F32), ALU.subtract, after=[t3, used[u]])
            B.free(b, t3)
            return t3

        def down(e, ta):
            h, l, tw, i = W.next([(0, 2, 1024, kp(wd[e], 2))])
            u, odd = e % 4, e % 2 == 1
            if not odd:
                dbanks[:] = [B.get(range(4)) for _ in range(2)]
            for f in range(2):
                c = slice(512 * f, 512 * f + 512)
                for k in range(2):
                    ps = dbanks[f][1][:, :]
                    P.mm(ps, ah[u][:, k, :], h[:, k, c], not odd and k == 0, False, after=[tw, ta, t_z, dbanks[f][2]])
                    P.mm(ps, al[u][:, k, :], h[:, k, c], False, False)
                    t = P.mm(ps, ah[u][:, k, :], l[:, k, c], False, odd and k == 1)
            W.free(i, t)
            used[u] = t
            return t

        back = [None, None]

        def leave(p, t):
            s = p % 2
            P.ts(eq[0][:, :], posrow[:, 0, :], sid[:, p:p + 1], None, ALU.is_equal)
            P.stt(PT[s][:, :], posrow[:, 1, :], sid[:, p:p + 1], eq[0][:, :], ALU.is_equal, ALU.add, after=[back[s]])
            for f in range(2):
                c = slice(512 * f, 512 * f + 512)
                td = split(Yh[s][:, c], Yl[s][:, c], dbanks[f][1][:, :], [t, back[s]])
                B.free(dbanks[f][0], td)
            return td

        def scatter(p, t):
            s = p % 2
            for d in range(8):
                ps = ybanks[d // 2][:, 256 * (d % 2):256 * (d % 2) + 256]
                c = slice(128 * d, 128 * d + 128)
                P.mm(ps, Yh[s][:, c], PT[s][:, :], p == 0 and d % 2 == 0, False, after=[t], loose=True)
                t2 = P.mm(ps, Yl[s][:, c], PT[s][:, :], False, p == 15, loose=True)
            back[s] = t2
            return t2

        def step():
            if not work:
                return
            try:
                next(work[0])
            except StopIteration:
                work.pop()

        work = [gather(0)]
        while work:
            step()
        up(0)
        tu, late = up(1), None
        for p in range(16):
            if p % 2 == 0 and p < 14:
                work.append(gather(p // 2 + 1))
                step()
            if p < 15:
                up(2 * p + 2)
            step()
            ta = turn(p, tu)
            if p < 15:
                tu = up(2 * p + 3)
            while len(work) > 0:
                step()
            if late:
                scatter(*late)
            down(2 * p, ta)
            late = (p, leave(p, down(2 * p + 1, ta)))
        t = scatter(*late)
        add_y([y[:, :].rearrange("p (a n) -> p a n", a=2) for y in ybanks], t)

    state, count = W.state(), P.count
    ends.append(W.i)
    enter("sparse", state, bounds[1], count, 1)
    sparse()
    after_sparse, n_sparse = W.state(), dict(P.count)
    if seq is None:
        W.rec = W.rec[:state[2]]
    enter("dense", state, bounds[1], count, 1)
    dense()
    ends.append(W.i)
    assert W.state()[:3] == after_sparse[:3] and P.count == n_sparse
    enter("end", W.state(), bounds[2], P.count)
    t_h = None
    if seq is not None:
        W.ahead()
    t_h = [x[2] for x in norm(H, 8, 1024, col["norm_final"], H, [t_h])]
    tap("h3", H[:, :, :], t_h)

    P.barrier()
    reset = R("reset", [128, 1024], F32, 70 * KB)
    t_reset = P.dma(reset[:, :], I["c_reset"], "reset", after=P.last())
    t_u2 = norm_split(H, 8, 1024, col["attn_pre_norm_2"], XUh[:, :, :], XUl[:, :, :], [t_h])
    w2 = I["w_in_2"][0]
    hq, hz = R("hq", [128, 4, 256], F32, 0), R("hz", [128, 4, 256], F32, 4 * KB)
    hv_, hg = R("hv", [128, 2, 512], F32, 8 * KB), R("hg", [128, 4, 256], F32, 12 * KB)
    sq_, sk_ = R("sq", [128, 4, 256], F32, 16 * KB), R("sk", [128, 4, 256], F32, 20 * KB)
    sv_ = R("sv", [128, 2, 512], F32, 24 * KB)

    def ev_f(dst, func):
        def ev(f, n, ps, t):
            t_g[0] = P.act(dst[:, f:f + n, :], ps, func, after=[t])
            return t_g[0]
        return ev

    linear(w2, 0, 512, XUh, XUl, 8, t_u2, ev_f(hq, ACT.Silu))
    linear(w2, 1536, 512, XUh, XUl, 8, t_u2, ev_f(hg, ACT.Silu))
    linear(w2, 512, 512, XUh, XUl, 8, t_u2, ev_f(hz, ACT.Copy))
    linear_tok(w2, 1024, 512, XUh, XUl, 8, t_u2, ev_tok(hv_))
    linear(w2, 2048, 512, XUh, XUl, 8, t_u2, ev_f(sq_, ACT.Copy))
    linear(w2, 2560, 512, XUh, XUl, 8, t_u2, ev_f(sk_, ACT.Copy))
    linear_tok(w2, 3072, 512, XUh, XUl, 8, t_u2, ev_tok(sv_))
    t_in = t_g[0]
    tap("hz", hz[:, :, :], t_in)
    tap("hq", hq[:, :, :], t_in)

    gam = col["hg_lower_gamma_2"]
    lb = mem["lb"]
    P.tt(lb[:, 0:4], gam[:, 0:4], gam[:, 4:8], ALU.max, after=[t_vec])
    P.tt(lb[:, 4:8], gam[:, 0:4], lb[:, 0:4], ALU.subtract)
    t = P.tt(lb[:, 8:12], gam[:, 4:8], lb[:, 0:4], ALU.subtract)
    t = P.act(lb[:, 12:20], lb[:, 4:12], ACT.Exp, after=[t])
    t = P.tt(lb[:, 20:24], lb[:, 12:16], lb[:, 16:20], ALU.add, after=[t])
    t = P.act(lb[:, 20:24], lb[:, 20:24], ACT.Ln, after=[t])
    P.tt(lb[:, 24:28], lb[:, 4:8], lb[:, 20:24], ALU.subtract, after=[t])
    t = P.tt(lb[:, 28:32], lb[:, 8:12], lb[:, 20:24], ALU.subtract)
    lA = lb[:, 24:28].unsqueeze(2).broadcast_to([128, 4, 256])
    lC = lb[:, 28:32].unsqueeze(2).broadcast_to([128, 4, 256])
    e1, e2, e3 = (R(f"he{j}", [128, 4, 256], F32, (28 + 4 * j) * KB) for j in range(3))
    hk, hb = R("hk", [128, 4, 256], F32, 40 * KB), R("hb", [128, 4, 256], F32, 44 * KB)
    a = lambda x: x[:, :, :]
    t = P.act(a(e1), a(hz), ACT.Abs, after=[t_in])
    t = P.act(a(e1), a(e1), ACT.Exp, after=[t], scale=-1.0)
    t = P.act(a(e1), a(e1), ACT.Ln, bias=1.0, scale=1.0)
    P.stt(a(e2), a(hz), 0.0, a(e1), ALU.min, ALU.subtract, after=[t])
    P.tt(a(e2), a(e2), lC, ALU.add)
    t = P.tt(a(hk), a(e2), a(hz), ALU.subtract)
    t_hk = P.act(a(hk), a(hk), ACT.Exp, after=[t])
    P.tt(a(e3), a(e2), lA, ALU.max)
    t = P.tt(a(e2), a(e2), lA, ALU.subtract)
    t = P.act(a(e2), a(e2), ACT.Abs, after=[t])
    t = P.act(a(e2), a(e2), ACT.Exp, after=[t], scale=-1.0)
    t = P.act(a(e2), a(e2), ACT.Ln, bias=1.0, scale=1.0)
    P.tt(a(e3), a(e3), a(e2), ALU.add, after=[t])
    t_b = P.put("dve", lambda e: e.tensor_tensor_scan(hb[:, :, :].rearrange("p a n -> p (a n)"), reset[:, :],
                                                      e3[:, :, :].rearrange("p a n -> p (a n)"), 0.0, ALU.mult, ALU.add), [t_reset])
    tap("hb", a(hb), t_b)
    tap("hk", a(hk), [t_b, t_hk])
    SC0, SC1 = R("SC0", [128, 4, 256], F32, 48 * KB), R("SC1", [128, 4, 128], F32, 52 * KB)
    Xs = [R(f"X{j}", [128, 4, 256], F32, (54 + 4 * j) * KB) for j in range(2)]
    diag = [SC0[:, :, 0:128], SC1[:, :, :]]
    id4 = ident.unsqueeze(1).broadcast_to([128, 4, 128])
    for j in range(2):
        b, ps, tf = B.get()
        for hd in range(4):
            t = P.mm(ps[:, 128 * hd:128 * hd + 128], hk[:, hd, 128 * j:128 * j + 128], hq[:, hd, 128 * j:128 * j + 128], after=[t_hk, t_in, tf])
        t_sc = P.tt(diag[j], ps[:, :].rearrange("p (a n) -> p a n", a=4), id4, ALU.mult, after=[t])
        B.free(b, t_sc)
    xt = [None, None]
    for lv in range(8):
        L = 2 << lv
        m = L // 2
        X = Xs[lv % 2]
        if L <= 64:
            v = lambda z: z[:, :, :].rearrange("p a (n l) -> p (a n) l", l=L)
            nb = 1024 // L
            mid = v(hb)[:, :, m - 1:m].broadcast_to([128, nb, m])
            P.tt(v(X)[:, :, 0:m], mid, v(hb)[:, :, 0:m], ALU.subtract, after=[t_b, xt[lv % 2]])
            t = P.tt(v(X)[:, :, m:L], v(hb)[:, :, m:L], mid, ALU.subtract)
        elif L == 128:
            v = lambda z: z[:, :, :].rearrange("p a (n l) -> p (a n) l", l=128)
            mid = v(hb)[:, :, 63:64].broadcast_to([128, 8, 64])
            P.tt(v(X)[:, :, 0:64], mid, v(hb)[:, :, 0:64], ALU.subtract, after=[xt[lv % 2]])
            t = P.copy(v(X)[:, :, 64:128], v(hb)[:, :, 64:128])
        else:
            v = lambda z: z[:, :, :]
            m = 128
            en = lambda c: hb[:, :, 64 * c + 63:64 * c + 64].broadcast_to([128, 4, 64])
            sl = lambda z, c: z[:, :, 64 * c:64 * c + 64]
            P.tt(sl(X, 0), en(0), sl(hb, 0), ALU.subtract, after=[xt[lv % 2]])
            P.tt(sl(X, 0), sl(X, 0), en(1), ALU.add)
            P.tt(sl(X, 1), en(1), sl(hb, 1), ALU.subtract)
            P.copy(sl(X, 2), sl(hb, 2))
            t = P.tt(sl(X, 3), sl(hb, 3), en(2), ALU.add)
        t = P.act(a(X), a(X), ACT.Exp, after=[t])
        if L == 256:
            P.tt(X[:, :, 0:128], X[:, :, 0:128], hk[:, :, 0:128], ALU.mult, after=[t, t_hk])
            t = P.tt(X[:, :, 128:256], X[:, :, 128:256], hq[:, :, 128:256], ALU.mult)
            b, ps, tf = B.get()
            for hd in range(4):
                t2 = P.mm(ps[:, 128 * hd:128 * hd + 128], X[:, hd, 0:128], X[:, hd, 128:256], after=[t, tf])
            t_sc = P.copy(SC0[:, :, 128:256], ps[:, :].rearrange("p (a n) -> p a n", a=4), after=[t2])
            B.free(b, t_sc)
        else:
            P.tt(v(X)[:, :, 0:m], v(X)[:, :, 0:m], v(hk)[:, :, 0:m], ALU.mult, after=[t, t_hk])
            t = P.tt(v(X)[:, :, m:L], v(X)[:, :, m:L], v(hq)[:, :, m:L], ALU.mult)
            mk = masks[:, 128 * lv:128 * lv + 128].unsqueeze(1).broadcast_to([128, 4, 128])
            for j in range(2):
                b, ps, tf = B.get()
                for hd in range(4):
                    s = X[:, hd, 128 * j:128 * j + 128]
                    t2 = P.mm(ps[:, 128 * hd:128 * hd + 128], s, s, after=[t, tf])
                t_sc = P.put("dve", lambda e, j=j, mk=mk, ps=ps: e.copy_predicated(
                    diag[j], mk, ps[:, :].rearrange("p (a n) -> p a n", a=4)), [t2])
                B.free(b, t_sc)
            xt[lv % 2] = t2
    tap("SC0", SC0[:, :, :], t_sc)
    oh = R("oh", [128, 4, 256], F32, 28 * KB)
    for q in range(2):
        b, ps, tf = B.get()
        for r in range(2):
            hd = 2 * q + r
            d = ps[:, 256 * r:256 * r + 256]
            P.mm(d, hv_[:, 0, 128 * hd:128 * hd + 128], SC0[:, hd, :], True, False, after=[t_sc, tf])
            t = P.mm(d[:, 128:256], hv_[:, 1, 128 * hd:128 * hd + 128], SC1[:, hd, :], False, True)
        t_oh = P.copy(oh[:, 2 * q:2 * q + 2, :], ps[:, :].rearrange("p (a n) -> p a n", a=2), after=[t])
        B.free(b, t_oh)
    MIh, MIl = R("MIh", [128, 8, 256], F32R, 62 * KB), R("MIl", [128, 8, 256], F32R, 0)
    norm(oh, 4, 512, col["hg_out_norm_2"], T8b, [t_oh])
    t = P.tt(T8b[:, 0:4, :], T8b[:, 0:4, :], a(hg), ALU.mult)
    tap("ohg", T8b[:, 0:4, :], t)
    t_mi = Ready([split(MIh[:, 0:4, :], MIl[:, 0:4, :], T8b[:, 0:4, :], [t])] * 4)
    busy[0] = t_mi[0]

    osb = R("osb", [128, 4, 256], F32, 32 * KB)
    Z = R("Z", [128, 4, 384], F32, 36 * KB)
    Sp = R("Sp", [128, 4, 384], F32, 42 * KB)
    P.barrier()
    t_pv = None
    for g in range(2):
        for hl in range(4):
            hd = 4 * g + hl
            o, tl = 64 * (hd % 2), hd // 2
            b, ps, tf = B.get()
            P.mm(ps[:, 0:256], sk_[o:o + 64, tl, 0:128], sq_[o:o + 64, tl, :], after=[t_in, tf])
            t = P.mm(ps[:, 256:384], sk_[o:o + 64, tl, 128:256], sq_[o:o + 64, tl, 128:256])
            P.stt(Z[:, hl, 0:128], ps[:, 0:128], 0.125, n_st, ALU.mult, ALU.add, after=[t, t_pv])
            P.ts(Z[:, hl, 128:256], ps[:, 128:256], 0.125, None, ALU.mult)
            t = P.stt(Z[:, hl, 256:384], ps[:, 256:384], 0.125, n_st, ALU.mult, ALU.add)
            B.free(b, t)
        t = P.act(a(Sp), a(Z), ACT.Abs, after=[t, t_pv])
        t = P.act(a(Sp), a(Sp), ACT.Exp, after=[t], scale=-1.0)
        t = P.act(a(Sp), a(Sp), ACT.Ln, bias=1.0, scale=1.0)
        t_sp = P.stt(a(Sp), a(Z), 0.0, a(Sp), ALU.max, ALU.add, after=[t])
        for hl in range(4):
            b, ps, tf = B.get()
            P.mm(ps[:, 0:256], tri, Sp[:, hl, 0:256], True, False, after=[t_sp, tf])
            P.mm(ps[:, 128:256], ones[:, :], Sp[:, hl, 256:384], False, True)
            t = P.mm(ps[:, 256:384], tri, Sp[:, hl, 256:384])
            t = P.tt(Z[:, hl, :], Z[:, hl, :], ps[:, 0:384], ALU.subtract, after=[t])
            B.free(b, t)
        t = P.act(a(Z), a(Z), ACT.Exp, after=[t])
        b, ps, tf = B.get()
        for hl in range(4):
            hd = 4 * g + hl
            o = 64 * (hl % 2)
            d = ps[o:o + 64, 256 * (hl // 2):256 * (hl // 2) + 256]
            P.mm(d, sv_[:, 0, 64 * hd:64 * hd + 64], Z[:, hl, 0:256], True, False, after=[t, tf])
            t_pv = P.mm(d[:, 128:256], sv_[:, 1, 64 * hd:64 * hd + 64], Z[:, hl, 256:384], False, True)
        t_os = P.copy(osb[:, 2 * g:2 * g + 2, :], ps[:, :].rearrange("p (a n) -> p a n", a=2), after=[t_pv])
        B.free(b, t_os)
    tap("osb", osb[:, :, :], t_os)
    t_mi += norm_split(osb, 4, 512, col["sb_out_norm_2"], MIh[:, 4:8, :], MIl[:, 4:8, :], [t_os])

    mx = R("mx", [128, 8, 256], F32, 48 * KB)
    linear(I["w_out_2"][0], 0, 1024, MIh, MIl, 8, t_mi, ev_to(mx))

    def post(src, gain, after):
        for k0, k1, t in norm(src, 8, 1024, gain, T8b, after):
            busy[0] = t = P.tt(H[:, k0:k1, :], H[:, k0:k1, :], T8b[:, k0:k1, :], ALU.add)
        return t

    t_h = post(mx, col["attn_post_norm_2"], [t_g[0]])
    tap("h4", H[:, :, :], t_h)

    P.barrier()
    t_u3 = norm_split(H, 8, 1024, col["ffn_pre_norm_2"], XUh[:, :, :], XUl[:, :, :], [t_h])
    pin = R("pin", [128, 2, 256], F32, 0)
    pT = R("pT", [128, 2, 256], F32, 2 * KB)
    PTh, PTl = R("PTh", [128, 2, 256], F32R, 4 * KB), R("PTl", [128, 2, 256], F32R, 6 * KB)
    wgu, wdn = I["w_gate_up_2"][0], I["w_down_2"][0]
    ys, t = gated("ffn", [(wgu[:, 256 * c:256 * c + 256], wgu[:, 2816 + 256 * c:2816 + 256 * c + 256],
                           wdn[256 * c:256 * c + 256, :], None, None) for c in range(11)], XUh, XUl, t_u3, 1)
    ff = R("ff", [128, 8, 256], F32, 52 * KB)
    for j in range(4):
        t2 = P.copy(ff[:, 2 * j:2 * j + 2, :], ys[j], after=[t])
        B.free(4 + j, t2)
    t_h = post(ff, col["ffn_post_norm_2"], [t2])
    tap("h5", H[:, :, :], t_h)

    t_p = P.dma(pin[:, :, :], I["p_2"][0, 0].rearrange("(t p) d -> p t d", p=128), "p", after=[t_u3])
    b, ps, tf = B.get()
    for j in range(4):
        t = P.tr(ps[:, 128 * j:128 * j + 128], pin[:, j % 2, 128 * (j // 2):128 * (j // 2) + 128], ident, after=[t_p, tf])
    t = P.copy(pT[:, :, :], ps[:, :].rearrange("p (a n) -> p a n", a=2), after=[t])
    B.free(b, t)
    t_pt = split(PTh[:, :, :], PTl[:, :, :], pT[:, :, :], [t])
    t_hx = split(XUh[:, :, :], XUl[:, :, :], H[:, :, :], [t_h] + P.last())
    pg = R("pg", [128, 8, 256], F32, 60 * KB)
    linear(I["ple_gate_2"][0], 0, 1024, XUh, XUl, 8, t_hx, ev_f(pg, ACT.Sigmoid))
    t_pg = t_g[0]

    def ev_ple(f, n, ps, t):
        t = P.tt(pg[:, f:f + n, :], pg[:, f:f + n, :], ps, ALU.mult, after=[t, t_pg])
        t_g[0] = P.tt(H[:, f:f + n, :], H[:, f:f + n, :], pg[:, f:f + n, :], ALU.add, after=[t_h])
        return t

    linear(I["ple_proj_2"][0], 0, 1024, PTh, PTl, 2, t_pt, ev_ple, k_cols=256)
    t_h = t_g[0]
    ot = R("ot", [128, 2, 1024], F32, 68 * KB)
    for j in range(2):
        for q in range(2):
            b, ps, tf = B.get()
            for r in range(4):
                t = P.tr(ps[:, 128 * r:128 * r + 128], H[:, 4 * q + r, 128 * j:128 * j + 128], ident, after=[t_h, tf])
            t = P.copy(ot[:, j, 512 * q:512 * q + 512], ps[:, :], after=[t])
            B.free(b, t)
        P.dma(out[0, 128 * j:128 * j + 128, :], ot[:, j, :], "out", after=[t])
    return W.rec, ends + [W.i]


def build(nc, I, out, taps=None):
    base = (nc.sbuf_base + 63) // 64 * 64
    at = [base]
    used = set()

    def sb(name, shape, dt, offset=None):
        n = 1
        for s in shape[1:]:
            n *= s
        n *= 1 if dt == U8 else 4
        if offset is None:
            offset = at[0]
            at[0] += (n + 63) // 64 * 64
        return nc.alloc_sbuf_tensor_at(name, shape, dt, offset=offset)

    mem = {"sb": sb}
    mem["raw"] = [sb(f"raw{i}", [128, PIECE], F32) for i in range(NRAW)]
    mem["hi"] = [sb(f"whi{i}", [128, PIECE], F32R) for i in range(NSPL)]
    mem["lo"] = [sb(f"wlo{i}", [128, PIECE], F32R) for i in range(NSPL)]
    mem["XUh"], mem["XUl"] = sb("XUh", [128, 8, 256], F32R), sb("XUl", [128, 8, 256], F32R)
    mem["H"] = sb("H", [128, 8, 256], F32)
    for name, part in (("T8", "hi"), ("T8b", "lo")):
        offset = at[0]
        mem[name] = sb(name, [128, 8, 256], F32)
        mem[part].append(sb(f"w{part}3", [128, PIECE], F32R, offset))
    mem["cst"] = sb("cst", [128, 896], F32)
    mem["ones"] = sb("ones", [128, 128], F32)
    mem["masks"] = sb("masks", [128, 896], U8)
    mem["vec"] = sb("vec", [128, 256], F32)
    mem["small"] = sb("small", [128, 64], F32)
    mem["brt"] = sb("brt", [128, 36], F32)
    mem["rs"] = sb("rs", [128, 512], F32)
    mem["cs"] = sb("cs", [128, 2, 256], F32)
    mem["sm"] = sb("sm", [128, 128], F32)
    mem["lb"] = sb("lb", [128, 32], F32)
    mem["flag"] = sb("flag", [128, 4], I32)
    top = nc.sbuf_usable_end // 64 * 64
    rbase = at[0]
    size = top - rbase
    made = {}

    def R(name, shape, dt, offset):
        if name not in made:
            n = 4
            for s in shape[1:]:
                n *= s
            assert offset + n <= size, (name, offset + n, size)
            made[name] = sb(name, shape, dt, rbase + offset)
        return made[name]

    mem["R"] = R
    mem["posi"] = R("posi", [128, 256], I32, 18 * KB)
    mem["ps"] = [nc.alloc_psum_tensor(f"ps{i}", [128, 512], F32) for i in range(8)]
    names = ("start", "sparse", "dense", "end")
    rec, bounds = program(nc, I, out, {n: Prog(n) for n in names}, mem, None, (0, 0, 0), taps)
    parts = {n: Prog(n) for n in names}
    program(nc, I, out, parts, mem, rec, bounds, taps)
    total = parts["end"].count
    sems = {n: nc.alloc_semaphore(f"s_{n}") for n in [e + n for n in names for e in Prog.ENGINES[:4]] + sorted(total)}
    runs = {n: p.emit(nc, sems) for n, p in parts.items()}
    flag = mem["flag"]

    def run(name, e):
        runs["start"](name, e)
        most = e.value_load(flag[0:1, 0:1])
        with e.If(most > CAP):
            runs["dense"](name, e)
        with e.If(most <= CAP):
            runs["sparse"](name, e)
        runs["end"](name, e)

    with nc.Block() as block:

        @block.tensor
        def _(e):
            run("pe", e)

        @block.scalar
        def _(e):
            run("act", e)

        @block.vector
        def _(e):
            run("dve", e)

        @block.gpsimd
        def _(e):
            run("pool", e)

        @block.sync
        def _(e):
            run("sp", e)
            for n in ("out", "taps"):
                if n in total:
                    e.wait_ge(sems[n], total[n])


def kernel(**inputs):
    import concourse.bacc as bacc
    from concourse.bass_utils import run_bass_kernel_spmd

    nc = bacc.Bacc("TRN2", target_bir_lowering=False, num_devices=1)
    arrays = {f"in_{k}": np.ascontiguousarray(v) for k, v in inputs.items()}
    arrays.update({f"in_{k}": v for k, v in constants().items()})
    aps = {k[3:]: nc.dram_tensor(k, a.shape, mybir.dt.from_np(a.dtype), kind="ExternalInput").ap() for k, a in arrays.items()}
    out = nc.dram_tensor("out_0", (1, 256, 1024), F32, kind="ExternalOutput").ap()
    build(nc, aps, out)
    r = run_bass_kernel_spmd(nc, [arrays], core_ids=[0])
    return r.results[0]["out_0"]
```

```python
import numpy as np
import concourse.bass as bass
from concourse import mybir

F32 = mybir.dt.float32
F32R = mybir.dt.float32r
I32 = mybir.dt.int32
U8 = mybir.dt.uint8
ALU = mybir.AluOpType
ACT = mybir.ActivationFunctionType
AX = mybir.AxisListType
KB = 1024
NEG = -1.0e30
EPS = 1e-6

NRAW = 4
NSPL = 3
PIECE = 2048
CAP = 64


def flat(x):
    if x is None:
        return []
    if isinstance(x, list):
        return [t for y in x for t in flat(y)]
    return [x]


class Prog:

    ENGINES = ("pe", "act", "dve", "pool", "sp")

    def __init__(self, part):
        self.part = part
        self.q = {e: [] for e in self.ENGINES}
        self.held = {e: [] for e in self.ENGINES}
        self.end = {}
        self.count = {}
        self.table = self.TABLES[ACT.Ln if part in ("start", "end") else ACT.Silu]
        self.tables = {0: self.table}

    TABLES = {ACT.Ln: "natural_log_exp_and_others", ACT.Exp: "natural_log_exp_and_others",
              ACT.Silu: "silu_and_others", ACT.Sigmoid: "sigmoid_and_others", ACT.Sin: "silu_and_others"}

    def put(self, e, fn, after, chain=True):
        waits = flat(after) + self.held[e]
        self.held[e] = []
        if chain and e in ("act", "dve", "pool") and e in self.end:
            waits.append((e, self.end[e], self.part))
        self.end[e] = len(self.q[e])
        self.q[e].append((fn, waits, None))
        return e, len(self.q[e]) - 1, self.part

    def dma(self, out, in_, sem, after=None, eng="sp"):
        waits = flat(after) + self.held[eng]
        self.held[eng] = []
        self.count[sem] = self.count.get(sem, 0) + 16
        self.q[eng].append((lambda e: e.dma_start(out, in_), waits, sem))
        return "dma", sem, self.count[sem]

    def last(self):
        return [(e, self.end[e], self.part) for e in ("pe", "act", "dve", "pool") if e in self.end]

    def barrier(self):
        for e in ("pe", "act", "dve", "pool"):
            self.held[e] += [t for t in self.last() if t[0] != e]

    def act(self, out, in_, func, after=None, chain=True, **kw):
        table = self.TABLES.get(func, self.table)
        if table != self.table:
            self.table = self.tables[len(self.q["act"])] = table
        return self.put("act", lambda e: e.activation(out, in_, func, **kw), after, chain)

    def tt(self, out, a, b, op, after=None, chain=True):
        return self.put("dve", lambda e: e.tensor_tensor(out, a, b, op), after, chain)

    def ts(self, out, a, s1, s2, op0, op1=None, after=None):
        if op1 is None:
            return self.put("dve", lambda e: e.tensor_scalar(out, a, s1, None, op0), after)
        return self.put("dve", lambda e: e.tensor_scalar(out, a, s1, s2, op0, op1), after)

    def stt(self, out, a, s, b, op0, op1, after=None, chain=True):
        return self.put("dve", lambda e: e.scalar_tensor_tensor(out=out, in0=a, scalar=s, in1=b, op0=op0, op1=op1), after, chain)

    def red(self, out, a, op, after=None):
        return self.put("dve", lambda e: e.tensor_reduce(out, a, AX.X, op), after)

    def copy(self, out, a, after=None):
        return self.put("dve", lambda e: e.tensor_copy(out, a), after)

    def mm(self, out, lhsT, rhs, start=True, stop=True, after=None, loose=False):
        return self.put("pe", lambda e: e.matmul(out, lhsT, rhs, start=start, stop=stop, skip_group_check=loose), after)

    def tr(self, out, in_, ident, after=None):
        return self.put("pe", lambda e: e.transpose(out, in_, ident), after)

    def emit(self, nc, sems):
        need = {e: set() for e in self.ENGINES}
        plans = {}
        for e in self.ENGINES:
            seen, plan = {}, []
            for fn, waits, sem in self.q[e]:
                best = {}
                for t in waits:
                    if t[0] != "dma" and t[2] != self.part:
                        continue
                    key, n = (t[0], t[1]) if t[0] != "dma" else (("dma", t[1]), t[2])
                    if key == e and e in ("pe", "sp"):
                        continue
                    if n == "all":
                        n = self.count[t[1]]
                    best[key] = max(best.get(key, -1), n)
                todo = []
                for key, n in best.items():
                    if seen.get(key, -1) < n:
                        seen[key] = n
                        todo.append((key, n))
                        if isinstance(key, str):
                            need[key].add(n)
                plan.append((fn, todo, sem))
            plans[e] = plan
        for e, n, _ in self.last():
            need[e].add(n)
        value = {}
        for e in self.ENGINES:
            n, value[e] = 0, {}
            for i in sorted(need[e]):
                n += 1
                value[e][i] = n

        def run(e, eng):
            for i, (fn, todo, sem) in enumerate(plans[e]):
                if e == "act" and i in self.tables:
                    eng.preload_act_table_set(self.tables[i])
                for key, n in todo:
                    if isinstance(key, str):
                        eng.wait_ge(sems[key + self.part], value[key][n])
                    else:
                        eng.wait_ge(sems[key[1]], n)
                ins = fn(eng)
                if sem is not None:
                    ins.then_inc(sems[sem], 16)
                elif i in need[e]:
                    ins.then_inc(sems[e + self.part], 1)
            for key, n, _ in self.last():
                eng.wait_ge(sems[key + self.part], value[key][n])

        return run


class Weights:

    def __init__(self, P, raw, hi, lo, seq):
        self.P, self.raw, self.hi, self.lo, self.seq = P, raw, hi, lo, seq
        self.base, self.slots = 0, len(hi)
        self.rec = []
        self.nload = self.nsplit = self.i = 0
        self.limit = len(seq) if seq is not None else 0
        self.split_tok, self.load_tok, self.free_tok = {}, {}, {}

    def _load(self, j):
        views, n = self.seq[j][:2]
        s = j % NRAW
        tok = None
        for off, a, b, v in views:
            dst = self.raw[s][:, off:off + a * b].rearrange("p (a b) -> p a b", a=a) if len(views) == 1 else None
            if dst is None:
                tot = sum(x[2] for x in views)
                dst = self.raw[s][:, 0:a * tot].rearrange("p (a b) -> p a b", a=a)[:, :, off:off + b]
            tok = self.P.dma(dst, v, f"w{s}", after=self.split_tok.get(j - NRAW))
        self.load_tok[j] = tok

    def _split(self, j):
        n, maps = self.seq[j][1:]
        s, d = j % NRAW, (j - self.base) % self.slots
        raw, hi, lo = self.raw[s], self.hi[d], self.lo[d]
        for dst, src in maps or [(lambda x: x[:, 0:n], lambda x: x[:, 0:n])]:
            t = self.P.act(dst(hi), src(raw), ACT.Copy, after=[self.load_tok[j], self.free_tok.get(j - self.slots)], chain=False)
            self.split_tok[j] = self.P.tt(dst(lo), src(raw), dst(hi).bitcast(F32), ALU.subtract,
                                          after=[t, self.load_tok[j], self.free_tok.get(j - self.slots)], chain=False)

    def preload(self):
        while self.nload < NRAW:
            self._load(self.nload)
            self.nload += 1

    def ahead(self, most=None):
        stop = self.limit if most is None else min(self.limit, self.nsplit + most)
        while self.nsplit < stop and self.nsplit < self.i + self.slots and \
                (self.nsplit < self.slots or self.nsplit - self.slots in self.free_tok):
            while self.nload < len(self.seq) and self.nload <= self.nsplit:
                self._load(self.nload)
                self.nload += 1
            self._split(self.nsplit)
            self.nsplit += 1
        while self.nload < len(self.seq) and self.nload - NRAW < self.nsplit:
            self._load(self.nload)
            self.nload += 1

    def next(self, views, maps=None, out=None):
        kt, cols = views[0][1], sum(v[2] for v in views)
        n = kt * cols
        assert n <= PIECE
        self.rec.append((views, n, maps))
        if self.seq is None:
            i = self.i
            self.i += 1
            self.free_tok[i] = None
            d = 0
            tok = None
        else:
            i = self.i
            self.ahead()
            self.i += 1
            d = (i - self.base) % self.slots
            tok = self.split_tok[i]
        n = out or n
        assert n <= PIECE
        h = self.hi[d][:, 0:n].rearrange("p (a b) -> p a b", a=kt)
        l = self.lo[d][:, 0:n].rearrange("p (a b) -> p a b", a=kt)
        return h, l, tok, i

    def free(self, i, tok):
        self.free_tok[i] = tok

    def state(self):
        return self.nload, self.nsplit, self.i, dict(self.load_tok)

    def enter(self, P, state, limit, hi, lo):
        self.P, self.limit = P, limit
        self.nload, self.nsplit, self.i, load = state
        self.hi, self.lo, self.base, self.slots = hi, lo, self.i, len(hi)
        self.load_tok = dict(load)
        self.split_tok = {j: None for j in range(self.nsplit)}
        self.free_tok = {j: None for j in range(self.i)}


class Banks:
    def __init__(self, P, banks):
        self.P, self.banks, self.i = P, banks, {}
        self.tok = [None] * len(banks)

    def get(self, among=None):
        among = tuple(among or range(len(self.banks)))
        i = self.i.get(among, 0)
        self.i[among] = i + 1
        b = among[i % len(among)]
        t, self.tok[b] = self.tok[b], None
        return b, self.banks[b], t

    def free(self, b, tok):
        self.tok[b] = flat(tok)



def constants():
    p = np.arange(128)
    ident = np.eye(128, dtype=np.float32)
    qk = np.where(p[None, :] <= p[:, None], 0.0, NEG).astype(np.float32)
    sl = np.where(p[None, :] >= p[:, None], 0.0, NEG).astype(np.float32)
    st = np.where(p[None, :] > p[:, None], 0.0, NEG).astype(np.float32)
    tri = (p[:, None] >= p[None, :]).astype(np.float32)
    perm = np.zeros((128, 128), np.float32)
    for m in range(128):
        if m % 32 < 16:
            perm[m + 16, m] = -1.0
        else:
            perm[m - 16, m] = 1.0
    inv = (np.float32(10000.0) ** (-(np.arange(16, dtype=np.float32)) / np.float32(16))).astype(np.float32)
    extra = np.zeros((128, 128), np.float32)
    extra[:, 0] = inv[p % 16]
    extra[:, 8:40] = np.arange(32, dtype=np.float32)[None, :]
    cst = np.concatenate([ident, qk, sl, st, tri, perm, extra], axis=1)
    masks = np.zeros((128, 7, 128), np.float32)
    for i in range(7):
        L = 2 << i
        same = (p[:, None] // L) == (p[None, :] // L)
        masks[:, i, :] = same & ((p[:, None] % L) < L // 2) & ((p[None, :] % L) >= L // 2)
    reset = np.tile((np.arange(1024) % 64 != 0).astype(np.float32)[None, :], (128, 1))
    slots = np.concatenate([np.tile(np.arange(256, dtype=np.float32)[None, :], (128, 1)),
                            (128 * np.arange(16)[None, :] + p[:, None]).astype(np.float32)], axis=1)
    return {"c_slots": slots, "c_mat": cst, "c_masks": masks.reshape(128, 7 * 128), "c_reset": reset}


def program(nc, I, out, parts, mem, seq, bounds, taps=None):
    P = parts["start"]
    W = Weights(P, mem["raw"], mem["hi"][:NSPL], mem["lo"][:NSPL], seq)
    W.limit = bounds[0]
    B = Banks(P, mem["ps"])
    ends = []

    def enter(name, state, limit, count, more=0):
        nonlocal P
        P = parts[name]
        P.count = dict(count)
        W.enter(P, state, limit, mem["hi"][:NSPL + more], mem["lo"][:NSPL + more])
        B.P = P
        B.tok = [None] * len(B.banks)
        busy[0] = None

    def tap(name, ap, after):
        if taps is not None:
            t = P.dma(taps[name], ap, "taps", after=after)
            for e in ("pe", "act", "dve"):
                P.held[e].append(t)

    def kp(v, kt):
        return v.rearrange("(k p) n -> p k n", p=128)

    XUh, XUl, H, T8, T8b = mem["XUh"], mem["XUl"], mem["H"], mem["T8"], mem["T8b"]
    cst, ones = mem["cst"], mem["ones"]
    ident = cst[:, 0:128]
    n_qk, n_sl, n_st, tri, perm = (cst[:, 128 * i:128 * (i + 1)] for i in range(1, 6))
    invf, iota = cst[:, 768:769], cst[:, 776:808]
    masks = mem["masks"]
    vec = mem["vec"]
    small = mem["small"]
    R = mem["R"]

    xin = R("xin", [128, 2, 1024], F32, 0)
    vraw = R("vraw", [128, 2, 128], F32, 16 * KB)
    t_x = P.dma(xin[:, :, :], I["x"][0].rearrange("(t p) d -> p t d", p=128), "x")
    t_id = P.dma(cst[:, :], I["c_mat"], "ident", eng="act")

    vecs = [("conv_w", I["conv_w"].rearrange("o k (t p) -> (o k t) p", p=128), 96),
            ("conv_b", I["conv_b"].rearrange("o (t p) -> (o t) p", p=128), 24),
            ("norm_mix", I["norm_mix"].rearrange("o (t p) -> (o t) p", p=128), 8),
            ("ssd_norm", I["ssd_norm"].rearrange("o (t p) -> (o t) p", p=128), 16),
            ("q_a_norm", I["q_a_norm"].rearrange("o (t p) -> (o t) p", p=128), 3),
            ("kv_a_norm", I["kv_a_norm"].rearrange("o (t p) -> (o t) p", p=128), 2),
            ("norm_xattn", I["norm_xattn"].rearrange("o (t p) -> (o t) p", p=128), 8),
            ("norm_mem", I["norm_mem"].rearrange("o (t p) -> (o t) p", p=128), 8),
            ("norm_moe", I["norm_moe"].rearrange("o (t p) -> (o t) p", p=128), 8),
            ("norm_final", I["norm_final"].rearrange("(t p) -> t p", p=128), 8)]
    vecs += [(n, I[n].rearrange("o (t p) -> (o t) p", p=128), k) for n, k in (
        ("attn_pre_norm_2", 8), ("hg_out_norm_2", 4), ("sb_out_norm_2", 4), ("attn_post_norm_2", 8),
        ("ffn_pre_norm_2", 8), ("ffn_post_norm_2", 8), ("hg_lower_gamma_2", 8))]
    col, at = {}, 0
    for name, view, n in vecs:
        assert at // 128 == (at + n - 1) // 128
        t_v = P.dma(vraw[at % 128:at % 128 + n, at // 128, :], view, "vecs", eng="act" if len(col) % 2 else "sp")
        col[name] = vec[:, at:at + n]
        at += n
    nvec = at
    if seq is not None:
        W.preload()
    dtb, alog = small[:, 0:1], small[:, 1:2]
    dsk = small[:, 8:24]
    for c in range(4):
        P.dma(small[32 * c:32 * c + 32, 0:1], I["dt_bias"].rearrange("o h -> h o"), "const")
        P.dma(small[32 * c:32 * c + 32, 1:2], I["a_log"].rearrange("o h -> h o"), "const")
    d32 = small[:, 32:64]
    P.dma(d32, I["d_skip"].broadcast_to([128, 32]), "const")
    brt = mem["brt"]
    P.dma(brt[:, 0:4], I["b_router_group"].broadcast_to([128, 4]), "const")
    P.dma(brt[:, 4:36], I["b_router_expert"].broadcast_to([128, 32]), "const")
    posi = mem["posi"]
    P.dma(posi[:, :], I["positions"].broadcast_to([128, 256]), "const")
    mraw = R("mraw", [128, 896], F32, 64 * KB)
    P.dma(mraw[:, :], I["c_masks"], "const")
    t_c = [t_id, ("dma", "const", "all")]
    t_ones = P.put("pool", lambda e: e.memset(ones[:, :], 1.0), None)
    epsc = small[:, 2:3]
    t_eps = P.put("pool", lambda e: e.memset(epsc, EPS), None)
    P.put("pool", lambda e: e.tensor_copy(masks[:, :], mraw[:, :]), [t_c])

    def split(h, l, src, after):
        t = P.act(h, src, ACT.Copy, after=after)
        return P.tt(l, src, h.bitcast(F32), ALU.subtract, after=[t] + flat(after))

    busy = [None]

    def norm_steps(res, src, nt, D, gain, dst, after, ng=1):
        n = ng * nt
        m = n // 2 if n == 8 else n
        t = P.act(T8[:, 0:m, :], src[:, 0:m, :], ACT.Square, after=[after, busy[0]])
        if m < n:
            t = [t, P.tt(T8[:, m:n, :], src[:, m:n, :], src[:, m:n, :], ALU.mult, after=[after, busy[0]])]
        v = T8[:, 0:n, :].rearrange("p (g k) n -> p g k n", g=ng)
        m = nt
        while m > 1 and m % 2 == 0:
            m //= 2
            t = P.tt(v[:, :, 0:m, :], v[:, :, 0:m, :], v[:, :, m:2 * m, :], ALU.add, after=[t])
        cuts = list(range(0, n, nt)) if ng > 1 else [0, n // 2] if n % 4 == 0 else [0]
        cuts = list(zip(cuts, cuts[1:] + [n]))
        k0, k1 = cuts[0]
        P.tt(T8b[:, k0:k1, :], src[:, k0:k1, :], gain[:, k0:k1].unsqueeze(2).broadcast_to([128, k1 - k0, 256]), ALU.mult,
             after=[t_vec, after])
        t_hg = None
        for k in range(k1, n):
            t_hg = P.act(T8b[:, k, :], src[:, k, :], ACT.Copy, after=[t_vec], chain=k == k1, scale=gain[:, k:k + 1])
        yield
        b, ps, tf = B.get()
        for k in range(m):
            tm = P.mm(ps[:, 0:256 * ng], ones[:, :], v[:, :, k, :], k == 0, k == m - 1, after=[t, tf, t_ones])
        r = mem["rs"][:, 0:256 * ng]
        t = P.act(r, ps[:, 0:256 * ng], ACT.Ln, after=[tm, t_eps, busy[0]], scale=1.0 / D, bias=epsc)
        B.free(b, t)
        t = P.act(r, r, ACT.Exp, scale=-0.5)
        yield
        for k0, k1 in cuts:
            g = k0 // nt
            t2 = P.tt(dst[:, k0:k1, :], T8b[:, k0:k1, :], r[:, 256 * g:256 * g + 256].unsqueeze(1).broadcast_to([128, k1 - k0, 256]),
                      ALU.mult, after=[t, t_hg])
            res.append((k0, k1, t2))
        busy[0] = t2

    def norm(*args):
        res = []
        finish(norm_steps(res, *args))
        return res

    class Ready(list):
        pass

    def norm_split_steps(ready, src, nt, D, gain, h, l, after, ng=1):
        res = []
        yield from norm_steps(res, src, nt, D, gain, T8b, after, ng)
        for k0, k1, t in res:
            busy[0] = split(h[:, k0:k1, :], l[:, k0:k1, :], T8b[:, k0:k1, :], [t])
            ready += [busy[0]] * (k1 - k0)

    def norm_split(*args):
        ready = Ready()
        finish(norm_split_steps(ready, *args))
        return ready

    def triple(ps, h, l, xh, xl, kt, first, last, after, k0=0, loose=False, hl=None):
        tiles = next((x for x in after if isinstance(x, Ready) and len(x) == kt), None)
        after = [x for x in after if x is not tiles]
        for k in range(kt):
            st, sp = first and k == 0, last and k == kt - 1
            t = tiles[k] if tiles else None
            P.mm(ps, h(k), xh(k), st, False, after=[after, t], loose=loose)
            P.mm(ps, h(k), xl(k), False, False, loose=loose)
            t = P.mm(ps, l(k), xh(k), False, sp, loose=loose)
        return t

    side = []

    def advance():
        if side:
            try:
                next(side[0])
            except StopIteration:
                side.pop(0)

    def finish(gen=None):
        if gen is not None:
            for _ in gen:
                pass
        while gen is None and side:
            advance()

    def linear(w, c0, ncol, xh, xl, kt, ready, evac, k_cols=256):
        for c in range(c0, c0 + ncol, k_cols):
            h, l, tw, i = W.next([(0, kt, k_cols, kp(w, kt)[:, :, c:c + k_cols])])
            b, ps, tf = B.get()
            nt = k_cols // 128
            for j in range(nt):
                t = triple(ps[:, 256 * j:256 * j + 256], lambda k: h[:, k, 128 * j:128 * j + 128],
                           lambda k: l[:, k, 128 * j:128 * j + 128], lambda k: xh[:, k, :], lambda k: xl[:, k, :],
                           kt, True, True, [tw, tf, ready])
            W.free(i, t)
            B.free(b, evac((c - c0) // 128, nt, ps[:, 0:256 * nt].rearrange("p (t n) -> p t n", t=nt), t))
            advance()

    def linear_tok(w, c0, ncol, xh, xl, kt, ready, evac):
        for c in range(c0, c0 + ncol, 256):
            h, l, tw, i = W.next([(0, kt, 256, kp(w, kt)[:, :, c:c + 256])])
            b, ps, tf = B.get()
            for j in range(2):
                t = triple(ps[:, 256 * j:256 * j + 256], lambda k: xh[:, k, 128 * j:128 * j + 128],
                           lambda k: xl[:, k, 128 * j:128 * j + 128], lambda k: h[:, k, :], lambda k: l[:, k, :],
                           kt, True, True, [tw, tf, ready])
            W.free(i, t)
            B.free(b, evac(c - c0, ps[:, :].rearrange("p (t n) -> p t n", t=2), t))
            advance()

    for d0 in range(0, 8, 2):
        b, ps, tf = B.get()
        for j in range(4):
            t = P.tr(ps[:, 128 * j:128 * j + 128], xin[:, j % 2, (d0 + j // 2) * 128:(d0 + j // 2 + 1) * 128],
                     ident, after=[t_x, t_id, tf])
        t = P.copy(H[:, d0:d0 + 2, :], ps[:, :].rearrange("p (a n) -> p a n", a=2), after=[t])
        B.free(b, t)
    t_h = t
    b, ps, tf = B.get()
    t_v = [t_id, ("dma", "vecs", "all")]
    t = P.tr(ps[:, 0:128], vraw[:, 0, :], ident, after=[t_v])
    t = P.tr(ps[0:128, 128:128 + nvec - 128], vraw[0:nvec - 128, 1, :], ident[0:nvec - 128, 0:nvec - 128])
    t_vec = P.copy(vec[:, 0:nvec], ps[:, 0:nvec], after=[t])
    B.free(b, t_vec)
    t_u = Ready()
    steps = norm_split_steps(t_u, H, 8, 1024, col["norm_mix"], XUh[:, :, :], XUl[:, :, :], [t_h])
    next(steps)
    if seq is not None:
        W.ahead(2)
    finish(steps)
    tap("u", T8b[:, :, :], t_u)

    w_in = I["w_in"][0]
    xh, xl = XUh, XUl
    dtT, acT = R("dtT", [128, 256], F32, 20 * KB), R("acT", [128, 256], F32, 21 * KB)
    dtk = R("dtk", [128, 2, 2, 32], F32, 22 * KB)
    qa, ckv, kpe = R("qa", [128, 3, 256], F32, 10 * KB), R("ckv", [128, 2, 256], F32, 13 * KB), R("kpe", [128, 256], F32, 15 * KB)
    rep4 = [(lambda x: x[:, 0:1024].rearrange("p (k c d) -> p k c d", k=8, c=4),
             lambda x: x[:, 0:256].rearrange("p (k d) -> p k d", k=8).unsqueeze(2).broadcast_to([128, 8, 4, 32]))]
    h, l, tw, i = W.next([(0, 8, 32, kp(w_in, 8)[:, :, 5120:5152])], rep4, 1024)
    b, ps, tf = B.get()

    t = triple(ps[:, 0:256], lambda k: h[:, k, :], lambda k: l[:, k, :],
               lambda k: xh[:, k, :], lambda k: xl[:, k, :], 8, True, True, [tw, tf, t_u])
    W.free(i, t)
    s1, s2, s3 = T8[:, 4, :], T8[:, 5, :], T8[:, 6, :]
    t = P.ts(s1, ps[:, 0:256], dtb, None, ALU.add, after=[t, t_c])
    B.free(b, t)
    t = P.act(s2, s1, ACT.Abs, after=[t])
    t = P.act(s2, s2, ACT.Exp, after=[t], scale=-1.0)
    t = P.act(s3, s2, ACT.Ln, scale=1.0, bias=1.0)
    t_dt = P.stt(dtT[:, :], s1, 0.0, s3, ALU.max, ALU.add, after=[t])
    t = P.act(small[:, 3:4], alog, ACT.Exp, after=[t_c])
    t = P.ts(s1, dtT[:, :], small[:, 3:4], -1.0, ALU.mult, ALU.mult, after=[t])
    for c in range(2):
        t_ac = P.put("dve", lambda e, c=c: e.tensor_tensor_scan(
            acT[:, 128 * c:128 * c + 128], ones[:, 0:128], s1[:, 128 * c:128 * c + 128], 0.0, ALU.mult, ALU.add), [t_ones])
    dest = [(qa, 0), (qa, 1), (qa, 2), (ckv, 0), (ckv, 1)]

    def ev_lora(f, n, ps, t, base):
        for j in range(n):
            d, k = dest[base + j]
            t = P.copy(d[:, k, :], ps[:, j, :], after=[t])
        return t

    linear(w_in, 5152, 512, xh, xl, 8, t_u, lambda f, n, ps, t: ev_lora(f, n, ps, t, f))
    b, ps, tf = B.get()
    for j, (c, n, m) in enumerate(((5664, 128, None), (5792, 32, rep4))):
        h, l, tw, i = W.next([(0, 8, n, kp(w_in, 8)[:, :, c:c + n])], m, 1024)
        t = triple(ps[:, 256 * j:256 * j + 256], lambda k: h[:, k, :], lambda k: l[:, k, :],
                   lambda k: xh[:, k, :], lambda k: xl[:, k, :], 8, True, True, [tw, tf])
        W.free(i, t)
    t = P.copy(ckv[:, 1, :], ps[:, 0:256], after=[t])
    t_lora = P.copy(kpe[:, :], ps[:, 256:512], after=[t])
    B.free(b, t_lora)
    tap("qa", qa[:, :, :], t_lora)
    tap("kpe", kpe[:, :], t_lora)

    b, ps, tf = B.get()
    for j, src in enumerate((dtT, acT)):
        for c in range(2):
            n = 2 * j + c
            t = P.tr(ps[:, 128 * n:128 * n + 128], src[:, 128 * c:128 * c + 128], ident, after=[tf, t_dt, t_ac])
    t_dtk = P.copy(dtk[:, :, :, :], ps[:, :].rearrange("p (a c n) -> p a c n", a=2, c=2)[:, :, :, 0:32], after=[t])
    B.free(b, t_dtk)
    tap("dtT", dtT[:, :], t_dtk)
    tap("acT", acT[:, :], t_dtk)

    for j in range(2):
        t_dsk = P.copy(dsk[64 * j:64 * j + 64, :],
                       d32[64 * j:64 * j + 64, :].rearrange("p (i two) -> p two i", two=2)[:, j, :], after=[t_c])

    cs = mem["cs"]
    ang, nn, tmp = T8[:, 0, :], T8[:, 1, :], T8[:, 2, :]
    t = P.copy(tmp, posi[:, :], after=[t_c, t_u])
    t = P.ts(ang, tmp, invf, None, ALU.mult)
    TWO = 2.0 * np.pi
    C1 = 6.28125
    C2 = float(np.float32(TWO - C1))
    C2 = float(np.float32(np.round((TWO - C1) * 2 ** 20) / 2 ** 20))
    C3 = float(np.float32(TWO - C1 - C2))
    MAGIC = 12582912.0
    for i, shift in ((0, np.pi / 2), (1, 0.0)):
        P.ts(nn, ang, 1.0 / TWO, shift / TWO, ALU.mult, ALU.add)
        P.ts(nn, nn, MAGIC, MAGIC, ALU.add, ALU.subtract)
        P.stt(tmp, nn, -C1, ang, ALU.mult, ALU.add)
        P.stt(tmp, nn, -C2, tmp, ALU.mult, ALU.add)
        P.stt(tmp, nn, -C3, tmp, ALU.mult, ALU.add)
        P.ts(tmp, tmp, float(np.float32(shift)), None, ALU.add)
        P.ts(tmp, tmp, float(np.float32(3.1415925)), float(np.float32(-3.1415925)), ALU.min, ALU.max)
        t = P.copy(cs[:, i, :], tmp)
    t_cs = P.act(cs[:, :, :], cs[:, :, :], ACT.Sin, after=[t])
    tap("cs", cs[:, :, :], t_cs)

    BT, CT = R("BT", [128, 4, 256], F32, 0), R("CT", [128, 4, 256], F32, 4 * KB)
    xs = R("xs", [128, 16, 256], F32, 24 * KB)
    xdt = R("xdt", [128, 2, 2048], F32, 40 * KB)
    Btok = R("Btok", [128, 4, 128], F32, 8 * KB)
    cw, cb = col["conv_w"], col["conv_b"]
    acc = T8b

    slot = [0]
    acc_tok = [None] * 4

    late_silu = []

    def silus():
        for dst, i, x, t in late_silu:
            acc_tok[i] = P.act(dst, x, ACT.Silu, after=[t], chain=False)
        late_silu.clear()
        return list(acc_tok)

    def ev_conv(ch, n, ps, t, put):
        silus()
        tiles = []
        for j in range(n):
            c = ch + j
            i = slot[0] % 4
            slot[0] += 1
            x = acc[:, i, :]
            t1 = P.act(x, ps[:, j, :], ACT.Identity, after=[t, t_vec, acc_tok[i]], chain=j == 0,
                       scale=cw[:, 72 + c:73 + c], bias=cb[:, c:c + 1])
            tiles.append([c, i, x, t1])
        for k in range(3):
            sh = 3 - k
            for j in range(n):
                c, i, x, t1 = tiles[j]
                tiles[j][3] = P.stt(x[:, sh:256], ps[:, j, 0:256 - sh], cw[:, 24 * k + c:24 * k + c + 1], x[:, sh:256],
                                    ALU.mult, ALU.add, after=[tiles[-1][3] if k == 0 else t1], chain=False)
        toks = [x[3] for x in tiles]
        late_silu.extend((put(c), i, x, t1) for c, i, x, t1 in tiles)
        return toks

    linear(w_in, 4096, 1024, xh, xl, 8, t_u,
           lambda f, n, ps, t: ev_conv(16 + f, n, ps, t, lambda c: BT[:, c - 16, :] if c < 20 else CT[:, c - 20, :]))
    t_bc = silus()
    linear(w_in, 2048, 2048, xh, xl, 8, t_u, lambda f, n, ps, t: ev_conv(f, n, ps, t, lambda c: xs[:, c, :]))
    t_xs = silus()
    tap("BT", BT[:, :, :], t_bc)
    tap("xs", xs[:, :, :], t_xs)
    acb = R("acb", [128, 8, 256], F32, 56 * KB)
    M = R("M", [128, 2, 8, 128], F32, 64 * KB)
    CE = R("CE", [128, 8, 128], F32, 72 * KB)
    xw = R("xw", [128, 512], F32, 16 * KB)
    S0 = R("S0", [128, 512], F32, 18 * KB)
    dte = R("dte", [128, 8], F32, 23 * KB)
    CB = R("CB", [128, 2, 128], F32, 20 * KB)
    below = R("below", [128, 128], F32, 23 * KB + 512)
    nac = R("nac", [128, 2, 32], F32, 23 * KB + 64)
    P.ts(nac[:, :, :], dtk[:, 1, :, :], -1.0, None, ALU.mult, after=[t_dtk])
    P.ts(below[:, :], n_sl, 0.0, None, ALU.is_equal, after=[t_c])
    def gate_y(g):
        sz = (T8, T8b)[g][:, :, :]
        t = P.act(sz, sz, ACT.Silu, after=[t_sz[0]])
        return P.tt(xs[:, 8 * g:8 * g + 8, :], xs[:, 8 * g:8 * g + 8, :], sz, ALU.mult, after=[t, t_ys[0]])

    def ssd_steps():
        t_y = t_pe = None
        b, ps, tf = B.get()
        for g in range(4):
            t = P.tr(ps[:, 128 * g:128 * g + 128], BT[:, g, 0:128], ident, after=[t_bc, tf])
        t_btok = P.copy(Btok[:, :, :], ps[:, :].rearrange("p (a n) -> p a n", a=4), after=[t])
        B.free(b, t_btok)
        for c in range(2):
            for g in range(4):
                b, ps, tf = B.get()
                for j in range(4):
                    t = P.tr(ps[:, 128 * j:128 * j + 128], xs[:, 4 * g + j, 128 * c:128 * c + 128], ident, after=[t_xs, tf])
                t_xdt = P.tt(xdt[:, c, 512 * g:512 * g + 512].rearrange("p (h d) -> p h d", d=64),
                             ps[:, :].rearrange("p (h d) -> p h d", d=64),
                             dtk[:, 0, c, 8 * g:8 * g + 8].unsqueeze(2).broadcast_to([128, 8, 64]), ALU.mult, after=[t, t_dtk])
                B.free(b, t_xdt)
        yield
        for g in range(4):
            for q in range(4):
                b, ps, tf = B.get()
                for j in range(2):
                    hd = 8 * g + 2 * q + j
                    t = P.mm(ps[:, 256 * j:256 * j + 256], ident[0:32, hd:hd + 1].broadcast_to([32, 128]), acT[0:32, :],
                             after=[t_ac, tf])
                t_acb = P.act(acb[:, 2 * q:2 * q + 2, :], ps[:, :].rearrange("p (a n) -> p a n", a=2), ACT.Copy,
                              after=[t, t_y])
                B.free(b, t_acb)
            b, ps, tf = B.get()
            for c in range(2):
                t = P.mm(ps[:, 128 * c:128 * c + 128], BT[:, g, 128 * c:128 * c + 128], CT[:, g, 128 * c:128 * c + 128],
                         after=[t_bc, tf])
            t_cb = P.tt(CB[:, :, :], ps[:, 0:256].rearrange("p (c n) -> p c n", c=2),
                        below[:, :].unsqueeze(1).broadcast_to([128, 2, 128]), ALU.mult, after=[t])
            B.free(b, t_cb)
            t = P.tt(dte[:, :], acb[:, :, 127], dtk[:, 1, 0, 8 * g:8 * g + 8], ALU.subtract, after=[t_acb, t_dtk])
            t_dte = P.act(dte[:, :], dte[:, :], ACT.Exp, after=[t])
            t_ce = P.act(CE[:, :, :], acb[:, :, 128:256], ACT.Exp, after=[t_pe])
            t_xw = P.tt(xw[:, :].rearrange("p (h d) -> p h d", d=64),
                        xdt[:, 0, 512 * g:512 * g + 512].rearrange("p (h d) -> p h d", d=64),
                        dte[:, :].unsqueeze(2).broadcast_to([128, 8, 64]), ALU.mult, after=[t_dte, t_pe])
            t_e = [None, None]
            for hl in range(8):
                t_e[0] = P.ts(M[:, 0, hl, :], acb[:, hl, 0:128], dtk[:, 1, 0, 8 * g + hl:8 * g + hl + 1], 0.0,
                              ALU.subtract, ALU.min, after=[t_acb, t_pe])
                t_e[1] = P.act(M[:, 1, hl, :], acb[:, hl, 128:256], ACT.Abs, after=[t_pe],
                               bias=nac[:, 1, 8 * g + hl:8 * g + hl + 1])
            for c in range(2):
                t_e[c] = P.act(M[:, c, :, :], M[:, c, :, :], ACT.Exp, after=[t_e[c]], scale=1.0 - 2.0 * c)
            for c in range(2):
                t_m = P.tt(M[:, c, :, :], M[:, c, :, :], CB[:, c, :].unsqueeze(1).broadcast_to([128, 8, 128]),
                           ALU.mult, after=[t_e[c]])
            t_ce = P.tt(CE[:, :, :], CE[:, :, :], CT[:, g, 128:256].unsqueeze(1).broadcast_to([128, 8, 128]), ALU.mult,
                        after=[t_ce, t_bc])
            yield
            if g == 3:
                gate_y(0)
            yield
            b, ps, tf = B.get()
            t = P.mm(ps[:, :], Btok[:, g, :], xw[:, :], after=[t_xw, t_btok, tf])
            t_s0 = P.copy(S0[:, :], ps[:, :], after=[t, t_pe])
            B.free(b, t_s0)
            for q in range(4):
                b, ps, tf = B.get()
                for j in range(2):
                    hl = 2 * q + j
                    hd = 8 * g + hl
                    o = 64 * j
                    P.mm(ps[o:o + 64, 0:128], xdt[:, 0, 64 * hd:64 * hd + 64], M[:, 0, hl, :], after=[t_m, t_xdt, tf])
                    P.mm(ps[o:o + 64, 128:256], xdt[:, 1, 64 * hd:64 * hd + 64], M[:, 1, hl, :], True, False)
                    t_pe = P.mm(ps[o:o + 64, 128:256], S0[:, 64 * hl:64 * hl + 64], CE[:, hl, :], False, True,
                                after=[t_s0, t_ce])
                i = 4 * g + q
                t_y = P.stt(xs[:, i, :], xs[:, i, :], dsk[:, i:i + 1], ps[:, 0:256], ALU.mult, ALU.add, after=[t_pe, t_dsk])
                B.free(b, t_y)
            t_ys[0] = t_y

    t_sz = [None]

    def ev_z(f, n, ps, t):
        t_sz[0] = P.act((T8, T8b)[f // 8][:, f % 8:f % 8 + n, :], ps, ACT.Copy, after=[t, last_acc])
        return t_sz[0]

    t_ys = [None]
    last_acc = P.last()
    side.append(ssd_steps())
    linear(w_in, 0, 2048, xh, xl, 8, t_u, ev_z)
    finish()
    YAh, YAl = R("YAh", [128, 16, 256], F32R, 40 * KB), R("YAl", [128, 16, 256], F32R, 56 * KB)
    t_ya = Ready()

    def ya_steps():
        t = gate_y(1)
        for g in range(0, 16, 8):
            yield from norm_split_steps(t_ya, xs[:, g:g + 8, :], 4, 512, col["ssd_norm"][:, g:g + 8],
                                        YAh[:, g:g + 8, :], YAl[:, g:g + 8, :], [t], 2)

    side.append(ya_steps())
    advance()
    G = R("G", [128, 8, 256], F32, 0)
    t_g = [None]

    def ev_gate(f, n, ps, t):
        t_g[0] = P.act(G[:, f:f + n, :], ps, ACT.Copy, after=[t, t_ys[0]])
        return t_g[0]

    linear(w_in, 5824, 1024, xh, xl, 8, t_u, ev_gate)

    def ev_ssd(f, n, ps, t):
        t_g[0] = P.tt(G[:, f:f + n, :], G[:, f:f + n, :], ps, ALU.mult, after=[t, t_g0])
        return t_g[0]

    finish()
    t_g0 = P.act(G[:, :, :], G[:, :, :], ACT.Sigmoid)
    XCh, XCl = R("XCh", [128, 5, 256], F32R, 16 * KB), R("XCl", [128, 5, 256], F32R, 21 * KB)
    t1, t_xc = Ready(), Ready()
    side.append(norm_split_steps(t1, qa, 3, 384, col["q_a_norm"], XCh[:, 0:3, :], XCl[:, 0:3, :], [t_lora, P.last()]))
    side.append(norm_split_steps(t_xc, ckv, 2, 256, col["kv_a_norm"], XCh[:, 3:5, :], XCl[:, 3:5, :], [t_lora]))
    linear(I["w_ssd_out"][0], 0, 1024, YAh, YAl, 16, t_ya, ev_ssd, k_cols=128)
    tap("G", G[:, :, :], t_g[0])
    finish()
    t_gs = t_g[0]

    qn, qp = R("qn", [128, 8, 256], F32, 26 * KB), R("qp", [128, 4, 256], F32, 34 * KB)
    kn, V = (R("kn", [128, 8, 256], F32, 38 * KB), T8b), R("V", [128, 2, 1024], F32, 46 * KB)
    kpm = R("kpm", [128, 4, 256], F32, 10 * KB)
    P.put("pool", lambda e: e.memset(kn[0][64:128, :, :], 0.0), [t_xc, P.last()])
    P.put("pool", lambda e: e.memset(kn[1][0:64, :, :], 0.0), [t_xc])
    t_zero = P.put("pool", lambda e: e.memset(kpm[:, :, :], 0.0), [t_xc])
    wq, wkv = I["w_q_b"][0], I["w_kv_b"][0]
    qmap = [(lambda x: x[:, 0:768].rearrange("p (k h d) -> p k h d", k=3, h=4),
             lambda x: x[:, 0:1152].rearrange("p (k h d) -> p k h d", k=3, h=4)[:, :, :, 0:64]),
            (lambda x: x[:, 768:1152].rearrange("p (k h d) -> p k h d", k=3, h=4),
             lambda x: x[:, 0:1152].rearrange("p (k h d) -> p k h d", k=3, h=4)[:, :, :, 64:96])]
    for q in range(4):
        h, l, tw, i = W.next([(0, 3, 384, kp(wq, 3)[:, :, 384 * q:384 * q + 384])], qmap)
        h, l = (x.rearrange("p a b -> p (a b)") for x in (h, l))

        b, ps, tf = B.get()
        for j in range(2):
            t = triple(ps[:, 256 * j:256 * j + 256], lambda k: h[:, 256 * k + 128 * j:256 * k + 128 * j + 128], lambda k: l[:, 256 * k + 128 * j:256 * k + 128 * j + 128],
                       lambda k: XCh[:, k, :], lambda k: XCl[:, k, :], 3, True, True, [tw, tf, t1])
        t2 = P.act(qn[:, 2 * q:2 * q + 2, :], ps[:, :].rearrange("p (a n) -> p a n", a=2), ACT.Copy, after=[t])
        B.free(b, t2)
        b, ps, tf = B.get()
        t = triple(ps[:, 0:256], lambda k: h[:, 768 + 128 * k:896 + 128 * k], lambda k: l[:, 768 + 128 * k:896 + 128 * k],
                   lambda k: XCh[:, k, :], lambda k: XCl[:, k, :], 3, True, True, [tf])
        W.free(i, t)
        t_q = P.act(qp[:, q, :], ps[:, 0:256], ACT.Copy, after=[t])
        B.free(b, t_q)
    toks = []
    for q in range(5):
        src = qp[:, q, :] if q < 4 else kpe[:, :]
        b, ps, tf = B.get()
        t = P.mm(ps[:, 0:256], perm, src, after=[t_q, t_lora, tf, t_c])
        t = P.tt(T8[:, q, :], ps[:, 0:256], cs[:, 1, :], ALU.mult, after=[t, t_cs], chain=q == 0)
        B.free(b, t)
    cos4 = cs[:, 0, :].unsqueeze(1).broadcast_to([128, 4, 256])
    P.tt(qp[:, :, :], qp[:, :, :], cos4, ALU.mult)
    P.tt(kpe[:, :], kpe[:, :], cs[:, 0, :], ALU.mult, chain=False)
    P.tt(qp[:, :, :], qp[:, :, :], T8[:, 0:4, :], ALU.add)
    P.tt(kpe[:, :], kpe[:, :], T8[:, 4, :], ALU.add, chain=False)
    kvmap = [(lambda x, k=k: x[:, 1024 * k:1024 * k + 1024].rearrange("p (t h d) -> p t h d", t=2, h=8),
              lambda x, k=k: x[:, 1024 * k:1024 * k + 1024].rearrange("p (h t d) -> p t h d", t=2, h=8)) for k in range(2)]
    for q in range(2):
        h, l, tw, i = W.next([(0, 2, 1024, kp(wkv, 2)[:, :, 1024 * q:1024 * q + 1024])], kvmap)

        for r in range(2):
            b, ps, tf = B.get()
            for j in range(2):
                a = 4 * r + 2 * j
                t = triple(ps[:, 256 * j:256 * j + 256], lambda k: h[:, k, 64 * a:64 * a + 128], lambda k: l[:, k, 64 * a:64 * a + 128],
                           lambda k: XCh[:, 3 + k, :], lambda k: XCl[:, 3 + k, :], 2, True, True, [tw, tf, t_xc])
            for o in range(2):
                p = slice(64 * o, 64 * o + 64)
                t_kn = P.act(kn[o][p, 4 * q + 2 * r:4 * q + 2 * r + 2, :], ps[p, :].rearrange("p (a n) -> p a n", a=2),
                             ACT.Copy, after=[t])
            B.free(b, t_kn)
        for j in range(2):
            b, ps, tf = B.get()
            t = triple(ps[:, :], lambda k: XCh[:, 3 + k, 128 * j:128 * j + 128], lambda k: XCl[:, 3 + k, 128 * j:128 * j + 128],
                       lambda k: h[:, k, 512:1024], lambda k: l[:, k, 512:1024], 2, True, True, [tf])
            t_v = P.act(V[:, j, 512 * q:512 * q + 512], ps[:, :], ACT.Copy, after=[t])
            B.free(b, t_v)
        W.free(i, t)
    t_r = P.last()
    for hl in range(4):
        p = slice(32 * hl, 32 * hl + 32)
        t_r = P.copy(kpm[p, hl, :], kpe[p, :], after=[t_zero])
    tap("qn", qn[:, :, :], t_r)
    tap("qp", qp[:, :, :], t_r)
    tap("kpr", kpe[:, :], t_r)
    tap("V", V[:, :, :], [t_r, t_v])
    Pm0, Pm1 = R("Pm0", [128, 4, 128], F32, 54 * KB), R("Pm1", [128, 4, 256], F32, 56 * KB)
    PT0, PT1 = R("PT0", [128, 4, 256], F32, 60 * KB), R("PT1", [128, 4, 128], F32, 64 * KB)
    OAh, OAl = R("OAh", [128, 8, 256], F32R, 66 * KB), R("OAl", [128, 8, 256], F32R, 16 * KB)
    sm = mem["sm"]
    SC = 96.0 ** -0.5
    t_oa = Ready()
    nqk4 = n_qk.unsqueeze(1).broadcast_to([128, 4, 128])

    def mla_scores(g):
        b0, bs = B.get(), [B.get() for _ in range(2)]
        for hl in range(4):
            hd = 4 * g + hl
            qN, kN = qn[:, hd // 2, :], kn[hd % 2][:, hd // 2, :]
            qP, kP = qp[:, g, :], kpm[:, hl, :]
            d0 = b0[1][:, 128 * hl:128 * hl + 128]
            P.mm(d0, qN[:, 0:128], kN[:, 0:128], True, False, after=[t_r, t_kn, t_zero, b0[2]])
            t0 = P.mm(d0, qP[:, 0:128], kP[:, 0:128], False, True)
            d1 = bs[hl // 2][1][:, 256 * (hl % 2):256 * (hl % 2) + 256]
            P.mm(d1, qN[:, 128:256], kN[:, :], True, False, after=[bs[hl // 2][2]])
            t1 = P.mm(d1, qP[:, 128:256], kP[:, :], False, True)
        return b0, bs, t0, t1

    def mla_soft(b0, bs, t0, t1, t_ptr):
        ta = P.stt(Pm0[:, :, :], b0[1][:, :].rearrange("p (a n) -> p a n", a=4), SC, nqk4, ALU.mult, ALU.add, after=[t0, t_ptr])
        B.free(b0[0], ta)
        for j in range(2):
            bb, pp, _ = bs[j]
            v = pp[:, :].rearrange("p (a n) -> p a n", a=2)
            P.ts(Pm1[:, 2 * j:2 * j + 2, 0:128], v[:, :, 0:128], SC, None, ALU.mult, after=[t1, t_ptr])
            ta = P.stt(Pm1[:, 2 * j:2 * j + 2, 128:256], v[:, :, 128:256], SC,
                       n_qk.unsqueeze(1).broadcast_to([128, 2, 128]), ALU.mult, ALU.add, chain=False)
            B.free(bb, [ta])
        P.red(sm[:, 0:4], Pm0[:, :, :], ALU.max)
        P.red(sm[:, 4:8], Pm1[:, :, :], ALU.max)
        t = P.ts(sm[:, 8:16], sm[:, 0:8], -1.0, None, ALU.mult)
        for hl in range(4):
            P.act(Pm0[:, hl, :], Pm0[:, hl, :], ACT.Exp, after=[t], chain=hl == 0, bias=sm[:, 8 + hl:9 + hl],
                  accum_out=sm[:, 16 + hl:17 + hl])
            t2 = P.act(Pm1[:, hl, :], Pm1[:, hl, :], ACT.Exp, chain=False, bias=sm[:, 12 + hl:13 + hl],
                       accum_out=sm[:, 20 + hl:21 + hl])
        P.put("dve", lambda e: e.reciprocal(sm[:, 24:32], sm[:, 16:24]), [t2])
        P.tt(Pm0[:, :, :], Pm0[:, :, :], sm[:, 24:28].unsqueeze(2).broadcast_to([128, 4, 128]), ALU.mult)
        return P.tt(Pm1[:, :, :], Pm1[:, :, :], sm[:, 28:32].unsqueeze(2).broadcast_to([128, 4, 256]), ALU.mult, chain=False)

    def mla_steps():
        t_pv = None
        t = mla_soft(*mla_scores(0), None)
        for g in range(4):
            yield
            bt = [B.get() for _ in range(3)]
            for hl in range(4):
                d = bt[hl // 2][1][:, 256 * (hl % 2):256 * (hl % 2) + 256]
                P.tr(d[:, 0:128], Pm0[:, hl, :], ident, after=[t, bt[hl // 2][2]])
                P.tr(d[:, 128:256], Pm1[:, hl, 0:128], ident)
                t_ptr = P.tr(bt[2][1][:, 128 * hl:128 * hl + 128], Pm1[:, hl, 128:256], ident, after=[bt[2][2]])
            if g < 3:
                sc = mla_scores(g + 1)
            t_p = []
            for j in range(2):
                t_p.append(P.act(PT0[:, 2 * j:2 * j + 2, :], bt[j][1][:, :].rearrange("p (a n) -> p a n", a=2), ACT.Copy,
                                 after=[t_ptr, t_pv], chain=j == 0))
                B.free(bt[j][0], t_p[-1])
            t_p.append(P.act(PT1[:, :, :], bt[2][1][:, :].rearrange("p (a n) -> p a n", a=4), ACT.Copy, chain=False))
            B.free(bt[2][0], t_p[-1])
            if g < 3:
                t = mla_soft(*sc, t_ptr)
            b, ps, tf = B.get()
            for j in range(2):
                for r in range(2):
                    hl = 2 * j + r
                    hd = 4 * g + hl
                    o = 64 * r
                    P.mm(ps[o:o + 64, 256 * j:256 * j + 256], V[:, 0, 64 * hd:64 * hd + 64], PT0[:, hl, :], True, False, after=[t_p, t_v, tf])
                    t_pv = P.mm(ps[o:o + 64, 256 * j + 128:256 * j + 256], V[:, 1, 64 * hd:64 * hd + 64], PT1[:, hl, :], False, True)
            t_oa.extend(2 * [split(OAh[:, 2 * g:2 * g + 2, :], OAl[:, 2 * g:2 * g + 2, :], ps[:, :].rearrange("p (a n) -> p a n", a=2), [t_pv])])
            B.free(b, t_oa[-1])

    G2 = T8
    t_rope = t_r

    def ev_gate2(f, n, ps, t):
        t_g[0] = P.act(G2[:, f:f + n, :], ps, ACT.Copy, after=[t, t_rope])
        return t_g[0]

    side.append(mla_steps())
    advance()
    linear(w_in, 6848, 1024, xh, xl, 8, t_u, ev_gate2)
    finish()
    t_g0 = P.act(G2[:, :, :], G2[:, :, :], ACT.Sigmoid)
    MXh, MXl = R("MXh", [128, 8, 256], F32R, 34 * KB), R("MXl", [128, 8, 256], F32R, 42 * KB)

    def ev_mla(f, n, ps, t):
        t = P.tt(G2[:, f:f + n, :], G2[:, f:f + n, :], ps, ALU.mult, after=[t, t_g0])
        t2 = P.tt(G[:, f:f + n, :], G[:, f:f + n, :], G2[:, f:f + n, :], ALU.add, after=[t_gs])
        t_mx.extend([split(MXh[:, f:f + n, :], MXl[:, f:f + n, :], G[:, f:f + n, :], [t2])] * n)
        return t

    t_mx = Ready()
    linear(I["w_mla_out"][0], 0, 1024, OAh, OAl, 8, t_oa, ev_mla)

    def ev_res(f, n, ps, t):
        t_g[0] = P.tt(H[:, f:f + n, :], H[:, f:f + n, :], ps, ALU.add, after=[t])
        return t_g[0]

    memin, memT = R("memin", [128, 2, 1024], F32, 0), R("memT", [128, 8, 256], F32, 8 * KB)
    MMh, MMl = R("MMh", [128, 8, 256], F32R, 16 * KB), R("MMl", [128, 8, 256], F32R, 24 * KB)
    t_mem = P.dma(memin[:, :, :], I["mem"][0].rearrange("(t p) d -> p t d", p=128), "mem", after=P.last())
    t_mm = Ready()

    def mem_steps():
        for d0 in range(0, 8, 2):
            b, ps, tf = B.get()
            for j in range(4):
                t = P.tr(ps[:, 128 * j:128 * j + 128], memin[:, j % 2, (d0 + j // 2) * 128:(d0 + j // 2 + 1) * 128],
                         ident, after=[t_mem, tf])
            t = P.act(memT[:, d0:d0 + 2, :], ps[:, :].rearrange("p (a n) -> p a n", a=2), ACT.Copy, after=[t])
            B.free(b, t)
        yield from norm_split_steps(t_mm, memT, 8, 1024, col["norm_mem"], MMh[:, :, :], MMl[:, :, :], [t])

    side.append(mem_steps())
    linear(I["w_o"][0], 0, 1024, MXh, MXl, 8, t_mx, ev_res)
    t_h = t_g[0]
    finish()
    tap("h1", H[:, :, :], t_h)

    XVh, XVl = R("XVh", [128, 8, 256], F32R, 32 * KB), R("XVl", [128, 8, 256], F32R, 40 * KB)
    t_xv = Ready()
    side.append(norm_split_steps(t_xv, H, 8, 1024, col["norm_xattn"], XVh[:, :, :], XVl[:, :, :], [t_h]))
    advance()
    q2, k2 = R("q2", [128, 8, 256], F32, 48 * KB), R("k2", [128, 8, 256], F32, 56 * KB)
    v2 = R("v2", [128, 2, 1024], F32, 64 * KB)

    def ev_to(dst):
        def ev(f, n, ps, t):
            t_g[0] = P.act(dst[:, f:f + n, :], ps, ACT.Copy, after=[t])
            return t_g[0]
        return ev

    def ev_tok(dst):
        def ev(c, ps, t):
            t_g[0] = P.act(dst[:, :, c:c + 256], ps, ACT.Copy, after=[t])
            return t_g[0]
        return ev

    linear(I["w_xkv"][0], 0, 1024, MMh, MMl, 8, t_mm, ev_to(k2))
    finish()
    linear(I["w_xq"][0], 0, 1024, XVh, XVl, 8, t_xv, ev_to(q2))
    t_qk = t_g[0]
    Px = [R(f"Px{j}", [128, 4, 256], F32, (32 + 4 * j) * KB) for j in range(2)]
    PXT = [R(f"PXT{j}", [128, 4, 256], F32, (40 + 4 * j) * KB) for j in range(2)]
    OXh, OXl = R("OXh", [128, 8, 256], F32R, 0), R("OXl", [128, 8, 256], F32R, 8 * KB)
    toks = []
    for j in range(2):
        bs = [B.get() for _ in range(2)]
        for hd in range(4):
            d = bs[hd // 2][1][:, 256 * (hd % 2):256 * (hd % 2) + 256]
            for e in range(2):
                t = P.mm(d, q2[:, 2 * hd + e, 128 * j:128 * j + 128], k2[:, 2 * hd + e, :], e == 0, e == 1, after=[t_qk, bs[hd // 2][2]])
        for r in range(2):
            t2 = P.ts(Px[j][:, 2 * r:2 * r + 2, :], bs[r][1][:, :].rearrange("p (a n) -> p a n", a=2), 1.0 / 16, None, ALU.mult, after=[t])
            B.free(bs[r][0], t2)
        sj = sm[:, 64 * j:64 * j + 64]
        P.red(sj[:, 0:4], Px[j][:, :, :], ALU.max)
        t = P.ts(sj[:, 8:12], sj[:, 0:4], -1.0, None, ALU.mult)
        for hd in range(4):
            t2 = P.act(Px[j][:, hd, :], Px[j][:, hd, :], ACT.Exp, after=[t], bias=sj[:, 8 + hd:9 + hd], accum_out=sj[:, 16 + hd:17 + hd])
        P.put("dve", lambda e, sj=sj: e.reciprocal(sj[:, 24:28], sj[:, 16:20]), [t2])
        toks.append(P.tt(Px[j][:, :, :], Px[j][:, :, :], sj[:, 24:28].unsqueeze(2).broadcast_to([128, 4, 256]), ALU.mult))
    t_ox = Ready()
    linear_tok(I["w_xkv"][0], 1024, 1024, MMh, MMl, 8, t_mm, ev_tok(v2))
    t_v2 = t_g[0]
    for mj in range(2):
        for r in range(2):
            b, ps, tf = B.get()
            for a in range(2):
                for j in range(2):
                    t = P.tr(ps[:, 256 * a + 128 * j:256 * a + 128 * j + 128], Px[j][:, 2 * r + a, 128 * mj:128 * mj + 128], ident, after=[toks, tf])
            t_px = P.act(PXT[mj][:, 2 * r:2 * r + 2, :], ps[:, :].rearrange("p (a n) -> p a n", a=2), ACT.Copy, after=[t])
            B.free(b, t_px)
    for hd in range(4):
        b, ps, tf = B.get()
        for e in range(2):
            for mj in range(2):
                t = P.mm(ps[:, 256 * e:256 * e + 256], v2[:, mj, 256 * hd + 128 * e:256 * hd + 128 * e + 128],
                         PXT[mj][:, hd, :], mj == 0, mj == 1, after=[t_px, t_v2, tf])
        t_ox += 2 * [split(OXh[:, 2 * hd:2 * hd + 2, :], OXl[:, 2 * hd:2 * hd + 2, :], ps[:, :].rearrange("p (a n) -> p a n", a=2), [t])]
        B.free(b, t_ox[-1])
    wr = R("wr", [128, 8, 36], F32, 46 * KB)
    for c, n, name in ((0, 4, "w_router_group"), (4, 32, "w_router_expert")):
        t_wr = P.dma(wr[:, :, c:c + n], kp(I[name][0], 8), "router", after=P.last())
    linear(I["w_xo"][0], 0, 1024, OXh, OXl, 8, t_ox, ev_res)
    t_h = t_g[0]
    tap("h2", H[:, :, :], t_h)

    t_xt, t_x8 = Ready(), []
    norm8 = norm(H, 8, 1024, col["norm_moe"], T8b, [t_h])
    for k0, k1, t in norm8:
        t_x8.append(t)
    CBt = R("CBt", [128, 32, 256], F32, 0)
    lg = R("lg", [128, 2, 40], F32, 32 * KB)
    rt = R("rt", [128, 256], F32, 31 * KB)
    comb = R("comb", [128, 2, 128], F32, 33 * KB)
    combT = R("combT", [128, 256], F32, 34 * KB)
    b, ps, tf = B.get()
    for j in range(2):
        for k in range(8):
            t = P.mm(ps[:, 64 * j:64 * j + 36], T8b[:, k, 128 * j:128 * j + 128], wr[:, k, :], k == 0, k == 7, after=[t_wr, tf, t_x8])
    t = P.tt(lg[:, :, 0:36], ps[:, 0:128].rearrange("p (a n) -> p a n", a=2)[:, :, 0:36],
             brt[:, 0:36].unsqueeze(1).broadcast_to([128, 2, 36]), ALU.add, after=[t, t_c])
    B.free(b, t)
    tap("lg", lg[:, :, 0:36], t)

    def first_of(dst, v, mx, n, s):
        P.tt(dst, v, mx.unsqueeze(2).broadcast_to([128, 2, n]), ALU.is_equal)
        P.ts(s, dst, -1000.0, 1000.0, ALU.mult, ALU.add)
        P.tt(s, s, iota[:, 0:n].unsqueeze(1).broadcast_to([128, 2, n]), ALU.add)
        P.red(rt[:, 254:256], s, ALU.min)
        return P.tt(dst, iota[:, 0:n].unsqueeze(1).broadcast_to([128, 2, n]),
                    rt[:, 254:256].unsqueeze(2).broadcast_to([128, 2, n]), ALU.is_equal)

    slots = R("slots", [128, 272], F32, 38 * KB)
    flag = mem["flag"]
    posrow = R("posrow", [128, 2, 256], F32, 36 * KB)
    ohs = R("ohs", [128, 2, 2, 32], F32, 40 * KB)
    sel = R("sel", [128, 2, 32], F32, 41 * KB)
    strict = R("strict", [128, 128], F32, 42 * KB)
    rk = R("rk", [128, 2, 64], F32, 43 * KB)
    t_slots = P.dma(slots[:, :], I["c_slots"], "slots", after=P.last())
    P.put("dve", lambda e: e.memset(comb[:, :, :], 0.0), None)
    P.tt(strict[:, :], ones[:, :], tri, ALU.subtract)
    XTh, XTl = R("XTh", [128, 2, 1024], F32R, 0), R("XTl", [128, 2, 1024], F32R, 8 * KB)
    turned_x = []
    for j in range(2):
        for q in range(2):
            b, ps, tf = B.get()
            for r in range(4):
                t = P.tr(ps[:, 128 * r:128 * r + 128], T8b[:, 4 * q + r, 128 * j:128 * j + 128], ident, after=[tf, t_xt])
            c = slice(512 * q, 512 * q + 512)
            t = P.act(XTh[:, j, c], ps[:, :], ACT.Copy, after=[t])
            turned_x.append((b, XTl[:, j, c], ps[:, :], XTh[:, j, c], t))

    def pair(i):
        return rt[:, 2 * i:2 * i + 2]

    def eight(i):
        return rt[:, 16 * i:16 * i + 16].rearrange("p (j n) -> p j n", j=2)

    def wide(x, n):
        return x.unsqueeze(2).broadcast_to([128, 2, n])

    gl, el = lg[:, :, 0:4], lg[:, :, 4:36]
    gm, gs, gw, m1, m2, dl, w1, w2 = (pair(i) for i in range(8))
    og, s4, e4 = (rt[:, 16 + 8 * i:24 + 8 * i].rearrange("p (j n) -> p j n", j=2) for i in range(3))
    ein, o1, o2, s8, ea = (eight(i) for i in range(3, 8))
    big = rt[:, 128:192].rearrange("p (j g e) -> p j g e", j=2, g=4)
    P.red(gm, gl, ALU.max)
    t = P.tt(e4, gl, wide(gm, 4), ALU.subtract)
    t_e = P.act(e4, e4, ACT.Exp, after=[t])
    first_of(og, gl, gm, 4, s4)
    P.tt(big, el.rearrange("p j (g e) -> p j g e", g=4), og.unsqueeze(3).broadcast_to([128, 2, 4, 8]), ALU.mult)
    P.red(ein, big.rearrange("p j g e -> p j e g"), ALU.add)
    P.red(m1, ein, ALU.max)
    first_of(o1, ein, m1, 8, s8)
    P.stt(ea, o1, -3.0e38, ein, ALU.mult, ALU.add)
    P.red(m2, ea, ALU.max)
    first_of(o2, ea, m2, 8, s8)
    t = P.tt(dl, m2, m1, ALU.subtract)
    t_w = P.act(w2, dl, ACT.Exp, after=[t])
    for k, o in enumerate((o1, o2)):
        P.tt(ohs[:, :, k, :].rearrange("p j (g e) -> p j g e", g=4), o.unsqueeze(2).broadcast_to([128, 2, 4, 8]),
             og.unsqueeze(3).broadcast_to([128, 2, 4, 8]), ALU.mult)
    t_sel = P.tt(sel[:, :, :], ohs[:, :, 0, :], ohs[:, :, 1, :], ALU.add)
    P.red(gs, e4, ALU.add, after=[t_e])
    P.put("dve", lambda e: e.reciprocal(gw, gs), None)
    P.ts(m1, w2, 1.0, None, ALU.add, after=[t_w])
    P.put("dve", lambda e: e.reciprocal(w1, m1), None)
    P.tt(w1, w1, gw, ALU.mult)
    P.tt(w2, w2, w1, ALU.mult)
    P.tt(comb[:, :, 0:32], ohs[:, :, 0, :], wide(w1, 32), ALU.mult)
    P.tt(rk[:, :, 32:64], ohs[:, :, 1, :], wide(w2, 32), ALU.mult)
    P.tt(comb[:, :, 0:32], comb[:, :, 0:32], rk[:, :, 32:64], ALU.add)
    for k0, k1, t in norm8:
        P.act(XUh[:, k0:k1, :], T8b[:, k0:k1, :], ACT.Copy, after=[t])
    b, ps, tf = B.get()
    P.mm(ps[:, 0:32], strict[:, :], sel[:, 0, :], after=[t_sel, tf])
    P.mm(ps[:, 32:64], ones[:, :], sel[:, 0, :], True, False)
    P.mm(ps[:, 32:64], strict[:, :], sel[:, 1, :], False, True)
    P.mm(ps[:, 64:96], ones[:, :], sel[:, 0, :], True, False)
    t = P.mm(ps[:, 64:96], ones[:, :], sel[:, 1, :], False, True)
    P.stt(rk[:, :, 0:32], iota.unsqueeze(1).broadcast_to([128, 2, 32]), 64.0, ps[:, 0:64].rearrange("p (j n) -> p j n", j=2),
          ALU.mult, ALU.add, after=[t])
    P.red(rt[:, 253:254], ps[:, 64:96], ALU.max)
    B.free(b, P.copy(flag[:, 0:1], rt[:, 253:254]))
    for k in range(2):
        P.tt(rk[:, :, 32:64], ohs[:, :, k, :], rk[:, :, 0:32], ALU.mult)
        t = P.red(comb[:, :, 32 + k:33 + k], rk[:, :, 32:64], ALU.add)
    pg = R("pgrp", [128, 8, 2, 2], F32, 30 * KB)
    P.ts(rk[:, 0, 0:8], iota[:, 0:8], -256.0, None, ALU.mult)
    P.tt(pg[:, :, :, :], comb[:, :, 32:34].unsqueeze(1).broadcast_to([128, 8, 2, 2]),
         rk[:, 0, 0:8].unsqueeze(2).unsqueeze(3).broadcast_to([128, 8, 2, 2]), ALU.add)
    for b, l, ps, h, tx in turned_x:
        B.free(b, P.tt(l, ps, h.bitcast(F32), ALU.subtract, after=[tx], chain=False))
    for k0, k1, tx in norm8:
        P.tt(XUl[:, k0:k1, :], T8b[:, k0:k1, :], XUh[:, k0:k1, :].bitcast(F32), ALU.subtract, after=P.last(), chain=False)
    b, ps, tf = B.get()
    for j in range(2):
        t2 = P.tr(ps[:, 128 * j:128 * j + 128], comb[:, j, :], ident, after=[t, tf])
    t = P.act(combT[:, :], ps[:, 0:256], ACT.Copy, after=[t2])
    B.free(b, t)
    tap("combT", combT[0:32, :], t)
    b, ps, tf = B.get()
    for k in range(2):
        t2 = P.mm(ps[:, 256 * k:256 * k + 256], ident[0:64, 32 + k:33 + k].broadcast_to([64, 128]), combT[0:64, :], after=[t, tf])
    t = P.act(posrow[:, :, :], ps[:, :].rearrange("p (a n) -> p a n", a=2), ACT.Copy, after=[t2])
    B.free(b, t)

    def gated(pfx, steps, xh, xl, ready, group):
        nb = 2 * group
        hs = [R(f"{pfx}hs{j}", [128, 2, 256], F32, (40 + 2 * j) * KB) for j in range(nb)]
        ah = [R(f"{pfx}ah{j}", [128, 2, 256], F32R, (40 + 2 * (nb + j)) * KB) for j in range(nb)]
        al = [R(f"{pfx}al{j}", [128, 2, 256], F32R, (40 + 2 * (2 * nb + j)) * KB) for j in range(nb)]
        ybanks = [B.banks[4 + j] for j in range(4)]
        yfree = flat([B.tok[4 + j] for j in range(4)])
        n = len(steps)
        used = [None] * nb

        def up(e):
            g, u, _, scale, ts = steps[e]
            res = []
            for w in (g, u):
                h, l, tw, i = W.next([(0, 8, 256, kp(w, 8))])
                b, ps, tf = B.get(range(4))
                for j in range(2):
                    t = triple(ps[:, 256 * j:256 * j + 256], lambda k: h[:, k, 128 * j:128 * j + 128],
                               lambda k: l[:, k, 128 * j:128 * j + 128], lambda k: xh[:, k, :], lambda k: xl[:, k, :],
                               8, True, True, [tw, tf, ready])
                W.free(i, t)
                res.append((b, ps[:, :].rearrange("p (a n) -> p a n", a=2), t))
            s = e % nb
            (bg, pg, tg), (bu, pu, tu) = res
            t = P.act(hs[s][:, :, :], pg, ACT.Silu, after=[tg, used[s]])
            B.free(bg, t)
            t = P.tt(hs[s][:, :, :], hs[s][:, :, :], pu, ALU.mult, after=[t, tu])
            B.free(bu, t)
            if scale is not None:
                t = P.tt(hs[s][:, :, :], hs[s][:, :, :], scale.unsqueeze(1).broadcast_to([128, 2, 256]), ALU.mult, after=[ts])
            return split(ah[s][:, :, :], al[s][:, :, :], hs[s][:, :, :], [t, used[s]])

        def down(e, ta):
            h, l, tw, i = W.next([(0, 2, 1024, kp(steps[e][2], 2))])
            s = e % nb
            for d in range(8):
                ps = ybanks[d // 2][:, 256 * (d % 2):256 * (d % 2) + 256]
                for k in range(2):
                    st, sp = e == 0 and k == 0 and d % 2 == 0, e == n - 1 and k == 1
                    c = slice(128 * d, 128 * d + 128)
                    P.mm(ps, h[:, k, c], ah[s][:, k, :], st, False, after=[tw, ta, yfree], loose=True)
                    P.mm(ps, h[:, k, c], al[s][:, k, :], False, False, loose=True)
                    t = P.mm(ps, l[:, k, c], ah[s][:, k, :], False, sp, loose=True)
            W.free(i, t)
            used[s] = t
            return t

        ta = {e: up(e) for e in range(group)}
        for e0 in range(0, n, group):
            for e in range(e0 + group, min(e0 + 2 * group, n)):
                ta[e] = up(e)
            for e in range(e0, min(e0 + group, n)):
                t = down(e, ta[e])
        return [y[:, :].rearrange("p (a n) -> p a n", a=2) for y in ybanks], t

    wg, wu, wd = I["w_exp_gate"][0], I["w_exp_up"][0], I["w_exp_down"][0]

    def add_y(ys, t):
        for j in range(4):
            P.tt(H[:, 2 * j:2 * j + 2, :], H[:, 2 * j:2 * j + 2, :], ys[j], ALU.add, after=[t], chain=False)

    def dense():
        for q in range(16):
            b, ps, tf = B.get()
            for j in range(2):
                e = 2 * q + j
                t2 = P.mm(ps[:, 256 * j:256 * j + 256], ident[0:32, e:e + 1].broadcast_to([32, 128]), combT[0:32, :], after=[t, tf])
            t_cb = P.act(CBt[:, 2 * q:2 * q + 2, :], ps[:, :].rearrange("p (a n) -> p a n", a=2), ACT.Copy, after=[t2])
            B.free(b, t_cb)
        add_y(*gated("moe", [(wg[e], wu[e], wd[e], CBt[:, e, :], t_cb) for e in range(32)], XUh, XUl, None, 2))

    def sparse():
        Pg = [R(f"Pg{i}", [128, 2, 256], F32R, (16 + 2 * i) * KB) for i in range(2)]
        PT = [R(f"PT_{i}", [128, 256], F32R, (20 + i) * KB) for i in range(2)]
        ah = [R(f"spah{i}", [128, 2, 128], F32R, (22 + i) * KB) for i in range(4)]
        al = [R(f"spal{i}", [128, 2, 128], F32R, (26 + i) * KB) for i in range(4)]
        hs = [R(f"sphs{i}", [128, 256], F32, (34 + i) * KB) for i in range(2)]
        wsl = R("wsl", [128, 16], F32, 30 * KB + 512)
        eq = [R(f"speq{i}", [128, 256], F32, (31 + i) * KB) for i in range(2)]
        Xgh = [R(f"Xgh{i}", [128, 8, 256], F32R, (40 + 16 * i) * KB) for i in range(2)]
        Xgl = [R(f"Xgl{i}", [128, 8, 256], F32R, (48 + 16 * i) * KB) for i in range(2)]
        Yh = [XUh[:, 4 * i:4 * i + 4, :].rearrange("p a n -> p (a n)") for i in range(2)]
        Yl = [XUl[:, 4 * i:4 * i + 4, :].rearrange("p a n -> p (a n)") for i in range(2)]
        iota256, sid = slots[:, 0:256], slots[:, 256:272]
        ybanks = [B.banks[4 + j] for j in range(4)]
        dbanks = [None, None]

        used = [None] * 4
        ready = {}

        def gather(g):
            s = g % 2
            for j in range(2):
                P.ts(eq[j][:, :], iota256, pg[:, g, j, 0:1], None, ALU.is_equal, after=[t_slots])
                t = P.stt(Pg[s][:, j, :], iota256, pg[:, g, j, 1:2], eq[j][:, :], ALU.is_equal, ALU.add, after=used)
            yield
            b, ps, tf = B.get((2, 3))
            for r in range(2):
                for j in range(2):
                    t2 = P.mm(ps[:, 2 * r:2 * r + 2], Pg[s][:, j, 128 * r:128 * r + 128].bitcast(F32),
                              comb[:, j, 4 * g + 2 * r:4 * g + 2 * r + 2], j == 0, j == 1, after=[t, tf])
            for r in range(2):
                for o in range(2):
                    p = slice(64 * o, 64 * o + 64)
                    t3 = P.act(wsl[p, 2 * g + r:2 * g + r + 1], ps[p, 2 * r + o:2 * r + o + 1], ACT.Copy, after=[t2])
            B.free(b, t3)
            toks = [t3]
            for q in range(4):
                for x, X in ((XTh, Xgh), (XTl, Xgl)):
                    b, ps, tf = B.get((2, 3))
                    for r in range(2):
                        for j in range(2):
                            k = 2 * q + r
                            t2 = P.mm(ps[:, 256 * r:256 * r + 256], x[:, j, 128 * k:128 * k + 128], Pg[s][:, j, :],
                                      j == 0, j == 1, after=[t, tf])
                    v = ps[:, :].rearrange("p (a n) -> p a n", a=2)
                    t3 = P.act(X[s][:, 2 * q:2 * q + 2, :], v, ACT.Copy, after=[t2])
                    B.free(b, t3)
                    toks.append(t3)
                    yield
            ready[g] = toks

        def up(e):
            g, s, p = e // 4, (e // 4) % 2, e // 2
            c = slice(128 * (p % 2), 128 * (p % 2) + 128)
            b, ps, tf = B.get((0, 1))
            for n, w in enumerate((wg[e], wu[e])):
                h, l, tw, i = W.next([(0, 8, 256, kp(w, 8))])
                t = triple(ps[:, 256 * n:256 * n + 256], lambda k: Xgh[s][:, k, c], lambda k: Xgl[s][:, k, c],
                           lambda k: h[:, k, :], lambda k: l[:, k, :], 8, True, True, [tw, tf, ready[g]])
                W.free(i, t)
            r = slice(64 * (e % 2), 64 * (e % 2) + 64)
            x = hs[p % 2]
            t = P.act(x[r, :], ps[r, 0:256], ACT.Silu, after=[t, turned[p % 2]])
            t = P.stt(x[r, :], x[r, :], wsl[r, p:p + 1], ps[r, 256:512], ALU.mult, ALU.mult, after=[t, ready[g]])
            B.free(b, t)
            return t

        turned = [None, None]

        def turn(p, t):
            b, ps, tf = B.get((2, 3))
            for k in range(2):
                t2 = P.tr(ps[:, 128 * k:128 * k + 128], hs[p % 2][:, 128 * k:128 * k + 128], ident, after=[t, tf])
            turned[p % 2] = t2
            v = ps[:, 0:256].rearrange("p (a n) -> p a n", a=2)
            own = [((2 * p + o) % 4, slice(64 * o, 64 * o + 64)) for o in range(2)]
            for u, c in own:
                t3 = P.act(ah[u][:, :, c], v[:, :, c], ACT.Copy, after=[t2, used[u]])
            for u, c in own:
                t3 = P.tt(al[u][:, :, c], v[:, :, c], ah[u][:, :, c].bitcast(F32), ALU.subtract, after=[t3, used[u]])
            B.free(b, t3)
            return t3

        def down(e, ta):
            h, l, tw, i = W.next([(0, 2, 1024, kp(wd[e], 2))])
            u, odd = e % 4, e % 2 == 1
            if not odd:
                dbanks[:] = [B.get((2, 3)) for _ in range(2)]
            for f in range(2):
                c = slice(512 * f, 512 * f + 512)
                for k in range(2):
                    ps = dbanks[f][1][:, :]
                    P.mm(ps, ah[u][:, k, :], h[:, k, c], not odd and k == 0, False, after=[tw, ta, t_z, dbanks[f][2]])
                    P.mm(ps, al[u][:, k, :], h[:, k, c], False, False)
                    t = P.mm(ps, ah[u][:, k, :], l[:, k, c], False, odd and k == 1)
            W.free(i, t)
            used[u] = t
            return t

        back = [None, None]

        def leave(p, t):
            s = p % 2
            P.ts(eq[0][:, :], posrow[:, 0, :], sid[:, p:p + 1], None, ALU.is_equal)
            P.stt(PT[s][:, :], posrow[:, 1, :], sid[:, p:p + 1], eq[0][:, :], ALU.is_equal, ALU.add, after=[back[s]])
            for f in range(2):
                c = slice(512 * f, 512 * f + 512)
                td = split(Yh[s][:, c], Yl[s][:, c], dbanks[f][1][:, :], [t, back[s]])
                B.free(dbanks[f][0], td)
            return td

        def scatter(p, t):
            s = p % 2
            for d in range(8):
                ps = ybanks[d // 2][:, 256 * (d % 2):256 * (d % 2) + 256]
                c = slice(128 * d, 128 * d + 128)
                P.mm(ps, Yh[s][:, c], PT[s][:, :], p == 0 and d % 2 == 0, False, after=[t], loose=True)
                t2 = P.mm(ps, Yl[s][:, c], PT[s][:, :], False, p == 15, loose=True)
            back[s] = t2
            return t2

        def step():
            if not work:
                return
            try:
                next(work[0])
            except StopIteration:
                work.pop()

        work = [gather(0)]
        step()
        if seq is not None:
            W.ahead(2)
        while work:
            step()
        for i in range(4):
            o = 64 * (1 - i % 2)
            for x in (ah[i], al[i]):
                t_z = P.ts(x[:, :, o:o + 64], ones[:, 0:128].rearrange("p (a n) -> p a n", a=2), 0.0, None, ALU.mult)
        up(0)
        tu, late = up(1), None
        for p in range(16):
            if p % 2 == 0 and p < 14:
                work.append(gather(p // 2 + 1))
                step()
            if p < 15:
                up(2 * p + 2)
            step()
            ta = turn(p, tu)
            if p < 15:
                tu = up(2 * p + 3)
            while len(work) > 0:
                step()
            if late:
                scatter(*late)
            down(2 * p, ta)
            late = (p, leave(p, down(2 * p + 1, ta)))
        t = scatter(*late)
        add_y([y[:, :].rearrange("p (a n) -> p a n", a=2) for y in ybanks], t)

    state, count = W.state(), P.count
    ends.append(W.i)
    enter("sparse", state, bounds[1], count, 1)
    sparse()
    after_sparse, n_sparse = W.state(), dict(P.count)
    if seq is None:
        W.rec = W.rec[:state[2]]
    enter("dense", state, bounds[1], count, 1)
    dense()
    ends.append(W.i)
    assert W.state()[:3] == after_sparse[:3] and P.count == n_sparse
    enter("end", W.state(), bounds[2], P.count)
    t_h = None
    t_h = [x[2] for x in norm(H, 8, 1024, col["norm_final"], H, [t_h])]
    if seq is not None:
        W.ahead(1)
    tap("h3", H[:, :, :], t_h)

    reset = R("reset", [128, 1024], F32, 70 * KB)
    t_reset = P.dma(reset[:, :], I["c_reset"], "reset", after=P.last())
    t_u2 = Ready()
    steps = norm_split_steps(t_u2, H, 8, 1024, col["attn_pre_norm_2"], XUh[:, :, :], XUl[:, :, :], [t_h])
    next(steps)
    if seq is not None:
        W.ahead(1)
    finish(steps)
    w2 = I["w_in_2"][0]
    hq, hz = R("hq", [128, 4, 256], F32, 0), R("hz", [128, 4, 256], F32, 4 * KB)
    hv_, hg = R("hv", [128, 2, 512], F32, 8 * KB), R("hg", [128, 4, 256], F32, 12 * KB)
    sq_, sk_ = R("sq", [128, 4, 256], F32, 16 * KB), R("sk", [128, 4, 256], F32, 20 * KB)
    sv_ = R("sv", [128, 2, 512], F32, 24 * KB)

    def ev_f(dst, func):
        def ev(f, n, ps, t):
            t_g[0] = P.act(dst[:, f:f + n, :], ps, func, after=[t])
            return t_g[0]
        return ev

    linear(w2, 0, 512, XUh, XUl, 8, t_u2, ev_f(hq, ACT.Silu))
    linear(w2, 512, 512, XUh, XUl, 8, t_u2, ev_f(hz, ACT.Copy))
    t_in = t_g[0]

    gam = col["hg_lower_gamma_2"]
    lb = mem["lb"]
    lA = lb[:, 24:28].unsqueeze(2).broadcast_to([128, 4, 256])
    lC = lb[:, 28:32].unsqueeze(2).broadcast_to([128, 4, 256])
    e1, e2, e3 = (R(f"he{j}", [128, 4, 256], F32, (28 + 4 * j) * KB) for j in range(3))
    hk, hb = R("hk", [128, 4, 256], F32, 40 * KB), R("hb", [128, 4, 256], F32, 44 * KB)
    a = lambda x: x[:, :, :]
    SC0, SC1 = R("SC0", [128, 4, 256], F32, 48 * KB), R("SC1", [128, 4, 128], F32, 52 * KB)
    Xs = [R(f"X{j}", [128, 4, 256], F32, (54 + 4 * j) * KB) for j in range(2)]
    diag = [SC0[:, :, 0:128], SC1[:, :, :]]
    OO = R("OO", [128, 8, 256], F32, 40 * KB)
    oh, osb = OO[:, 0:4, :], OO[:, 4:8, :]
    t_o = []

    def hgrn_steps():
        P.tt(lb[:, 0:4], gam[:, 0:4], gam[:, 4:8], ALU.max, after=[t_vec])
        P.tt(lb[:, 4:8], gam[:, 0:4], lb[:, 0:4], ALU.subtract)
        t = P.tt(lb[:, 8:12], gam[:, 4:8], lb[:, 0:4], ALU.subtract)
        t = P.act(lb[:, 12:20], lb[:, 4:12], ACT.Exp, after=[t])
        t = P.tt(lb[:, 20:24], lb[:, 12:16], lb[:, 16:20], ALU.add, after=[t])
        t = P.act(lb[:, 20:24], lb[:, 20:24], ACT.Ln, after=[t])
        P.tt(lb[:, 24:28], lb[:, 4:8], lb[:, 20:24], ALU.subtract, after=[t])
        t = P.tt(lb[:, 28:32], lb[:, 8:12], lb[:, 20:24], ALU.subtract)
        t = P.act(a(e1), a(hz), ACT.Abs, after=[t_in])
        t = P.act(a(e1), a(e1), ACT.Exp, after=[t], scale=-1.0)
        t = P.act(a(e1), a(e1), ACT.Ln, bias=1.0, scale=1.0)
        P.stt(a(e2), a(hz), 0.0, a(e1), ALU.min, ALU.subtract, after=[t])
        P.tt(a(e2), a(e2), lC, ALU.add)
        t = P.tt(a(hk), a(e2), a(hz), ALU.subtract)
        t_hk = P.act(a(hk), a(hk), ACT.Exp, after=[t])
        P.tt(a(e3), a(e2), lA, ALU.max)
        t = P.tt(a(e2), a(e2), lA, ALU.subtract)
        t = P.act(a(e2), a(e2), ACT.Abs, after=[t])
        t = P.act(a(e2), a(e2), ACT.Exp, after=[t], scale=-1.0)
        t = P.act(a(e2), a(e2), ACT.Ln, bias=1.0, scale=1.0)
        P.tt(a(e3), a(e3), a(e2), ALU.add, after=[t])
        t_b = P.put("dve", lambda e: e.tensor_tensor_scan(hb[:, :, :].rearrange("p a n -> p (a n)"), reset[:, :],
                                                          e3[:, :, :].rearrange("p a n -> p (a n)"), 0.0, ALU.mult, ALU.add), [t_reset])
        yield
        id4 = ident.unsqueeze(1).broadcast_to([128, 4, 128])
        for j in range(2):
            b, ps, tf = B.get()
            for hd in range(4):
                t = P.mm(ps[:, 128 * hd:128 * hd + 128], hk[:, hd, 128 * j:128 * j + 128], hq[:, hd, 128 * j:128 * j + 128], after=[t_hk, t_in, tf])
            t_sc = P.tt(diag[j], ps[:, :].rearrange("p (a n) -> p a n", a=4), id4, ALU.mult, after=[t])
            B.free(b, t_sc)
        xt = [None, None]
        t_x = {}

        def build(lv):
            L = 2 << lv
            m = L // 2
            X = Xs[lv % 2]
            if L <= 64:
                v = lambda z: z[:, :, :].rearrange("p a (n l) -> p (a n) l", l=L)
                nb = 1024 // L
                mid = v(hb)[:, :, m - 1:m].broadcast_to([128, nb, m])
                P.tt(v(X)[:, :, 0:m], mid, v(hb)[:, :, 0:m], ALU.subtract, after=[t_b, xt[lv % 2]])
                t = P.tt(v(X)[:, :, m:L], v(hb)[:, :, m:L], mid, ALU.subtract)
            elif L == 128:
                v = lambda z: z[:, :, :].rearrange("p a (n l) -> p (a n) l", l=128)
                mid = v(hb)[:, :, 63:64].broadcast_to([128, 8, 64])
                P.tt(v(X)[:, :, 0:64], mid, v(hb)[:, :, 0:64], ALU.subtract, after=[xt[lv % 2]])
                t = P.copy(v(X)[:, :, 64:128], v(hb)[:, :, 64:128])
            else:
                v = lambda z: z[:, :, :]
                m = 128
                en = lambda c: hb[:, :, 64 * c + 63:64 * c + 64].broadcast_to([128, 4, 64])
                sl = lambda z, c: z[:, :, 64 * c:64 * c + 64]
                P.tt(sl(X, 0), en(0), sl(hb, 0), ALU.subtract, after=[xt[lv % 2]])
                P.tt(sl(X, 0), sl(X, 0), en(1), ALU.add)
                P.tt(sl(X, 1), en(1), sl(hb, 1), ALU.subtract)
                P.copy(sl(X, 2), sl(hb, 2))
                t = P.tt(sl(X, 3), sl(hb, 3), en(2), ALU.add)
            t = P.act(a(X), a(X), ACT.Exp, after=[t])
            if L == 256:
                P.tt(X[:, :, 0:128], X[:, :, 0:128], hk[:, :, 0:128], ALU.mult, after=[t, t_hk])
                t_x[lv] = P.tt(X[:, :, 128:256], X[:, :, 128:256], hq[:, :, 128:256], ALU.mult)
            else:
                P.tt(v(X)[:, :, 0:m], v(X)[:, :, 0:m], v(hk)[:, :, 0:m], ALU.mult, after=[t, t_hk])
                t_x[lv] = P.tt(v(X)[:, :, m:L], v(X)[:, :, m:L], v(hq)[:, :, m:L], ALU.mult)

        def scores(lv):
            X = Xs[lv % 2]
            if lv == 7:
                b, ps, tf = B.get()
                for hd in range(4):
                    t = P.mm(ps[:, 128 * hd:128 * hd + 128], X[:, hd, 0:128], X[:, hd, 128:256], after=[t_x[lv], tf])
                t_sc = P.copy(SC0[:, :, 128:256], ps[:, :].rearrange("p (a n) -> p a n", a=4), after=[t])
                B.free(b, t_sc)
                return t_sc
            mk = masks[:, 128 * lv:128 * lv + 128].unsqueeze(1).broadcast_to([128, 4, 128])
            for j in range(2):
                b, ps, tf = B.get()
                for hd in range(4):
                    x = X[:, hd, 128 * j:128 * j + 128]
                    t = P.mm(ps[:, 128 * hd:128 * hd + 128], x, x, after=[t_x[lv], tf])
                t_sc = P.put("dve", lambda e, j=j, ps=ps: e.copy_predicated(
                    diag[j], mk, ps[:, :].rearrange("p (a n) -> p a n", a=4)), [t])
                B.free(b, t_sc)
            xt[lv % 2] = t

        for lv in range(8):
            build(lv)
            if lv:
                scores(lv - 1)
            yield
        t_sc = scores(7)
        yield
        for q in range(2):
            b, ps, tf = B.get()
            for r in range(2):
                hd = 2 * q + r
                d = ps[:, 256 * r:256 * r + 256]
                P.mm(d, hv_[:, 0, 128 * hd:128 * hd + 128], SC0[:, hd, :], True, False, after=[t_sc, t_hv[0], tf])
                t = P.mm(d[:, 128:256], hv_[:, 1, 128 * hd:128 * hd + 128], SC1[:, hd, :], False, True)
            t = P.copy(oh[:, 2 * q:2 * q + 2, :], ps[:, :].rearrange("p (a n) -> p a n", a=2), after=[t])
            B.free(b, t)
            t_o.append(t)

    t_hv = [None]
    side.append(hgrn_steps())
    advance()
    linear_tok(w2, 1024, 512, XUh, XUl, 8, t_u2, ev_tok(hv_))
    t_hv[0] = t_g[0]
    linear(w2, 2048, 512, XUh, XUl, 8, t_u2, ev_f(sq_, ACT.Copy))
    linear(w2, 2560, 512, XUh, XUl, 8, t_u2, ev_f(sk_, ACT.Copy))
    linear_tok(w2, 3072, 512, XUh, XUl, 8, t_u2, ev_tok(sv_))
    t_in2 = t_g[0]

    def flat4(x):
        return x[:, 0:6, :].rearrange("p a n -> p (a n)").rearrange("p (a n) -> p a n", a=4)

    Zs = [flat4(T8), R("Z1", [128, 4, 384], F32, 28 * KB)[:, :, :]]
    Sps = [flat4(T8b), R("Sp1", [128, 4, 384], F32, 34 * KB)[:, :, :]]

    def stick_steps(g, after):
        Z, Sp = Zs[g], Sps[g]
        for hl in range(4):
            hd = 4 * g + hl
            o, tl = 64 * (hd % 2), hd // 2
            b, ps, tf = B.get()
            P.mm(ps[:, 0:256], sk_[o:o + 64, tl, 0:128], sq_[o:o + 64, tl, :], after=[t_in2, tf])
            t = P.mm(ps[:, 256:384], sk_[o:o + 64, tl, 128:256], sq_[o:o + 64, tl, 128:256])
            P.stt(Z[:, hl, 0:128], ps[:, 0:128], 0.125, n_st, ALU.mult, ALU.add, after=[t, after])
            P.ts(Z[:, hl, 128:256], ps[:, 128:256], 0.125, None, ALU.mult)
            t = P.stt(Z[:, hl, 256:384], ps[:, 256:384], 0.125, n_st, ALU.mult, ALU.add)
            B.free(b, t)
        t = P.act(Sp, Z, ACT.Abs, after=[t, after])
        t = P.act(Sp, Sp, ACT.Exp, after=[t], scale=-1.0)
        t = P.act(Sp, Sp, ACT.Ln, bias=1.0, scale=1.0)
        t_sp = P.stt(Sp, Z, 0.0, Sp, ALU.max, ALU.add, after=[t])
        yield
        for hl in range(4):
            b, ps, tf = B.get()
            P.mm(ps[:, 0:256], tri, Sp[:, hl, 0:256], True, False, after=[t_sp, tf])
            P.mm(ps[:, 128:256], ones[:, :], Sp[:, hl, 256:384], False, True)
            t = P.mm(ps[:, 256:384], tri, Sp[:, hl, 256:384])
            t = P.tt(Z[:, hl, :], Z[:, hl, :], ps[:, 0:384], ALU.subtract, after=[t])
            B.free(b, t)
        t = P.act(Z, Z, ACT.Exp, after=[t])
        yield
        b, ps, tf = B.get()
        for hl in range(4):
            hd = 4 * g + hl
            o = 64 * (hl % 2)
            d = ps[o:o + 64, 256 * (hl // 2):256 * (hl // 2) + 256]
            P.mm(d, sv_[:, 0, 64 * hd:64 * hd + 64], Z[:, hl, 0:256], True, False, after=[t, tf])
            t_pv = P.mm(d[:, 128:256], sv_[:, 1, 64 * hd:64 * hd + 64], Z[:, hl, 256:384], False, True)
        t = P.copy(osb[:, 2 * g:2 * g + 2, :], ps[:, :].rearrange("p (a n) -> p a n", a=2), after=[t_pv, t_o])
        B.free(b, t)
        t_o.append(t)

    chains = side[:1] + [stick_steps(g, P.last()) for g in range(2)]
    side.clear()
    while chains:
        for x in list(chains):
            if next(x, 0) == 0:
                chains.remove(x)

    MIh, MIl = R("MIh", [128, 8, 256], F32R, 62 * KB), R("MIl", [128, 8, 256], F32R, 0)
    t_mi = Ready()
    t_hg = [None]
    i0 = sum(n for name, _, n in vecs[:[x[0] for x in vecs].index("hg_out_norm_2")])

    def mi_steps():
        res = []
        yield from norm_steps(res, OO, 4, 512, vec[:, i0:i0 + 8], T8b, [t_o, P.last()], 2)
        yield
        t_hg[0] = P.act(a(hg), a(hg), ACT.Silu, after=[t_g[0]])
        t = P.tt(T8b[:, 0:4, :], T8b[:, 0:4, :], a(hg), ALU.mult, after=[t_hg[0]])
        t_mi.extend([split(MIh[:, 0:4, :], MIl[:, 0:4, :], T8b[:, 0:4, :], [t])] * 4)
        t_mi.extend([split(MIh[:, 4:8, :], MIl[:, 4:8, :], T8b[:, 4:8, :], [res[1][2]])] * 4)
        busy[0] = t_mi[4]

    side.append(mi_steps())
    advance()
    linear(w2, 1536, 512, XUh, XUl, 8, t_u2, ev_f(hg, ACT.Copy))
    finish()

    mx = R("mx", [128, 8, 256], F32, 48 * KB)
    pin = R("pin", [128, 2, 256], F32, 16 * KB)
    pT = R("pT", [128, 2, 256], F32, 18 * KB)
    PTh, PTl = R("PTh", [128, 2, 256], F32R, 20 * KB), R("PTl", [128, 2, 256], F32R, 22 * KB)
    t_p = P.dma(pin[:, :, :], I["p_2"][0, 0].rearrange("(t p) d -> p t d", p=128), "p", after=P.last())
    linear(I["w_out_2"][0], 0, 1024, MIh, MIl, 8, t_mi, ev_to(mx))

    def post(src, gain, after):
        ready = Ready()
        for k0, k1, t in norm(src, 8, 1024, gain, T8b, after):
            busy[0] = t = P.tt(H[:, k0:k1, :], H[:, k0:k1, :], T8b[:, k0:k1, :], ALU.add, after=[t], chain=False)
            ready.extend([t] * (k1 - k0))
        return ready

    t_h = post(mx, col["attn_post_norm_2"], [t_g[0]])
    tap("h4", H[:, :, :], t_h)

    t_u3 = norm_split(H, 8, 1024, col["ffn_pre_norm_2"], XUh[:, :, :], XUl[:, :, :], [t_h])
    b, ps, tf = B.get()
    for j in range(4):
        t = P.tr(ps[:, 128 * j:128 * j + 128], pin[:, j % 2, 128 * (j // 2):128 * (j // 2) + 128], ident, after=[t_p, tf])
    t = P.copy(pT[:, :, :], ps[:, :].rearrange("p (a n) -> p a n", a=2), after=[t])
    B.free(b, t)
    t_pt = split(PTh[:, :, :], PTl[:, :, :], pT[:, :, :], [t])
    wgu, wdn = I["w_gate_up_2"][0], I["w_down_2"][0]
    ys, t = gated("ffn", [(wgu[:, 256 * c:256 * c + 256], wgu[:, 2816 + 256 * c:2816 + 256 * c + 256],
                           wdn[256 * c:256 * c + 256, :], None, None) for c in range(11)], XUh, XUl, t_u3, 1)
    ff = R("ff", [128, 8, 256], F32, 52 * KB)
    t_ff = []
    for j in range(4):
        f = ff[:, 2 * j:2 * j + 2, :]
        t_ff.append(P.act(f, ys[j], ACT.Copy, after=[t], chain=False) if j < 2 else P.copy(f, ys[j], after=[t]))
        B.free(4 + j, t_ff[-1])
    t_h = post(ff, col["ffn_post_norm_2"], [t_ff])
    tap("h5", H[:, :, :], t_h)

    t_hx = Ready()
    for k0 in (0, 4):
        c = slice(k0, k0 + 4)
        t_hx.extend([split(XUh[:, c, :], XUl[:, c, :], H[:, c, :], [t_h[k0], t_u3])] * 4)
    pg = R("pg", [128, 8, 256], F32, 60 * KB)
    linear(I["ple_gate_2"][0], 0, 1024, XUh, XUl, 8, t_hx, ev_f(pg, ACT.Sigmoid))
    t_pg = t_g[0]

    def ev_ple(f, n, ps, t):
        t = P.tt(pg[:, f:f + n, :], pg[:, f:f + n, :], ps, ALU.mult, after=[t, t_pg])
        t_g[0] = P.tt(H[:, f:f + n, :], H[:, f:f + n, :], pg[:, f:f + n, :], ALU.add, after=[t_h])
        return t

    linear(I["ple_proj_2"][0], 0, 1024, PTh, PTl, 2, t_pt, ev_ple, k_cols=256)
    t_h = t_g[0]
    ot = R("ot", [128, 2, 1024], F32, 68 * KB)
    for j in range(2):
        for q in range(2):
            b, ps, tf = B.get()
            for r in range(4):
                t = P.tr(ps[:, 128 * r:128 * r + 128], H[:, 4 * q + r, 128 * j:128 * j + 128], ident, after=[t_h, tf])
            t = P.copy(ot[:, j, 512 * q:512 * q + 512], ps[:, :], after=[t])
            B.free(b, t)
        P.dma(out[0, 128 * j:128 * j + 128, :], ot[:, j, :], "out", after=[t])
    return W.rec, ends + [W.i]


def build(nc, I, out, taps=None):
    base = (nc.sbuf_base + 63) // 64 * 64
    at = [base]
    used = set()

    def sb(name, shape, dt, offset=None):
        n = 1
        for s in shape[1:]:
            n *= s
        n *= 1 if dt == U8 else 4
        if offset is None:
            offset = at[0]
            at[0] += (n + 63) // 64 * 64
        return nc.alloc_sbuf_tensor_at(name, shape, dt, offset=offset)

    mem = {"sb": sb}
    mem["raw"] = [sb(f"raw{i}", [128, PIECE], F32) for i in range(NRAW)]
    mem["hi"] = [sb(f"whi{i}", [128, PIECE], F32R) for i in range(NSPL)]
    mem["lo"] = [sb(f"wlo{i}", [128, PIECE], F32R) for i in range(NSPL)]
    mem["XUh"], mem["XUl"] = sb("XUh", [128, 8, 256], F32R), sb("XUl", [128, 8, 256], F32R)
    mem["H"] = sb("H", [128, 8, 256], F32)
    for name, part in (("T8", "hi"), ("T8b", "lo")):
        offset = at[0]
        mem[name] = sb(name, [128, 8, 256], F32)
        mem[part].append(sb(f"w{part}3", [128, PIECE], F32R, offset))
    mem["cst"] = sb("cst", [128, 896], F32)
    mem["ones"] = sb("ones", [128, 128], F32)
    mem["masks"] = sb("masks", [128, 896], U8)
    mem["vec"] = sb("vec", [128, 256], F32)
    mem["small"] = sb("small", [128, 64], F32)
    mem["brt"] = sb("brt", [128, 36], F32)
    mem["rs"] = sb("rs", [128, 512], F32)
    mem["cs"] = sb("cs", [128, 2, 256], F32)
    mem["sm"] = sb("sm", [128, 128], F32)
    mem["lb"] = sb("lb", [128, 32], F32)
    mem["flag"] = sb("flag", [128, 4], I32)
    top = nc.sbuf_usable_end // 64 * 64
    rbase = at[0]
    size = top - rbase
    made = {}

    def R(name, shape, dt, offset):
        if name not in made:
            n = 4
            for s in shape[1:]:
                n *= s
            assert offset + n <= size, (name, offset + n, size)
            made[name] = sb(name, shape, dt, rbase + offset)
        return made[name]

    mem["R"] = R
    mem["posi"] = R("posi", [128, 256], I32, 18 * KB)
    mem["ps"] = [nc.alloc_psum_tensor(f"ps{i}", [128, 512], F32) for i in range(8)]
    names = ("start", "sparse", "dense", "end")
    rec, bounds = program(nc, I, out, {n: Prog(n) for n in names}, mem, None, (0, 0, 0), taps)
    parts = {n: Prog(n) for n in names}
    program(nc, I, out, parts, mem, rec, bounds, taps)
    total = parts["end"].count
    sems = {n: nc.alloc_semaphore(f"s_{n}") for n in [e + n for n in names for e in Prog.ENGINES[:4]] + sorted(total)}
    runs = {n: p.emit(nc, sems) for n, p in parts.items()}
    flag = mem["flag"]

    def run(name, e):
        runs["start"](name, e)
        most = e.value_load(flag[0:1, 0:1])
        with e.If(most > CAP):
            runs["dense"](name, e)
        with e.If(most <= CAP):
            runs["sparse"](name, e)
        runs["end"](name, e)

    with nc.Block() as block:

        @block.tensor
        def _(e):
            run("pe", e)

        @block.scalar
        def _(e):
            run("act", e)

        @block.vector
        def _(e):
            run("dve", e)

        @block.gpsimd
        def _(e):
            run("pool", e)

        @block.sync
        def _(e):
            run("sp", e)
            for n in ("out", "taps"):
                if n in total:
                    e.wait_ge(sems[n], total[n])


def kernel(**inputs):
    import concourse.bacc as bacc
    from concourse.bass_utils import run_bass_kernel_spmd

    nc = bacc.Bacc("TRN2", target_bir_lowering=False, num_devices=1)
    arrays = {f"in_{k}": np.ascontiguousarray(v) for k, v in inputs.items()}
    arrays.update({f"in_{k}": v for k, v in constants().items()})
    aps = {k[3:]: nc.dram_tensor(k, a.shape, mybir.dt.from_np(a.dtype), kind="ExternalInput").ap() for k, a in arrays.items()}
    out = nc.dram_tensor("out_0", (1, 256, 1024), F32, kind="ExternalOutput").ap()
    build(nc, aps, out)
    r = run_bass_kernel_spmd(nc, [arrays], core_ids=[0])
    return r.results[0]["out_0"]
```
